# Optimizing a Trainium2 kernel written in Bass

```python
import jax, jax.numpy as jnp
from jax import lax
import numpy as np

D_MODEL = 1024
BATCH = 1
SEQ = 512
DEPTH = 1

HEAD_DIM = 64
NSA_HEADS = 8
NSA_KV_HEADS = 2
SWA_HEADS = 8
SWA_KV_HEADS = 2
CMP_BLOCK = 32
CMP_STRIDE = 16
CMP_HIDDEN = 256
SLC_BLOCK = 64
N_SELECT = 16
NSA_WINDOW = 512
SWA_WINDOW = 128
Q_BLOCK = 128
RMS_EPS = 1e-6
NEG = -1e30
BIG = 1e30
NSA_WIDTH = NSA_HEADS * HEAD_DIM
SWA_WIDTH = SWA_HEADS * HEAD_DIM
KV_NSA = NSA_KV_HEADS * HEAD_DIM
KV_SWA = SWA_KV_HEADS * HEAD_DIM
SPLIT_SIZES = (NSA_WIDTH, 2 * KV_NSA, 2 * KV_NSA, 2 * KV_NSA, 3 * NSA_HEADS, NSA_WIDTH,
               SWA_WIDTH, 2 * KV_SWA, SWA_WIDTH, 2 * D_MODEL)
D_IN = sum(SPLIT_SIZES)


def split_points():
    pts, acc = [], 0
    for s in SPLIT_SIZES[:-1]:
        acc += s
        pts.append(acc)
    return pts

def alibi_slopes(n, n_kv):
    s = 2.0 ** (-8.0 * (np.arange(n) + 1) / n)
    return jnp.asarray(s, dtype=jnp.float32).reshape(n_kv, n // n_kv)

def rms_norm(x, g):
    xf = x.astype(jnp.float32)
    y = xf * lax.rsqrt(jnp.mean(xf * xf, axis=-1, keepdims=True) + RMS_EPS)
    return (y * g.astype(jnp.float32)).astype(x.dtype)

def q_heads(t, n_kv, r):
    B, S, _ = t.shape
    return t.reshape(B, S, n_kv, r, HEAD_DIM).transpose(0, 2, 3, 1, 4)

def kv_heads(t, n_kv):
    B, S, _ = t.shape
    return t.reshape(B, S, n_kv, HEAD_DIM).transpose(0, 2, 1, 3)

def merge_heads(o):
    B, G, r, S, dh = o.shape
    return o.transpose(0, 3, 1, 2, 4).reshape(B, S, G * r * dh)

def banded_attention(q, k, v, slopes, window, sinks=None):
    B, G, r, S, dh = q.shape
    nprev = window // Q_BLOCK
    nqb = S // Q_BLOCK
    lk = (nprev + 1) * Q_BLOCK
    pad = nprev * Q_BLOCK
    kp = jnp.pad(k, ((0, 0), (0, 0), (pad, 0), (0, 0)))
    vp = jnp.pad(v, ((0, 0), (0, 0), (pad, 0), (0, 0)))
    idx = jnp.arange(nqb)[:, None] * Q_BLOCK + jnp.arange(lk)[None, :]
    kb = kp[:, :, idx].astype(jnp.float32)
    vb = vp[:, :, idx].astype(jnp.float32)
    qb = q.reshape(B, G, r, nqb, Q_BLOCK, dh).astype(jnp.float32)
    s = jnp.einsum('bgrnqd,bgnkd->bgrnqk', qb, kb) * (dh ** -0.5)
    qpos = jnp.arange(nqb)[:, None] * Q_BLOCK + jnp.arange(Q_BLOCK)[None, :]
    kpos = idx - pad
    dist = qpos[:, :, None] - kpos[:, None, :]
    valid = (dist >= 0) & (dist < window) & (kpos[:, None, :] >= 0)
    s = s - slopes[None, :, :, None, None, None] * dist.astype(jnp.float32)
    s = jnp.where(valid, s, NEG)
    if sinks is not None:
        sink = jnp.broadcast_to(sinks.astype(jnp.float32).reshape(1, G, r, 1, 1, 1), s.shape[:-1] + (1,))
        p = jax.nn.softmax(jnp.concatenate([s, sink], axis=-1), axis=-1)[..., :-1]
    else:
        p = jax.nn.softmax(s, axis=-1)
    o = jnp.einsum('bgrnqk,bgnkd->bgrnqd', p, vb)
    return o.reshape(B, G, r, S, dh).astype(q.dtype)

def compress_blocks(t, pe, w1, w2):
    B, G, S, dh = t.shape
    nc = (S - CMP_BLOCK) // CMP_STRIDE + 1
    idx = jnp.arange(nc)[:, None] * CMP_STRIDE + jnp.arange(CMP_BLOCK)[None, :]
    blk = t[:, :, idx] + pe
    flat = blk.reshape(B, G, nc, CMP_BLOCK * dh)
    return jax.nn.silu(flat @ w1) @ w2

def compressed_attention(q, kc, vc, slopes):
    B, G, r, S, dh = q.shape
    nc = kc.shape[2]
    s = jnp.einsum('bgrqd,bgcd->bgrqc', q.astype(jnp.float32), kc.astype(jnp.float32)) * (dh ** -0.5)
    end = jnp.arange(nc) * CMP_STRIDE + CMP_BLOCK - 1
    dist = jnp.arange(S)[:, None] - end[None, :]
    valid = dist >= 0
    s = s - slopes[None, :, :, None, None] * dist.astype(jnp.float32)
    s = jnp.where(valid, s, NEG)
    p = jax.nn.softmax(s, axis=-1) * jnp.any(valid, axis=-1)[:, None].astype(jnp.float32)
    o = jnp.einsum('bgrqc,bgcd->bgrqd', p, vc.astype(jnp.float32))
    return o.astype(q.dtype), p

def select_blocks(p_cmp):
    p = p_cmp.sum(axis=2)
    S, nc = p.shape[2], p.shape[3]
    nsb = S // SLC_BLOCK
    ratio = SLC_BLOCK // CMP_STRIDE
    span = CMP_BLOCK // CMP_STRIDE
    offs = (jnp.arange(ratio)[:, None] + jnp.arange(span)[None, :]).reshape(-1)
    cidx = ratio * jnp.arange(nsb)[:, None] - offs[None, :]
    ok = (cidx >= 0) & (cidx < nc)
    imp = jnp.where(ok, p[..., jnp.clip(cidx, 0, nc - 1)], 0.0).sum(axis=-1)
    cur = jnp.arange(S) // SLC_BLOCK
    j = jnp.arange(nsb)
    causal = j[None, :] <= cur[:, None]
    forced = (j[None, :] == 0) | (j[None, :] == cur[:, None]) | (j[None, :] == cur[:, None] - 1)
    score = jnp.where(causal & forced, BIG, jnp.where(causal, imp, NEG))
    _, idx = lax.top_k(score, min(N_SELECT, nsb))
    return idx

def selected_attention(q, k, v, blk_idx, slopes):
    B, G, r, S, dh = q.shape
    nsb = S // SLC_BLOCK
    n_sel = blk_idx.shape[-1]
    nqc = S // Q_BLOCK
    kb = k.reshape(B, G, nsb, SLC_BLOCK, dh)
    vb = v.reshape(B, G, nsb, SLC_BLOCK, dh)
    qc = q.reshape(B, G, r, nqc, Q_BLOCK, dh).transpose(3, 0, 1, 2, 4, 5)
    ic = blk_idx.reshape(B, G, nqc, Q_BLOCK, n_sel).transpose(2, 0, 1, 3, 4)
    qpos = jnp.arange(S).reshape(nqc, Q_BLOCK)
    gather = jax.vmap(jax.vmap(lambda blocks, ix: blocks[ix]))

    def one_block(args):
        q_i, ix, qp = args
        k_sel = gather(kb, ix).astype(jnp.float32)
        v_sel = gather(vb, ix).astype(jnp.float32)
        kpos = ix[..., None] * SLC_BLOCK + jnp.arange(SLC_BLOCK)
        dist = (qp[None, None, :, None, None] - kpos)[:, :, None]
        s = jnp.einsum('bgrqd,bgqnkd->bgrqnk', q_i.astype(jnp.float32), k_sel) * (dh ** -0.5)
        s = s - slopes[None, :, :, None, None, None] * dist.astype(jnp.float32)
        s = jnp.where(dist >= 0, s, NEG).reshape(B, G, r, Q_BLOCK, n_sel * SLC_BLOCK)
        p = jax.nn.softmax(s, axis=-1)
        return jnp.einsum('bgrqk,bgqkd->bgrqd', p, v_sel.reshape(B, G, Q_BLOCK, n_sel * SLC_BLOCK, dh))

    o = lax.map(one_block, (qc, ic, qpos))
    return o.transpose(1, 2, 3, 0, 4, 5).reshape(B, G, r, S, dh).astype(q.dtype)

def first_inputs(seed: int = 0) -> dict:
    key = jax.random.key(seed)
    ks = jax.random.split(key, 20)
    D, L, dh = D_MODEL, DEPTH, HEAD_DIM
    nrm = lambda k, shape, fan: jax.random.normal(k, shape, jnp.float32) * (fan ** -0.5)
    return {
        'x': jax.random.normal(ks[0], (BATCH, SEQ, D), jnp.float32),
        'c': jax.random.normal(ks[1], (BATCH, D), jnp.float32),
        'w_ada': nrm(ks[2], (L, D, 3 * D), D) * 0.5,
        'b_ada': 0.01 * jax.random.normal(ks[3], (L, 3 * D), jnp.float32),
        'g_pre': 1.0 + 0.05 * jax.random.normal(ks[4], (L, D), jnp.float32),
        'g_post': 1.0 + 0.05 * jax.random.normal(ks[5], (L, D), jnp.float32),
        'w_in': nrm(ks[6], (L, D, D_IN), D),
        'pe_cmp_k': 0.02 * jax.random.normal(ks[7], (L, CMP_BLOCK, dh), jnp.float32),
        'pe_cmp_v': 0.02 * jax.random.normal(ks[8], (L, CMP_BLOCK, dh), jnp.float32),
        'w_cmp_k1': nrm(ks[9], (L, CMP_BLOCK * dh, CMP_HIDDEN), CMP_BLOCK * dh),
        'w_cmp_k2': nrm(ks[10], (L, CMP_HIDDEN, dh), CMP_HIDDEN),
        'w_cmp_v1': nrm(ks[11], (L, CMP_BLOCK * dh, CMP_HIDDEN), CMP_BLOCK * dh),
        'w_cmp_v2': nrm(ks[12], (L, CMP_HIDDEN, dh), CMP_HIDDEN),
        'w_o_nsa': nrm(ks[13], (L, NSA_WIDTH, D), NSA_WIDTH),
        'w_o_swa': nrm(ks[14], (L, SWA_WIDTH, D), SWA_WIDTH),
        'w_out': nrm(ks[15], (L, D, D), D),
        'sinks': jax.random.normal(ks[16], (L, SWA_HEADS), jnp.float32),
    }

def first_block(x, c, w_ada, b_ada, g_pre, g_post, w_in, pe_cmp_k, pe_cmp_v, w_cmp_k1, w_cmp_k2,
              w_cmp_v1, w_cmp_v2, w_o_nsa, w_o_swa, w_out, sinks):
    B, S, D = x.shape
    ra = NSA_HEADS // NSA_KV_HEADS
    rb = SWA_HEADS // SWA_KV_HEADS
    slopes_a = alibi_slopes(NSA_HEADS, NSA_KV_HEADS)
    slopes_b = alibi_slopes(SWA_HEADS, SWA_KV_HEADS)
    pts = split_points()
    for l in range(DEPTH):
        mod = c @ w_ada[l] + b_ada[l]
        shift, scale, gate = jnp.split(mod, 3, axis=-1)
        h = rms_norm(x, g_pre[l]) * (1.0 + scale[:, None, :]) + shift[:, None, :]
        proj = h @ w_in[l]
        q_a, kv_c, kv_s, kv_w, g_nsa, z_a, q_b, kv_b, z_b, merge = jnp.split(proj, pts, axis=-1)

        qa = q_heads(q_a, NSA_KV_HEADS, ra)
        kc_raw, vc_raw = jnp.split(kv_c, 2, axis=-1)
        ks_, vs_ = jnp.split(kv_s, 2, axis=-1)
        kw_, vw_ = jnp.split(kv_w, 2, axis=-1)
        kc = compress_blocks(kv_heads(kc_raw, NSA_KV_HEADS), pe_cmp_k[l], w_cmp_k1[l], w_cmp_k2[l])
        vc = compress_blocks(kv_heads(vc_raw, NSA_KV_HEADS), pe_cmp_v[l], w_cmp_v1[l], w_cmp_v2[l])
        o_cmp, p_cmp = compressed_attention(qa, kc, vc, slopes_a)
        blk_idx = select_blocks(p_cmp)
        o_slc = selected_attention(qa, kv_heads(ks_, NSA_KV_HEADS), kv_heads(vs_, NSA_KV_HEADS), blk_idx, slopes_a)
        o_win = banded_attention(qa, kv_heads(kw_, NSA_KV_HEADS), kv_heads(vw_, NSA_KV_HEADS), slopes_a, NSA_WINDOW)
        gts = jax.nn.sigmoid(g_nsa.reshape(B, S, 3, NSA_KV_HEADS, ra)).transpose(2, 0, 3, 4, 1)[..., None]
        o_a = gts[0] * o_cmp + gts[1] * o_slc + gts[2] * o_win
        y_a = (merge_heads(o_a) * jax.nn.silu(z_a)) @ w_o_nsa[l]

        qb = q_heads(q_b, SWA_KV_HEADS, rb)
        kb_, vb_ = jnp.split(kv_b, 2, axis=-1)
        o_b = banded_attention(qb, kv_heads(kb_, SWA_KV_HEADS), kv_heads(vb_, SWA_KV_HEADS), slopes_b,
                               SWA_WINDOW, sinks=sinks[l])
        y_b = (merge_heads(o_b) * jax.nn.silu(z_b)) @ w_o_swa[l]

        m_a, m_b = jnp.split(merge, 2, axis=-1)
        y = (jax.nn.sigmoid(m_a) * y_a + jax.nn.sigmoid(m_b) * y_b) @ w_out[l]
        x = x + gate[:, None, :] * rms_norm(y, g_post[l])
    return x


DEPTH_2 = 2

N_MIXERS = 2
N_A = (DEPTH_2 + 1) // 2
N_B = DEPTH_2 // 2
N_META = 16
EXPAND = 2
E_CONV = EXPAND * D_MODEL
CONV_WIDTH = 3
E_MLSTM = EXPAND * D_MODEL
N_HEADS = 4
DV = E_MLSTM // N_HEADS
DK = DV // 2
QK = N_HEADS * DK
CHUNK = 64


def _rmsnorm(x, w):
    xf = x.astype(jnp.float32)
    y = xf * lax.rsqrt(jnp.mean(xf * xf, axis=-1, keepdims=True) + RMS_EPS)
    return (y * w.astype(jnp.float32)).astype(x.dtype)

def _short_conv_mixer(u, w_in, w_conv, w_out):
    proj = u @ w_in
    b_gate, c_gate, xin, z = jnp.split(proj, 4, axis=-1)
    y = lax.conv_general_dilated(
        c_gate * xin, w_conv[:, None, :].astype(u.dtype),
        window_strides=(1,), padding=[(CONV_WIDTH - 1, 0)],
        dimension_numbers=("NWC", "WIO", "NWC"), feature_group_count=E_CONV)
    return (jax.nn.silu(z) * b_gate * y) @ w_out

def _mlstm_chunk(carry, inp):
    c_state, n_state, m_state = carry
    q, k, v, logi, logf = inp
    L = q.shape[-2]
    b = jnp.cumsum(logf, axis=-1)
    causal = jnp.tril(jnp.ones((L, L), dtype=bool))
    log_d = jnp.where(causal, b[..., :, None] - b[..., None, :] + logi[..., None, :], -jnp.inf)
    log_inter = b + m_state[..., None]
    m_row = jnp.maximum(log_inter, jnp.max(log_d, axis=-1))
    d = jnp.exp(log_d - m_row[..., None])
    inter = jnp.exp(log_inter - m_row)
    s = jnp.einsum("bhtd,bhsd->bhts", q, k) * d
    num = jnp.einsum("bhts,bhsv->bhtv", s, v) + inter[..., None] * jnp.einsum("bhtd,bhdv->bhtv", q, c_state)
    den = jnp.sum(s, axis=-1) + inter * jnp.einsum("bhtd,bhd->bht", q, n_state)
    h = num / jnp.maximum(jnp.abs(den), jnp.exp(-m_row))[..., None]
    log_w = b[..., -1:] - b + logi
    m_new = jnp.maximum(b[..., -1] + m_state, jnp.max(log_w, axis=-1))
    decay = jnp.exp(b[..., -1] + m_state - m_new)
    w = jnp.exp(log_w - m_new[..., None])
    c_new = decay[..., None, None] * c_state + jnp.einsum("bhs,bhsd,bhsv->bhdv", w, k, v)
    n_new = decay[..., None] * n_state + jnp.einsum("bhs,bhsd->bhd", w, k)
    return (c_new, n_new, m_new), h

def _mlstm_mixer(u, w_in, gate_b, head_norm_w, w_out):
    bsz, T, _ = u.shape
    proj = u @ w_in
    q, k, v, o, z, g = jnp.split(
        proj, [QK, 2 * QK, 2 * QK + E_MLSTM, 2 * QK + 2 * E_MLSTM, 2 * QK + 3 * E_MLSTM], axis=-1)
    g = g.astype(jnp.float32) + gate_b.astype(jnp.float32)
    logi = jnp.transpose(g[..., :N_HEADS], (0, 2, 1))
    logf = jnp.transpose(jax.nn.log_sigmoid(g[..., N_HEADS:]), (0, 2, 1))

    def heads(a, dh):
        return a.astype(jnp.float32).reshape(bsz, T, N_HEADS, dh).transpose(0, 2, 1, 3)

    q = heads(q, DK) * (DK ** -0.5)
    k = heads(k, DK)
    v = heads(v, DV)
    seqs = (q, k, v, logi, logf)

    def chunks(a):
        real = a[:, :, N_META:]
        nc = real.shape[2] // CHUNK
        return jnp.moveaxis(real.reshape(bsz, N_HEADS, nc, CHUNK, *real.shape[3:]), 2, 0)

    carry0 = (jnp.zeros((bsz, N_HEADS, DK, DV), jnp.float32),
              jnp.zeros((bsz, N_HEADS, DK), jnp.float32),
              jnp.zeros((bsz, N_HEADS), jnp.float32))
    carry, h_meta = _mlstm_chunk(carry0, tuple(a[:, :, :N_META] for a in seqs))
    _, h_real = lax.scan(_mlstm_chunk, carry, tuple(chunks(a) for a in seqs))
    h_real = jnp.moveaxis(h_real, 0, 2).reshape(bsz, N_HEADS, T - N_META, DV)
    h = jnp.concatenate([h_meta, h_real], axis=2).transpose(0, 2, 1, 3)
    h = h * lax.rsqrt(jnp.mean(h * h, axis=-1, keepdims=True) + RMS_EPS)
    h = h * head_norm_w.astype(jnp.float32).reshape(N_HEADS, DV)
    h = h.reshape(bsz, T, E_MLSTM).astype(u.dtype) * jax.nn.sigmoid(o) * jax.nn.silu(z)
    return h @ w_out

def second_inputs(seed: int = 0) -> dict:
    key = jax.random.key(seed)
    ks = jax.random.split(key, 12)
    f32 = jnp.float32
    x = jax.random.normal(ks[0], (BATCH, SEQ, D_MODEL), f32)
    meta_tokens = jax.random.normal(ks[1], (N_META, D_MODEL), f32)
    norm_w = 1.0 + 0.05 * jax.random.normal(ks[2], (DEPTH_2, D_MODEL), f32)
    conv_in_w = jax.random.normal(ks[3], (N_A, D_MODEL, 4 * E_CONV), f32) * D_MODEL ** -0.5
    conv_w = jax.random.normal(ks[4], (N_A, CONV_WIDTH, E_CONV), f32) * CONV_WIDTH ** -0.5
    conv_out_w = jax.random.normal(ks[5], (N_A, E_CONV, D_MODEL), f32) * E_CONV ** -0.5
    n_in = 2 * QK + 3 * E_MLSTM + 2 * N_HEADS
    mlstm_in_w = jax.random.normal(ks[6], (N_B, D_MODEL, n_in), f32) * D_MODEL ** -0.5
    i_bias = 0.1 * jax.random.normal(ks[7], (N_B, N_HEADS), f32)
    f_bias = jnp.linspace(3.0, 6.0, N_HEADS, dtype=f32)[None, :] + 0.1 * jax.random.normal(ks[8], (N_B, N_HEADS), f32)
    mlstm_gate_b = jnp.concatenate([i_bias, f_bias], axis=-1)
    mlstm_head_norm_w = 1.0 + 0.05 * jax.random.normal(ks[9], (N_B, E_MLSTM), f32)
    mlstm_out_w = jax.random.normal(ks[10], (N_B, E_MLSTM, D_MODEL), f32) * E_MLSTM ** -0.5
    final_norm_w = 1.0 + 0.05 * jax.random.normal(ks[11], (D_MODEL,), f32)
    return {"x": x, "meta_tokens": meta_tokens, "norm_w": norm_w, "conv_in_w": conv_in_w,
            "conv_w": conv_w, "conv_out_w": conv_out_w, "mlstm_in_w": mlstm_in_w,
            "mlstm_gate_b": mlstm_gate_b, "mlstm_head_norm_w": mlstm_head_norm_w,
            "mlstm_out_w": mlstm_out_w, "final_norm_w": final_norm_w}

def second_block(x, meta_tokens, norm_w, conv_in_w, conv_w, conv_out_w, mlstm_in_w,
              mlstm_gate_b, mlstm_head_norm_w, mlstm_out_w, final_norm_w):
    bsz = x.shape[0]
    meta = jnp.broadcast_to(meta_tokens.astype(x.dtype)[None], (bsz, N_META, D_MODEL))
    h = jnp.concatenate([meta, x], axis=1)
    for i in range(DEPTH_2):
        u = _rmsnorm(h, norm_w[i])
        j = i // N_MIXERS
        if i % N_MIXERS == 0:
            h = h + _short_conv_mixer(u, conv_in_w[j], conv_w[j], conv_out_w[j])
        else:
            h = h + _mlstm_mixer(u, mlstm_in_w[j], mlstm_gate_b[j], mlstm_head_norm_w[j], mlstm_out_w[j])
    h = _rmsnorm(h, final_norm_w)
    return h[:, N_META:]


def setup_inputs(seed=0):
    out = dict(first_inputs(seed))
    for name, value in second_inputs(seed + 1).items():
        if name != "x":
            out[name + "_2"] = value
    return out


def reference(
    x, c, w_ada, b_ada, g_pre, g_post, w_in, pe_cmp_k, pe_cmp_v, w_cmp_k1, w_cmp_k2, w_cmp_v1,
    w_cmp_v2, w_o_nsa, w_o_swa, w_out, sinks, meta_tokens_2, norm_w_2, conv_in_w_2, conv_w_2,
    conv_out_w_2, mlstm_in_w_2, mlstm_gate_b_2, mlstm_head_norm_w_2, mlstm_out_w_2,
    final_norm_w_2,
):
    x = first_block(
        x, c, w_ada, b_ada, g_pre, g_post, w_in, pe_cmp_k, pe_cmp_v, w_cmp_k1, w_cmp_k2,
        w_cmp_v1, w_cmp_v2, w_o_nsa, w_o_swa, w_out, sinks,
    )
    return second_block(
        x, meta_tokens_2, norm_w_2, conv_in_w_2, conv_w_2, conv_out_w_2, mlstm_in_w_2,
        mlstm_gate_b_2, mlstm_head_norm_w_2, mlstm_out_w_2, final_norm_w_2,
    )


_drawn_inputs = setup_inputs


def setup_inputs(seed=0):
    import zlib

    import numpy as np

    out = dict(_drawn_inputs(seed))
    spreads = {}
    factors = {'b_ada': 2.928, 'pe_cmp_k': 45.209, 'pe_cmp_v': 8.0, 'mlstm_head_norm_w_2': 4.69}
    for name, (base, spread) in spreads.items():
        noise = np.random.default_rng([zlib.crc32(name.encode()), seed]).standard_normal(out[name].shape)
        drawn = base * np.exp(spread * noise) if base else spread * noise
        out[name] = __import__('jax').numpy.asarray(drawn.astype(out[name].dtype))
    for name, factor in factors.items():
        out[name] = (out[name] * factor).astype(out[name].dtype)
    return out
```

```python
import numpy as np

import concourse.bass as bass
from concourse import mybir
from concourse.alu_op_type import AluOpType as ALU
from contextlib import ExitStack, contextmanager

F32 = mybir.dt.float32
F32R = mybir.dt.float32r
ACT = mybir.ActivationFunctionType
AX = mybir.AxisListType

P = 128
D = 1024
KD = D // P
T1 = 512
META = 16
T2 = META + T1
EPS = 1e-6
NEG = -1e30
DH = 64
NH = 8
QT = T1 // P
NPAIR = NH // 2
CB, CS = 32, 16
NC = (T1 - CB) // CS + 1
WINDOW = 128
LH = 4
DK, DV = 256, 512
KE = 2 * D // P
CHUNK = 2048

TB1 = [(0, 0, T1)]
TB2 = [(0, 0, META + 256), (1, META + 256, 256)]
STILES = [(0, META)] + [(META + P * j, P) for j in range(T1 // P)]

N_ADA = 8
N_PROJ, N_CMP, N_ATT, N_WO, N_OUT = 8, 4, 16, 4, 4
N_CIN, N_COUT, N_MLSTM = 32, 8, 40
STAGES = dict(proj=N_PROJ, cmp=N_CMP, att=N_ATT, wo=N_WO, out=N_OUT,
              cin=N_CIN, cout=N_COUT, mlstm=N_MLSTM)
START = {}
for _name, _n in STAGES.items():
    START[_name] = sum(v for k, v in list(STAGES.items())[:len(START)])
N_CHUNKS = sum(STAGES.values())
N_SMALL = 16


class Counter:

    def __init__(self, name, sem, known):
        self.name, self.sem, self.known, self.n = name, sem, known, 0
        self.loop, self.outer, self.loops = None, 0, {}

    def enter(self, loop):
        self.loop, self.outer, self.n = loop, self.n, 0

    def leave(self, trips):
        self.loops[self.loop] = (self.outer, self.n)
        self.n = self.outer + trips * self.n
        self.loop = None


class Engine:

    def __init__(self, eng, counters, known, points):
        self.e, self.counters, self.known, self.points = eng, counters, known, points
        self.own = counters[0]
        self.loop = None
        self.i = 0

    @contextmanager
    def trips(self, name, count):
        for c in self.counters:
            c.enter(name)
        self.loop = name
        with self.e.bass.Fori(0, count, 1, engines=[self.e.engine]) as i:
            self.i = i
            yield i
        for c in self.counters:
            c.leave(count)
        self.loop, self.i = None, 0

    def done(self, ins, point=None, counter=None):
        c = counter or self.own
        ins.then_inc(c.sem, 1)
        c.n += 1
        if point:
            self.points[point] = (c.name, c.loop, c.n)
        return ins

    def value(self, name, loop, local, lag=0):
        if loop is None:
            return local
        first, per, trips = self.known["loops"][name, loop]
        if loop == self.loop:
            assert first + local - lag * per >= 0
            return self.i * per + (first + local - lag * per)
        return first + (trips - 1) * per + local

    def wait(self, point, lag=0):
        if point in self.known["points"]:
            name, loop, local = self.known["points"][point]
            self.e.wait_ge(self.known["sems"][name], self.value(name, loop, local, lag))
        else:
            assert not self.known["points"], point

    def after_own(self):
        if self.known["points"]:
            self.e.wait_ge(self.own.sem, self.value(self.own.name, self.loop, self.own.n))


def build(nc, known, wstream, w_ada, x_t, meta_t, c_t, b_ada, g_pre, g_post, w_gate, pe_k, pe_v, w_k2, w_v2,
          sinks, norm_w, conv_w, w_mgate, mgate_b, head_w, out_t):
    points, ctx = {}, ExitStack()
    with ctx:
        def sb(name, shape, dt=F32, stack=ctx, side="left"):
            return stack.enter_context(nc.sbuf_tensor(name, [P] + list(shape), dt, side=side))

        def psum(name, shape):
            return ctx.enter_context(nc.psum_tensor(name, [P] + list(shape), F32))

        def sem(name):
            return ctx.enter_context(nc.semaphore(name))

        raw_full = [sem("raw_full0"), sem("raw_full1")]
        s_hi = sem("chunk_hi")
        s_lo = sem("chunk_lo")
        s_small = sem("small_in")
        s_x = sem("x_in")
        s_x2 = sem("x_again")
        s_const = sem("const")
        s_ada = [sem(f"ada{i}") for i in range(N_ADA)]
        s_out = sem("out_stored")
        s_pe, s_chunk, s_act, s_dve = sem("pe"), sem("pe_chunk"), sem("act"), sem("dve")
        known["sems"] = dict(pe=s_pe, chunk=s_chunk, act=s_act, dve=s_dve)

        lin = [psum("lin0", [2, 512]), psum("lin1", [2, 512])]
        aux = [psum(f"aux{i}", [512]) for i in range(4)]

        raw = [sb(f"w_raw{i}", [CHUNK]) for i in range(2)]
        whi = [sb(f"w_hi{i}", [CHUNK], F32R) for i in range(2)]
        wlo = [sb(f"w_lo{i}", [CHUNK], F32R) for i in range(2)]
        xhi = sb("x_hi", [KD, T2], F32R)
        xlo = sb("x_lo", [KD, T2], F32R)
        res = sb("residual", [KD, T2])
        ident = sb("ident", [P])
        ones = sb("ones", [P])
        tmp = sb("tmp", [2, T2])
        sq = sb("squares", [2, T2])
        ssum = sb("square_sum", [T2])
        rstd = sb("rstd", [T2])
        mask = sb("mask", [P])
        eps = sb("eps", [1])
        norm_c = sb("norm_c", [3, KD])
        conv_c = sb("conv_c", [KE, 3])
        head_c = sb("head_c", [KE])
        mb_c = sb("mgate_b_c", [1])

        one, stage_c, stage_d = ExitStack(), ExitStack(), ExitStack()

        def sb1(name, shape, dt=F32):
            return sb(name, shape, dt, one)

        K_C, V_C, K_S, V_S, K_W, V_W, Q_B, K_B, V_B = 4, 5, 6, 7, 8, 9, 10, 14, 15
        o_tok = sb1("o_tok", [2, 2, P])
        dist = sb1("dist", [T1])
        dist_w = sb1("dist_w", [2 * P])
        dist_c = sb1("dist_c", [QT, 32])
        c_in = sb1("c_in", [KD])
        c_hi = sb1("c_hi", [KD, 2], F32R)
        c_lo = sb1("c_lo", [KD, 2], F32R)
        bada = sb1("b_ada_c", [24])
        mod = sb1("mod", [24])
        gpre = sb1("g_pre_c", [KD])
        gpost = sb1("g_post_c", [KD])
        scale_c = sb1("scale_c", [KD])
        gate = sb1("gates", [QT, 24])
        gcur = sb1("gates_pair", [2, QT, 3])
        slopes = sb1("slopes", [NH])
        scur = sb1("slopes_pair", [2])
        sink_c = sb1("sinks_c", [NH])
        sinkcur = sb1("sinks_pair", [2])
        seen = sb1("cmp_seen", [1])
        nmaxs = sb1("neg_max", [2, 4])
        prob_ss = sb1("prob_sum", [2, 4])
        coefs = sb1("coef", [2, 4])
        pe_c = sb1("pe_c", [2, CB])
        kct = sb1("kc_T", [2 * NC])
        vct = sb1("vc_tok", [2, DH])
        wg = sb("w_gate_raw", [KD, 24], stack=stage_c)
        wg_hi = sb("w_gate_hi", [KD, 24], F32R, stage_c)
        wg_lo = sb("w_gate_lo", [KD, 24], F32R, stage_c)
        w2k = sb("w_cmp_k2", [2, P], stack=stage_c)
        w2v = sb("w_cmp_v2", [2, DH], stack=stage_c)
        cmp_th = sb("cmp_th", [2 * NC], stack=stage_c)
        hid = sb("cmp_hid", [2, 2, 2 * NC], stack=stage_c)
        stage_a = ExitStack()
        ada_w = sb("ada_shift_scale", [N_ADA, CHUNK], stack=stage_a, side="right")
        stage_a.close()
        proj = sb("proj", [16, T1], stack=stage_d, side="right")
        probs = [sb(f"prob{i}", [1316], stack=stage_d, side="right") for i in range(2)]
        probs_T = [sb(f"prob_T{i}", [1408], stack=stage_d, side="right") for i in range(2)]
        cin = sb("cmp_in", [CB // 2, 2, NC], stack=stage_c)
        cin_hi = [sb(f"cmp_in_hi{s}", [CB // 2, 2, NC], F32R, stage_c) for s in range(2)]
        cin_lo = [sb(f"cmp_in_lo{s}", [CB // 2, 2, NC], F32R, stage_c) for s in range(2)]
        stage_c.close()
        zz = sb1("z", [2, NPAIR, T1])
        m_a = sb1("merge_a", [KD, T1])
        m_b = res
        stage_d.close()
        stage_e = ExitStack()
        yhi = sb("y_hi", [KD, T1], F32R, stage_e, "right")
        ylo = sb("y_lo", [KD, T1], F32R, stage_e, "right")
        stage_e.close()
        one.close()

        two, conv, ml = ExitStack(), ExitStack(), ExitStack()
        vhi = sb("conv_hi", [KE, T2], F32R, conv)
        vlo = sb("conv_lo", [KE, T2], F32R, conv)
        cb = sb("conv_b", [T2], stack=conv)
        cc = sb("conv_c_gate", [T2], stack=conv)
        cv = sb("conv_in", [2 + T2], stack=conv)
        cy = sb("conv_y", [T2], stack=conv)
        cz = sb("conv_tanh", [T2], stack=conv)
        conv.close()

        def sb2(name, shape, dt=F32):
            return sb(name, shape, dt, ml)

        ghi = sb2("mix_hi", [4, T2], F32R)
        glo = sb2("mix_lo", [4, T2], F32R)
        qk = sb2("qk_T", [4, T2])
        v_T = sb2("v_T", [4, T2])
        v_tok = sb2("v_tok", [len(STILES), DV])
        att = sb2("att_T", [len(STILES), T2])
        oz = sb2("oz", [4, T2])
        neg_m = sb2("neg_m", [LH, T2])
        e_m = sb2("e_m", [LH, T2])
        rden = sb2("rden", [T2])
        u_c = sb2("u_c", [len(STILES), LH])
        ucur = sb2("u_head", [len(STILES)])
        hcur = sb2("head_w_cur", [4])
        ml.close()
        rows = sb("gate_rows", [7, T2], stack=two)
        wm = sb("w_mgate_raw", [KD, P], stack=two)
        wm_hi = sb("w_mgate_hi", [KD, P], F32R, two)
        wm_lo = sb("w_mgate_lo", [KD, P], F32R, two)
        sel = sb("select", [LH, P], stack=two)
        two.close()

        loops = {}
        pe_n, ch_n = Counter("pe", s_pe, known), Counter("chunk", s_chunk, known)
        act_n, dve_n = Counter("act", s_act, known), Counter("dve", s_dve, known)
        block = ctx.enter_context(nc.Block())


        @block.sync
        def _(eng):
            for c in range(N_ADA):
                eng.dma_start(ada_w[:, c, :], w_ada[c, :, :]).then_inc(s_ada[c], 16)
            for h in range(2):
                eng.dma_start(raw[h][:], wstream[h, :, :]).then_inc(raw_full[h], 16)
            with eng.bass.Fori(0, N_CHUNKS // 2 - 1, 1, engines=[eng.engine]) as i:
                for h in range(2):
                    eng.wait_ge(s_lo, i * 2 + (h + 1))
                    eng.dma_start(raw[h][:], wstream[bass.ds(i * 2 + (h + 2), 1), :, :]
                                  .rearrange("a p n -> (a p) n")).then_inc(raw_full[h], 16)
            eng.wait_ge(s_lo, N_CHUNKS - 1)
            eng.dma_start(raw[0][:], wstream[N_CHUNKS, :, :]).then_inc(raw_full[0], 16)
            eng.wait_ge(s_out, 16 * KD)

        @block.gpsimd
        def _(eng):
            small = [(c_in[:], c_t), (bada[:], b_ada), (gpre[:], g_pre), (gpost[:], g_post), (wg[:], w_gate),
                     (sink_c[:], sinks), (w2k[:], w_k2), (w2v[:], w_v2), (norm_c[:], norm_w),
                     (conv_c[:], conv_w), (head_c[:], head_w), (mb_c[:], mgate_b),
                     (pe_c[0:DH, 0, :], pe_k), (pe_c[DH:P, 0, :], pe_k),
                     (pe_c[0:DH, 1, :], pe_v), (pe_c[DH:P, 1, :], pe_v)]
            assert len(small) == N_SMALL
            for dst, src in small:
                eng.dma_start(dst, src).then_inc(s_small, 16)
            eng.memset(ident[:], 0.0).then_inc(s_const, 1)
            eng.memset(ones[:], 1.0).then_inc(s_const, 1)
            eng.memset(mask[:], 0.0).then_inc(s_const, 1)
            eng.memset(eps[:], EPS).then_inc(s_const, 1)
            for h in range(NH):
                eng.memset(slopes[:, h:h + 1], 2.0 ** -(8.0 * (h + 1) / NH)).then_inc(s_const, 1)
            eng.memset(seen[:], 1.0).then_inc(s_const, 1)
            eng.iota(dist[:], [[1, T1]], base=-(T1 - P), channel_multiplier=-1,
                     allow_small_or_imprecise_dtypes=True).then_inc(s_const, 1)
            eng.iota(dist_c[:], [[-P, QT], [CS, 32]], base=CB - 1, channel_multiplier=-1,
                     allow_small_or_imprecise_dtypes=True).then_inc(s_const, 1)
            eng.wait_ge(s_const, 15)
            eng.affine_select(out=ident[:], in_=ident[:], compare_op=ALU.not_equal, fill=1.0, base=0,
                              pattern=[[-1, P]], channel_multiplier=1).then_inc(s_const, 1)
            eng.affine_select(out=mask[:], in_=mask[:], compare_op=ALU.is_ge, fill=NEG, base=0,
                              pattern=[[1, P]], channel_multiplier=-1).then_inc(s_const, 1)
            eng.affine_select(out=seen[:], in_=seen[:], compare_op=ALU.is_ge, fill=0.0, base=-(CB - 1),
                              pattern=[[0, 1]], channel_multiplier=1).then_inc(s_const, 1)
            eng.affine_select(out=dist[:], in_=dist[:], compare_op=ALU.is_ge, fill=NEG, base=T1 - P,
                              pattern=[[-1, T1]], channel_multiplier=1).then_inc(s_const, 1)
            eng.affine_select(out=dist_c[:], in_=dist_c[:], compare_op=ALU.is_ge, fill=NEG, base=-(CB - 1),
                              pattern=[[P, QT], [-CS, 32]], channel_multiplier=1).then_inc(s_const, 1)
            eng.wait_ge(s_const, 20)
            eng.affine_select(out=dist_w[:], in_=dist[:, T1 - 2 * P:T1], compare_op=ALU.is_gt, fill=NEG,
                              base=0, pattern=[[1, 2 * P]], channel_multiplier=-1).then_inc(s_const, 1)
            with eng.bass.Fori(0, N_CHUNKS // 2, 1, engines=[eng.engine]) as i:
                for h in range(2):
                    eng.wait_ge(s_hi, i * 2 + (h + 1))
                    eng.tensor_tensor(wlo[h][:], raw[h][:], whi[h][:].bitcast(F32), ALU.subtract).then_inc(s_lo, 1)
            eng.wait_ge(s_hi, N_CHUNKS + 1)
            eng.tensor_tensor(wlo[0][:], raw[0][:], whi[0][:].bitcast(F32), ALU.subtract).then_inc(s_lo, 1)


        def chunk_lands_and_splits(a, per, first):
            h = first % 2
            a.e.wait_ge(raw_full[h], a.i * (8 * per) + 16 * (first // 2 + 1) if per else 16 * (first // 2 + 1))
            if per:
                a.e.wait_ge(s_chunk, a.i * per + (N_ADA + first - 1))
            elif first > 1:
                a.e.wait_ge(s_chunk, N_ADA + first - 1)
            a.e.activation(whi[h][:], raw[h][:], ACT.Copy).then_inc(s_hi, 1)

        def all_chunks(a, stage):
            a.e.wait_ge(s_chunk, N_ADA + START[stage] + STAGES[stage])

        def chunk_ready(t, per, first):
            t.e.wait_ge(s_lo, t.i * per + (first + 1) if per else first + 1)

        def group(t, half, col, stride, kts, outs, hi_of, lo_of, point=None, chunk_end=False, part=None):
            ks = range(kts) if part is None else range(part * kts // 2, (part + 1) * kts // 2)
            n = 3 * ks[0]
            for k in ks:
                c0 = k * stride + col
                for w, x in ((whi, hi_of), (whi, lo_of), (wlo, hi_of)):
                    for o, (_, t0, cnt) in outs:
                        ins = t.e.matmul(o, w[half][:, c0:c0 + P], x(k, t0, cnt), start=(n == 0),
                                         stop=(n == 3 * kts - 1))
                    n += 1
            if part != 0:
                t.done(ins, point, ch_n if chunk_end else None)

        def lin_outs(slot, tbs):
            return [(lin[slot][:, b, 0:n], (b, t0, n)) for b, t0, n in tbs]

        def x_hi(k, t0, n):
            return xhi[:, k, t0:t0 + n]

        def x_lo(k, t0, n):
            return xlo[:, k, t0:t0 + n]


        def norm_squares_act(a, nm, src, t0, n, tiles, ready=None):
            for k in range(tiles):
                if ready:
                    a.wait(f"{ready}{k}")
                if k >= 2:
                    a.wait(f"{nm}_add{k - 2}")
                a.done(a.e.activation(sq[:, k % 2, 0:n], src(k, t0, n), ACT.Square), f"{nm}_sq{k}")

        def norm_adds_dve(v, nm, n, tiles):
            for k in range(tiles):
                v.wait(f"{nm}_sq{k}")
                if k == 1:
                    v.done(v.e.tensor_tensor(ssum[:, 0:n], sq[:, 0, 0:n], sq[:, 1, 0:n], ALU.add), f"{nm}_add1")
                elif k > 1:
                    v.after_own()
                    v.done(v.e.tensor_tensor(ssum[:, 0:n], ssum[:, 0:n], sq[:, k % 2, 0:n], ALU.add), f"{nm}_add{k}")
                else:
                    points[f"{nm}_add0"] = (v.own.name, v.loop, v.own.n + 1)

        def norm_total_pe(t, nm, tbs, tiles, banks=(2, 3)):
            t.wait(f"{nm}_add{tiles - 1}")
            for (b, t0, n), bank in zip(tbs, banks):
                t.done(t.e.matmul(aux[bank][:, 0:n], ones[:], ssum[:, t0:t0 + n], start=True, stop=True),
                       f"{nm}_tot{b}")

        def norm_root_act(a, nm, tbs, width, banks=(2, 3)):
            for (b, t0, n), bank in zip(tbs, banks):
                a.wait(f"{nm}_tot{b}")
                a.done(a.e.activation(rstd[:, t0:t0 + n], aux[bank][:, 0:n], ACT.Sqrt, bias=eps[:], scale=1.0 / width),
                       f"{nm}_root")

        def norm_invert_dve(v, nm, n):
            v.wait(f"{nm}_root")
            v.done(v.e.reciprocal(rstd[:, 0:n], rstd[:, 0:n]), f"{nm}_rstd")
            v.after_own()

        def norm_apply_dve(v, nm, src, t0, n, weight):
            def low(k):
                v.wait(f"{nm}_hi{k}")
                v.done(v.e.tensor_tensor(xlo[:, k, 0:n], tmp[:, k % 2, 0:n], xhi[:, k, 0:n].bitcast(F32), ALU.subtract),
                       f"{nm}_lo{k}")
            for k in range(KD):
                v.after_own()
                v.done(v.e.scalar_tensor_tensor(tmp[:, k % 2, 0:n], src(k, t0, n), weight(k), rstd[:, 0:n],
                                                ALU.mult, ALU.mult), f"{nm}_n{k}")
                if k >= 1:
                    low(k - 1)
            low(KD - 1)

        def norm_high_act(a, nm, n):
            for k in range(KD):
                a.wait(f"{nm}_n{k}")
                a.done(a.e.activation(xhi[:, k, 0:n], tmp[:, k % 2, 0:n], ACT.Copy), f"{nm}_hi{k}")

        def residual(k, t0, n):
            return res[:, k, t0:t0 + n]

        v_banks = [aux[2], aux[3], lin[0][:, 1, :]]

        def att_banks(e):
            return (aux[0], aux[1], aux[2]) if e == 0 else (aux[3], lin[0][:, 1, :], lin[1][:, 1, :])

        def v_of(tile, j, e):
            return proj[:, tile, P * j + e * DH:P * j + (e + 1) * DH]

        SBLOCKS = [(b, max(STILES[j][0], t0), t0 + n - max(STILES[j][0], t0), j)
                   for b, t0, n in TB2 for j in range(len(STILES)) if STILES[j][0] < t0 + n]

        PAIR = [(e * DH, e * DH + DH) for e in range(2)]


        @block.tensor
        def _(eng):
            t = Engine(eng, [pe_n, ch_n], known, points)

            def ada_group(half, col, out, point, chunk_end):
                n = 0
                for k in range(KD):
                    c0 = k * 256 + col
                    for w, x in ((whi, c_hi), (whi, c_lo), (wlo, c_hi)):
                        ins = eng.matmul(out, w[half][:, c0:c0 + P], x[:, k, :], start=(n == 0), stop=(n == 3 * KD - 1))
                        n += 1
                t.done(ins, point, ch_n if chunk_end else None)

            eng.wait_ge(s_small, 16 * N_SMALL)
            for c in range(N_ADA):
                eng.wait_ge(s_ada[c], 16)
                for g in range(2):
                    j = 2 * c + g
                    for k in range(KD):
                        ins = eng.matmul(aux[0][:, j:j + 1], ada_w[:, c, k * 256 + g * P:k * 256 + g * P + P],
                                         c_in[:, k:k + 1], start=(k == 0), stop=(k == KD - 1))
                t.done(ins, None, ch_n)
            eng.wait_ge(s_const, 21)
            norm_total_pe(t, "n0", TB1, KD)

            t.wait(f"n0b_lo{KD - 1}")
            with t.trips("proj", 2):
                for c in range(4):
                    chunk_ready(t, 4, START["proj"] + c)
                    for g in range(2):
                        j = 2 * c + g
                        t.wait(f"proj_ev{(j - 2) % 8}", 0 if j >= 2 else 1)
                        group(t, c % 2, g * P, 256, KD, lin_outs(g, TB1), x_hi, x_lo, f"proj_g{j}", g == 1)
            t.wait("wg_split")
            for i in range(QT):
                n = 0
                for k in range(KD):
                    for x, w in ((xhi, wg_hi), (xlo, wg_hi), (xhi, wg_lo)):
                        ins = eng.matmul(aux[1][:, 24 * i:24 * i + 24], x[:, k, P * i:P * i + P], w[:, k, :],
                                         start=(n == 0), stop=(n == 3 * KD - 1))
                        n += 1
            t.done(ins, "gates")

            t.wait("proj_ev7")
            t.wait("n0_root")
            for s, tile in enumerate((V_S, V_W, V_B)):
                for i in range(QT):
                    ins = eng.transpose(v_banks[s][:, P * i:P * i + P], proj[:, tile, P * i:P * i + P], ident[:])
                t.done(ins, f"vt{s}")

            for src in range(2):
                t.wait(f"cin_lo{src}")
                if src == 1:
                    t.wait("vtok2")
                for j in range(2):
                    c = 2 * src + j
                    chunk_ready(t, 0, START["cmp"] + c)
                    n = 0
                    for k in range(16):
                        for w, x in ((whi, cin_hi[src]), (whi, cin_lo[src]), (wlo, cin_hi[src])):
                            ins = eng.matmul(lin[j][:, src, 0:2 * NC], w[c % 2][:, k * P:k * P + P],
                                             x[:, k, :, :].rearrange("p g j -> p (g j)"), start=(n == 0), stop=(n == 47))
                            n += 1
                    t.done(ins, None, ch_n)
            t.wait("gate_th")
            t.wait("hid0")
            for j in range(2):
                ins = eng.matmul(aux[0][:, 0:2 * NC], w2k[:, j, :], hid[:, 0, j, :], start=(j == 0), stop=(j == 1))
            t.done(ins, "kc")
            t.wait("hid1")
            for g in range(2):
                for j in range(2):
                    ins = eng.matmul(aux[1][0:NC, 128 + g * DH:128 + (g + 1) * DH], hid[:, 1, j, g * NC:(g + 1) * NC],
                                     w2v[:, j, :], start=(j == 0), stop=(j == 1))
            t.done(ins, "vc")

            t.wait("kvc_ready")
            t.wait("vtok2")
            with t.trips("att", NPAIR):
                def scores(s):
                    i, e = divmod(s, 2)
                    lo, hi = PAIR[e]
                    b = att_banks(e)
                    keys, k0 = P * (i + 1), max(0, P * (i - 1))
                    if s >= 2:
                        t.wait(f"out{s - 2}")
                    if e == 0 and i >= 2:
                        t.wait(f"o_T_ev{i - 2}")
                    qa = proj[lo:hi, K_C, P * i:P * i + P]
                    qb = proj[lo:hi, V_C, P * i:P * i + P]
                    eng.matmul(b[0][:, 0:keys], qa, proj[lo:hi, K_S, 0:keys], start=True, stop=True)
                    eng.matmul(b[1][:, 0:keys], qa, proj[lo:hi, K_W, 0:keys], start=True, stop=True)
                    eng.matmul(b[2][:, 0:NC], qa, kct[lo:hi, e * NC:(e + 1) * NC], start=True, stop=True)
                    w0 = 32 + (P if i == 0 else 0)
                    t.done(eng.matmul(b[2][:, w0:w0 + keys - k0], qb, proj[lo:hi, K_B, k0:keys], start=True, stop=True),
                           f"s{s}")

                def turn_outputs(i):
                    t.wait(f"out{2 * i + 1}")
                    for x in range(2):
                        ins = eng.transpose(aux[1][:, P * x:P * x + P], o_tok[:, i % 2, x, :], ident[:])
                    t.done(ins, f"o_T{i}")

                t.wait("staged")
                scores(0)
                for s in range(2 * QT):
                    i, e = divmod(s, 2)
                    b = att_banks(e)
                    prob, prob_T = probs[e], probs_T[e]
                    c, g = divmod(s, 2)
                    if g == 0:
                        chunk_ready(t, 4, START["att"] + c)
                    if s >= 2:
                        t.wait(f"att_ev{s - 2}")
                    if c < 3:
                        group(t, c % 2, g * P, 256, KD, lin_outs(g, TB1), x_hi, x_lo, part=0)
                    else:
                        ada_group(c % 2, g * P, lin[g][:, 0, 0:2], f"att_g{s}", g == 1)
                    t.wait(f"exp{s}")
                    for j in range(i + 1):
                        eng.transpose(b[0][:, P * j:P * j + P], prob[:, P * j:P * j + P], ident[:])
                    for j in range(i + 1):
                        eng.transpose(b[1][:, P * j:P * j + P], prob[:, 512 + P * j:512 + P * j + P], ident[:])
                    eng.transpose(b[2][0:NC, 0:P], prob[:, 1024:1024 + NC], ident[:])
                    js = (1,) if i == 0 else (0, 1)
                    for j in js:
                        ins = eng.transpose(b[2][:, P + P * j:2 * P + P * j],
                                            prob[:, 1056 + P * j:1056 + P * j + P], ident[:])
                    t.done(ins, f"pt{s}")
                    if s + 1 < 2 * QT:
                        scores(s + 1)
                    if c < 3:
                        group(t, c % 2, g * P, 256, KD, lin_outs(g, TB1), x_hi, x_lo, f"att_g{s}", g == 1, part=1)
                    t.wait(f"pt_ev{s}_act")
                    t.wait(f"pt_ev{s}_dve")
                    o = b[0]
                    eng.matmul(o[:, 0:DH], prob_T[0:NC, 1024:1152], vct[0:NC, e, :], start=True, stop=True)
                    for x, tile in ((0, V_S), (1, V_W)):
                        for j in range(i + 1):
                            eng.matmul(o[:, DH * (x + 1):DH * (x + 2)], prob_T[:, 512 * x + P * j:512 * x + P * j + P],
                                       v_of(tile, j, e), start=(j == 0), stop=(j == i))
                    for j in js:
                        ins = eng.matmul(o[:, 3 * DH:4 * DH], prob_T[:, 1152 + P * j:1152 + P * j + P],
                                         v_of(V_B, i - 1 + j, e), start=(j == js[0]), stop=(j == 1))
                    t.done(ins, f"pv{s}")
                    if e == 0 and i:
                        turn_outputs(i - 1)
                turn_outputs(QT - 1)
                t.wait(f"o_T_ev{QT - 1}")

            t.wait(f"og_lo{KD - 1}")
            t.wait("att_ev6")
            t.wait("att_ev7")
            for c in range(N_WO):
                chunk_ready(t, 0, START["wo"] + c)
                for m in range(2):
                    for x in range(2):
                        j = 4 * c + 2 * m + x
                        if j >= 2:
                            t.wait(f"wo_ev{j - 2}")
                        group(t, c % 2, x * 1024 + m * P, 256, 4, lin_outs(x, TB1),
                              lambda k, t0, n, x=x: x_hi(4 * x + k, t0, n), lambda k, t0, n, x=x: x_lo(4 * x + k, t0, n),
                              f"wo_g{j}", m == 1 and x == 1)
            t.wait(f"y_lo{KD - 1}")
            t.wait("wo_ev14")
            for c in range(N_OUT):
                chunk_ready(t, 0, START["out"] + c)
                for g in range(2):
                    j = 2 * c + g
                    if j >= 2:
                        t.wait(f"out_ev{j - 2}")
                    else:
                        t.wait(f"wo_ev{14 + j}")
                    group(t, c % 2, g * P, 256, KD, lin_outs(g, TB1), lambda k, t0, n: yhi[:, k, t0:t0 + n],
                          lambda k, t0, n: ylo[:, k, t0:t0 + n], f"out_g{j}", g == 1)
            norm_total_pe(t, "n1", TB1, KD)
            norm_total_pe(t, "n2", TB2, KD)

            t.wait(f"n2b_lo{KD - 1}")
            with t.trips("cin", 8):
                for c in range(4):
                    chunk_ready(t, 4, START["cin"] + c)
                    for g in range(2):
                        j = 2 * c + g
                        t.wait(f"cin_ev{(j - 2) % 8}", 0 if j >= 2 else 1)
                        group(t, c % 2, g * P, 256, KD, lin_outs(g, TB2), x_hi, x_lo, f"cin_g{j}", g == 1)
            t.wait("conv_lo1")
            t.wait("cin_ev6")
            t.wait("cin_ev7")
            with t.trips("cout", 2):
                for c in range(4):
                    chunk_ready(t, 4, START["cout"] + c)
                    t.wait(f"cout_ev{(c - 2) % 4}", 0 if c >= 2 else 1)
                    group(t, c % 2, 0, P, KE, lin_outs(c % 2, TB2), lambda k, t0, n: vhi[:, k, t0:t0 + n],
                          lambda k, t0, n: vlo[:, k, t0:t0 + n], None, True)
            norm_total_pe(t, "n3", TB2, KD)

            t.wait(f"n3b_lo{KD - 1}")
            t.wait("wm_split")
            for b, t0, n in TB2:
                m = 0
                for k in range(KD):
                    for w, x in ((wm_hi, xhi), (wm_hi, xlo), (wm_lo, xhi)):
                        ins = eng.matmul(aux[b][:, 0:n], w[:, k, :], x[:, k, t0:t0 + n], start=(m == 0), stop=(m == 3 * KD - 1))
                        m += 1
            t.done(ins, "mgates")
            t.wait("rows_done")
            t.wait("rows_em")
            for x in range(2):
                for h in range(LH):
                    for b, t0, n in TB2:
                        q = (x * LH + h) * 2 + b
                        if q >= 2:
                            t.wait(f"bc_ev{q - 2}")
                        t.done(eng.matmul(aux[2 + b][:, 0:n], sel[0:LH, h, :], rows[0:LH, 5 + x, t0:t0 + n],
                                          start=True, stop=True), f"bc{q}")
            for j, (s0, ln) in enumerate(STILES):
                ins = eng.transpose(aux[0][0:ln, LH * j:LH * j + LH], rows[0:LH, 4, s0:s0 + ln], ident[0:LH, 0:LH])
            t.done(ins, "u_T")

            t.wait("ml_ready")
            with t.trips("mlstm", LH):
                def projections(chunks):
                    for c in chunks:
                        chunk_ready(t, 10, START["mlstm"] + c)
                        for g in range(2):
                            j = 2 * c + g
                            t.wait(f"ml_ev{j - 2}" if j >= 2 else f"mlo_ev{6 + j}", 0 if j >= 2 else 1)
                            group(t, c % 2, g * P, 256, KD, lin_outs(g, TB2), x_hi, x_lo, f"ml_g{j}", g == 1)
                projections(range(4))
                t.wait("ml_ev7")
                q = 0
                for j, (s0, ln) in enumerate(STILES):
                    if j >= 2:
                        t.wait(f"vtk{j - 2}")
                    else:
                        t.wait("hn_root", 1)
                    for vt in range(4):
                        ins = eng.transpose(aux[2 + j % 2][0:ln, P * vt:P * vt + P], v_T[:, vt, s0:s0 + ln], ident[:])
                    t.done(ins, f"vtr{j}")
                for q, (b, t0, n, j) in enumerate(SBLOCKS):
                    s0, ln = STILES[j]
                    if q >= 2:
                        t.wait(f"st_ev{q - 2}")
                    for k in range(2):
                        ins = eng.matmul(aux[q % 2][0:ln, 0:n], qk[:, 2 + k, s0:s0 + ln], qk[:, k, t0:t0 + n],
                                         start=(k == 0), stop=(k == 1))
                    t.done(ins, f"st{q}")
                projections(range(4, 6))
                t.wait(f"st_ev{len(SBLOCKS) - 1}")
                t.wait(f"vtk{len(STILES) - 1}")
                for x in range(5):
                    for b, t0, n in TB2:
                        q = 2 * x + b
                        if x >= 1:
                            t.wait(f"h_ev{q - 2}")
                        js = [j for j, (s0, _) in enumerate(STILES) if s0 < t0 + n]
                        for j in js:
                            s0, ln = STILES[j]
                            f = max(s0, t0)
                            w = ones[0:ln, :] if x == 0 else v_tok[0:ln, j, P * (x - 1):P * x]
                            ins = eng.matmul(aux[2 + b][:, f - t0:n], w, att[0:ln, j, f:t0 + n],
                                             start=(j == 0), stop=(j == js[-1]))
                        t.done(ins, f"h{q}")
                projections(range(6, 7))
                norm_total_pe(t, "hn", TB2, 4)
                projections(range(7, 8))
                t.wait("g_lo3")
                for c in range(8, 10):
                    chunk_ready(t, 10, START["mlstm"] + c)
                    for g in range(4):
                        j = 4 * (c - 8) + g
                        t.wait(f"mlo_ev{j - 2}" if j >= 2 else f"ml_ev{14 + j}")
                        group(t, c % 2, g * P, 512, 4, lin_outs(g % 2, TB2), lambda k, t0, n: ghi[:, k, t0:t0 + n],
                              lambda k, t0, n: glo[:, k, t0:t0 + n], f"mlo_g{j}", g == 3)
            norm_total_pe(t, "n4", TB1, KD)
            loops.update({(c.name, k): v for c in (pe_n, ch_n) for k, v in c.loops.items()})


        @block.scalar
        def _(eng):
            a = Engine(eng, [act_n], known, points)
            act = eng.activation

            eng.dma_start(res[:, :, META:T2], x_t).then_inc(s_x, 16)
            eng.dma_start(res[:, :, 0:META], meta_t).then_inc(s_x, 16)
            eng.wait_ge(s_x, 32)
            norm_squares_act(a, "n0", residual, META, T1, KD)
            chunk_lands_and_splits(a, 0, 0)
            eng.wait_ge(s_const, 21)
            norm_root_act(a, "n0", TB1, D)
            for k in range(KD):
                a.wait(f"n0b_n{k}")
                a.done(act(xhi[:, k, 0:T1], tmp[:, k % 2, 0:T1], ACT.Identity, bias=mod[:, k:k + 1]), f"n0b_hi{k}")

            with a.trips("proj", 2):
                for c in range(4):
                    chunk_lands_and_splits(a, 4, START["proj"] + c + 1)
            a.wait("gates")
            a.done(act(gate[:].rearrange("p i b -> p (i b)"), aux[1][:, 0:24 * QT], ACT.Tanh, scale=0.5), "gate_th")
            for src in range(2):
                a.wait(f"cin_sum{src}")
                a.done(act(cin_hi[src][:], cin[:], ACT.Copy), f"cin_hi{src}")
            for src in range(2):
                for j in range(2):
                    c = 2 * src + j
                    chunk_lands_and_splits(a, 0, START["cmp"] + c + 1)
                    eng.wait_ge(s_chunk, N_ADA + START["cmp"] + c + 1)
                    if c:
                        a.wait(f"hid_use{c - 1}")
                    a.done(act(cmp_th[:], lin[j][:, src, 0:2 * NC], ACT.Tanh, scale=0.5), f"cmp_th{c}")

            with a.trips("att", NPAIR):
                def exps(s):
                    i, e = divmod(s, 2)
                    keys, w0 = P * (i + 1), 1056 + (P if i == 0 else 0)
                    a.wait(f"max{s}")
                    spans = [(1024, 1024 + NC), (0, keys), (512, 512 + keys), (w0, 1313)]
                    for x, (p0, p1) in enumerate(spans):
                        a.done(act(probs[e][:, p0:p1], probs[e][:, p0:p1], ACT.Exp, bias=nmaxs[:, e, x:x + 1],
                                   accum_out=prob_ss[:, e, x:x + 1]), f"exp{s}")

                for s in range(2 * QT):
                    i, e = divmod(s, 2)
                    c, g = divmod(s, 2)
                    if g == 0:
                        chunk_lands_and_splits(a, 4, START["att"] + c + 1)
                    if s == 0:
                        exps(0)
                    a.wait(f"pt{s}")
                    keys = P * (i + 1)
                    a.done(act(probs_T[e][:, 0:keys], att_banks(e)[0][:, 0:keys], ACT.Copy), f"pt_ev{s}_act")
                    if s + 1 < 2 * QT:
                        exps(s + 1)
                    if c in (0, 1, 2):
                        if g == 1:
                            eng.wait_ge(s_chunk, a.i * 4 + (N_ADA + START["att"] + c + 1))
                        else:
                            a.wait(f"att_g{s}")
                        src = lin[g][:, 0, 0:T1]
                        if c == 0:
                            a.done(act(tmp[:, g, 0:T1], src, ACT.Tanh, scale=0.5), f"z_th{g}")
                        else:
                            dst = m_a[:, bass.ds(a.i * 2 + g, 1), :] if c == 1 else \
                                m_b[:, bass.ds(a.i * 2 + g, 1), META:T2]
                            a.done(act(dst.rearrange("p a n -> p (a n)"), src, ACT.Tanh, scale=0.5), f"att_ev{s}")

            for k in range(KD):
                a.wait(f"og{k}")
                a.done(act(xhi[:, k, 0:T1], tmp[:, k % 2, 0:T1], ACT.Copy), f"og_hi{k}")
            for c in range(N_WO):
                chunk_lands_and_splits(a, 0, START["wo"] + c + 1)
                for m in range(2):
                    k = 2 * c + m
                    a.wait(f"y{k}")
                    a.done(act(yhi[:, k, :], tmp[:, 1, 0:T1], ACT.Copy), f"y_hi{k}")
            eng.dma_start(res[:, :, META:T2], x_t).then_inc(s_x2, 16)
            for c in range(N_OUT):
                chunk_lands_and_splits(a, 0, START["out"] + c + 1)
                for g in range(2):
                    j = 2 * c + g
                    if g == 0:
                        a.wait(f"out_g{j}")
                    else:
                        eng.wait_ge(s_chunk, N_ADA + START["out"] + c + 1)
                    a.done(act(m_a[:, j, :], lin[g][:, 0, 0:T1], ACT.Copy, scale=0.5), f"out_ev{j}")
            a.after_own()
            norm_squares_act(a, "n1", lambda k, t0, n: m_a[:, k, 0:n], 0, T1, KD)
            norm_root_act(a, "n1", TB1, D)
            norm_squares_act(a, "n2", residual, 0, T2, KD, "x1_")
            norm_root_act(a, "n2", TB2, D)
            norm_high_act(a, "n2b", T2)

            def slot_full(stage, per, c, g, point):
                if g == 1:
                    eng.wait_ge(s_chunk, a.i * per + (N_ADA + START[stage] + c + 1))
                else:
                    a.wait(point)

            with a.trips("cin", 8):
                for c in range(4):
                    u = c // 2
                    chunk_lands_and_splits(a, 4, START["cin"] + c + 1)
                    if c % 2 == 0:
                        for g, dst in ((0, cb), (1, cc)):
                            slot_full("cin", 4, c, g, f"cin_g{2 * c}")
                            a.wait(f"conv_lo{1 - u}", 0 if u else 1)
                            for b, t0, n in TB2:
                                a.done(act(dst[:, t0:t0 + n], lin[g][:, b, 0:n], ACT.Copy), f"cin_ev{2 * c + g}")
                    else:
                        slot_full("cin", 4, c, 1, None)
                        for b, t0, n in TB2:
                            a.done(act(cz[:, t0:t0 + n], lin[1][:, b, 0:n], ACT.Tanh, scale=0.5), f"conv_th{u}")
                        a.wait(f"conv{u}")
                        a.done(act(vhi[:, bass.ds(a.i * 2 + u, 1), :].rearrange("p a n -> p (a n)"), tmp[:, u, :], ACT.Copy),
                               f"conv_hi{u}")
            with a.trips("cout", 2):
                for c in range(4):
                    chunk_lands_and_splits(a, 4, START["cout"] + c + 1)
            a.wait("cout_ev3")
            norm_squares_act(a, "n3", residual, 0, T2, KD)
            norm_root_act(a, "n3", TB2, D)
            norm_high_act(a, "n3b", T2)

            all_chunks(a, "cout")
            eng.dma_start(wm[:], w_mgate).then_inc(s_x2, 16)
            a.wait("rows_f")
            a.done(act(rows[0:LH, 2, :], rows[0:LH, 1, :], ACT.Abs))
            a.after_own()
            a.done(act(rows[0:LH, 2, :], rows[0:LH, 2, :], ACT.Exp, scale=-1.0))
            a.after_own()
            a.done(act(rows[0:LH, 2, :], rows[0:LH, 2, :], ACT.Ln, bias=1.0), "rows_ln")
            a.wait("rows_m")
            a.done(act(rows[0:LH, 6, :], rows[0:LH, 6, :], ACT.Exp, scale=-1.0), "rows_em")

            with a.trips("mlstm", LH):
                def evacs(c):
                    for g in range(2):
                        j = 2 * c + g
                        slot_full("mlstm", 10, c, g, f"ml_g{j}")
                        if j < 4:
                            dst = qk[:, j, :]
                        elif j < 8:
                            dst = v_T[:, j - 4, :]
                        elif j < 12:
                            dst = oz[:, j - 8, :]
                        if j >= 12:
                            a.wait(f"oz{j - 13}" if j > 12 else "g_lo3", 0 if j > 12 else 1)
                            for b, t0, n in TB2:
                                a.done(act(tmp[:, 0, t0:t0 + n], lin[g][:, b, 0:n], ACT.Tanh, scale=0.5), f"z_ml{j - 12}")
                        else:
                            fn = ACT.Tanh if j >= 8 else ACT.Copy
                            for b, t0, n in TB2:
                                a.done(act(dst[:, t0:t0 + n], lin[g][:, b, 0:n], fn, scale=0.5 if j >= 8 else 1.0),
                                       f"ml_ev{j}")

                for c in range(4):
                    chunk_lands_and_splits(a, 10, START["mlstm"] + c + 1)
                    if c == 0:
                        a.wait("g_lo3", 1)
                    evacs(c)
                a.wait("masked")
                for j, (s0, ln) in enumerate(STILES):
                    if s0 + ln < T2:
                        a.done(act(att[0:ln, j, s0 + ln:T2], neg_m[0:ln, bass.ds(a.i, 1), s0 + ln:T2]
                                   .rearrange("p a n -> p (a n)"), ACT.Exp, bias=ucur[0:ln, j:j + 1]))
                    a.done(act(att[0:ln, j, s0:s0 + ln], att[0:ln, j, s0:s0 + ln], ACT.Exp, bias=ucur[0:ln, j:j + 1]),
                           f"decay{j}")
                for c in (4, 5):
                    chunk_lands_and_splits(a, 10, START["mlstm"] + c + 1)
                    evacs(c)
                for b, t0, n in TB2:
                    a.wait(f"h{b}")
                    a.done(act(rden[:, t0:t0 + n], aux[2 + b][:, 0:n], ACT.Abs), f"h_ev{b}")
                chunk_lands_and_splits(a, 10, START["mlstm"] + 7)
                norm_squares_act(a, "hn", lambda k, t0, n: v_T[:, k, t0:t0 + n], 0, T2, 4, "h_done")
                evacs(6)
                chunk_lands_and_splits(a, 10, START["mlstm"] + 8)
                norm_root_act(a, "hn", TB2, DV)
                evacs(7)
                chunk_lands_and_splits(a, 10, START["mlstm"] + 9)
                for k in range(4):
                    a.wait(f"g{k}")
                    a.done(act(ghi[:, k, :], tmp[:, 1, :], ACT.Copy), f"g_hi{k}")
                chunk_lands_and_splits(a, 10, START["mlstm"] + 10)
            a.wait("mlo_ev7")
            norm_squares_act(a, "n4", residual, META, T1, KD)
            norm_root_act(a, "n4", TB1, D)
            for k in range(KD):
                a.wait(f"out_t{k}")
                eng.dma_start(out_t[P * k:P * k + P, :], res[:, k, META:T2]).then_inc(s_out, 16)
            loops.update({("act", k): v for k, v in act_n.loops.items()})



        @block.vector
        def _(eng):
            v = Engine(eng, [dve_n], known, points)
            tt, ts, stt, copy = eng.tensor_tensor, eng.tensor_scalar, eng.scalar_tensor_tensor, eng.tensor_copy

            def move(out, src):
                return ts(out, src, 1.0, None, ALU.mult)

            def flat(ap):
                return ap.rearrange("p a n -> p (a n)")

            eng.wait_ge(s_small, 16 * N_SMALL)
            for j in range(2):
                v.done(copy(c_hi[:, :, j], c_in[:]))
            v.done(copy(wg_hi[:], wg[:]))
            v.after_own()
            for j in range(2):
                v.done(tt(c_lo[:, :, j], c_in[:], c_hi[:, :, j].bitcast(F32), ALU.subtract), "c_split")
            v.done(tt(wg_lo[:], wg[:], wg_hi[:].bitcast(F32), ALU.subtract), "wg_split")

            norm_adds_dve(v, "n0", T1, KD)
            eng.wait_ge(s_chunk, N_ADA)
            v.done(tt(mod[:, 0:16], aux[0][:, 0:16], bada[:, 0:16], ALU.add))
            v.after_own()
            v.done(stt(scale_c[:], mod[:, 8:16], 1.0, gpre[:], ALU.add, ALU.mult))
            norm_invert_dve(v, "n0", T1)

            def low(k):
                v.wait(f"n0b_hi{k}")
                v.done(stt(xlo[:, k, 0:T1], tmp[:, k % 2, 0:T1], mod[:, k:k + 1], xhi[:, k, 0:T1].bitcast(F32),
                           ALU.add, ALU.subtract), f"n0b_lo{k}")
            for k in range(KD):
                v.after_own()
                v.done(stt(tmp[:, k % 2, 0:T1], res[:, k, META:T2], scale_c[:, k:k + 1], rstd[:, 0:T1],
                           ALU.mult, ALU.mult), f"n0b_n{k}")
                if k:
                    low(k - 1)
            low(KD - 1)

            def tile_full(stage, per, c, last, point):
                if last:
                    eng.wait_ge(s_chunk, v.i * per + (N_ADA + START[stage] + c + 1) if per
                                else N_ADA + START[stage] + c + 1)
                else:
                    v.wait(point)

            with v.trips("proj", 2):
                for c in range(4):
                    for g in range(2):
                        j = 2 * c + g
                        tile_full("proj", 4, c, g == 1, f"proj_g{j}")
                        v.done(move(flat(proj[:, bass.ds(v.i * 8 + j, 1), :]), lin[g][:, 0, :]), f"proj_ev{j}")
            v.after_own()

            for src in range(2):
                if src:
                    v.wait(f"cin_hi{src - 1}")
                    v.after_own()
                for g in range(2):
                    gs = slice(g * DH, (g + 1) * DH)
                    rows_of = proj[gs, K_C + src, :].rearrange("p (j a r) -> p r a j", a=8, r=2)
                    emb = pe_c[gs, src, :].rearrange("p (a r) -> p r a", r=2)
                    for r in range(2):
                        for a1 in range(2):
                            v.done(tt(cin[r * DH:(r + 1) * DH, 8 * a1:8 * a1 + 8, g, :], rows_of[:, r, :, a1:a1 + NC],
                                      emb[:, r, 8 * a1:8 * a1 + 8].unsqueeze(2).to_broadcast([DH, 8, NC]), ALU.add),
                                   f"cin_sum{src}")
                v.wait(f"cin_hi{src}")
                v.done(tt(cin_lo[src][:], cin[:], cin_hi[src][:].bitcast(F32), ALU.subtract), f"cin_lo{src}")
            for s, tile in enumerate((V_S, V_W, V_B)):
                v.wait(f"vt{s}")
                v.done(copy(proj[:, tile, :], v_banks[s][:, 0:T1]), f"vtok{s}")
            v.wait("gate_th")
            v.done(ts(gate[:], gate[:], 0.5, 0.5, ALU.mult, ALU.add))
            v.after_own()
            eng.wait_ge(s_const, 21)
            v.done(ts(gate[:, 0, 0:NH], gate[:, 0, 0:NH], seen[:], None, ALU.mult))
            for src in range(2):
                for j in range(2):
                    c = 2 * src + j
                    v.wait(f"cmp_th{c}")
                    v.done(stt(hid[:, src, j, :], cmp_th[:], 1.0, lin[j][:, src, 0:2 * NC], ALU.add, ALU.mult),
                           f"hid_use{c}")
                points[f"hid{src}"] = ("dve", None, v.own.n)
            v.wait("kc")
            v.done(ts(kct[:], aux[0][:, 0:2 * NC], 0.5, None, ALU.mult))
            v.wait("vc")
            v.done(ts(vct[0:NC, :, :].rearrange("p g d -> p (g d)"), aux[1][0:NC, 128:256], 0.5, None, ALU.mult),
                   "kvc_ready")

            with v.trips("att", NPAIR):
                v.done(ts(proj[:, K_C, :], flat(proj[:, bass.ds(v.i, 1), :]), DH ** -0.5, None, ALU.mult))
                v.done(ts(proj[:, V_C, :], flat(proj[:, bass.ds(v.i + Q_B, 1), :]), DH ** -0.5, None, ALU.mult))
                for e in range(2):
                    v.done(move(scur[:, e:e + 1], slopes[:, bass.ds(v.i + 4 * e, 1)]))
                    v.done(move(sinkcur[:, e:e + 1], sink_c[:, bass.ds(v.i + 4 * e, 1)]))
                    for br in range(3):
                        v.done(move(gcur[:, e, :, br:br + 1], gate[:, :, bass.ds(v.i + (4 * e + NH * br), 1)]), "staged")
                v.after_own()
                def maxima(s):
                    i, e = divmod(s, 2)
                    b, prob = att_banks(e), probs[e]
                    keys, k0, w0 = P * (i + 1), max(0, P * (i - 1)), (P if i == 0 else 0)
                    v.wait(f"s{s}")
                    v.after_own()
                    sl = scur[:, e:e + 1]
                    v.done(stt(prob[:, 1024:1024 + NC], dist_c[:, i, 0:NC], sl, b[2][:, 0:NC], ALU.mult, ALU.add))
                    v.done(stt(prob[:, 0:keys], dist[:, T1 - keys:T1], sl, b[0][:, 0:keys], ALU.mult, ALU.add))
                    v.done(stt(prob[:, 512:512 + keys], dist[:, T1 - keys:T1], sl, b[1][:, 0:keys], ALU.mult, ALU.add))
                    v.done(stt(prob[:, 1056 + w0:1312], dist_w[:, w0:2 * P], sl, b[2][:, 32 + w0:32 + w0 + keys - k0],
                               ALU.mult, ALU.add))
                    v.done(copy(prob[:, 1312:1313], sinkcur[:, e:e + 1]))
                    v.after_own()
                    spans = [(1024, 1024 + NC), (0, keys), (512, 512 + keys), (1056 + w0, 1313)]
                    for x, (p0, p1) in enumerate(spans):
                        v.done(eng.tensor_reduce(nmaxs[:, e, x:x + 1], prob[:, p0:p1], AX.X, ALU.max, negate=True),
                               f"max{s}")

                def outputs_turned(i):
                    v.wait(f"o_T{i}")
                    for x in range(2):
                        v.done(move(flat(proj[:, bass.ds(v.i + Q_B * x, 1), P * i:P * i + P]),
                                    aux[1][:, P * x:P * x + P]), f"o_T_ev{i}")

                maxima(0)
                for s in range(2 * QT):
                    i, e = divmod(s, 2)
                    b, prob_T, coef = att_banks(e), probs_T[e], coefs[:, e, :]
                    keys, w0 = P * (i + 1), (P if i == 0 else 0)
                    v.wait(f"pt{s}")
                    v.done(copy(prob_T[0:NC, 1024:1152], b[2][0:NC, 0:P]))
                    v.done(copy(prob_T[:, 1152 + w0:1408], b[2][:, P + w0:3 * P]))
                    v.done(copy(prob_T[:, 512:512 + keys], b[1][:, 0:keys]), f"pt_ev{s}_dve")
                    v.wait(f"exp{s}")
                    v.done(eng.reciprocal(coef, prob_ss[:, e, :]))
                    v.after_own()
                    v.done(tt(coef[:, 0:3], coef[:, 0:3], gcur[:, e, i, :], ALU.mult))
                    if s + 1 < 2 * QT:
                        maxima(s + 1)
                    v.wait(f"pv{s}")
                    v.after_own()
                    o, es = b[0], slice(e * DH, (e + 1) * DH)
                    o_a, o_b = o_tok[:, i % 2, 0, es], o_tok[:, i % 2, 1, es]
                    v.done(ts(o_a, o[:, 0:DH], coef[:, 0:1], None, ALU.mult))
                    v.done(ts(o_b, o[:, 3 * DH:4 * DH], coef[:, 3:4], None, ALU.mult))
                    for x in (1, 2):
                        v.after_own()
                        v.done(stt(o_a, o[:, x * DH:(x + 1) * DH], coef[:, x:x + 1], o_a, ALU.mult, ALU.add), f"out{s}")
                    c, g = divmod(s, 2)
                    if c == 0:
                        v.wait(f"z_th{g}")
                        v.done(stt(flat(zz[:, g, bass.ds(v.i, 1), :]), tmp[:, g, 0:T1], 1.0, lin[g][:, 0, :],
                                   ALU.add, ALU.mult), f"att_ev{s}")
                    if c == 3:
                        tile_full("att", 4, c, g == 1, f"att_g{s}")
                        v.done(tt(mod[:, bass.ds(v.i * 2 + (16 + g), 1)], lin[g][:, 0, 0:1],
                                  bada[:, bass.ds(v.i * 2 + (16 + g), 1)], ALU.add), f"att_ev{s}")
                    if e == 0 and i:
                        outputs_turned(i - 1)
                outputs_turned(QT - 1)
                v.after_own()

            all_chunks(v, "att")

            def low_og(k):
                v.wait(f"og_hi{k}")
                v.done(tt(xlo[:, k, 0:T1], tmp[:, k % 2, 0:T1], xhi[:, k, 0:T1].bitcast(F32), ALU.subtract), f"og_lo{k}")
            for k in range(KD):
                x, pr = divmod(k, NPAIR)
                v.after_own()
                v.done(stt(tmp[:, k % 2, 0:T1], zz[:, x, pr, :], 0.5, proj[:, Q_B * x + pr, :], ALU.mult, ALU.mult), f"og{k}")
                if k:
                    low_og(k - 1)
            low_og(KD - 1)
            for k in range(KD):
                c, m = divmod(k, 2)
                v.wait(f"wo_g{2 * k}")
                v.after_own()
                v.done(stt(tmp[:, 0, 0:T1], m_a[:, k, :], 1.0, lin[0][:, 0, :], ALU.add, ALU.mult), f"wo_ev{2 * k}")
                tile_full("wo", 0, c, m == 1, f"wo_g{2 * k + 1}")
                v.done(stt(sq[:, 0, 0:T1], m_b[:, k, META:T2], 1.0, lin[1][:, 0, :], ALU.add, ALU.mult), f"wo_ev{2 * k + 1}")
                v.after_own()
                v.done(tt(tmp[:, 1, 0:T1], tmp[:, 0, 0:T1], sq[:, 0, 0:T1], ALU.add), f"y{k}")
                v.wait(f"y_hi{k}")
                v.done(tt(ylo[:, k, :], tmp[:, 1, 0:T1], yhi[:, k, :].bitcast(F32), ALU.subtract), f"y_lo{k}")
            v.done(tt(gpost[:], gpost[:], mod[:, 16:24], ALU.mult))
            norm_adds_dve(v, "n1", T1, KD)
            norm_invert_dve(v, "n1", T1)
            eng.wait_ge(s_x2, 16)
            for k in range(KD):
                v.after_own()
                v.done(stt(tmp[:, k % 2, 0:T1], m_a[:, k, :], gpost[:, k:k + 1], rstd[:, 0:T1], ALU.mult, ALU.mult))
                v.after_own()
                v.done(tt(res[:, k, META:T2], res[:, k, META:T2], tmp[:, k % 2, 0:T1], ALU.add), f"x1_{k}")
            norm_adds_dve(v, "n2", T2, KD)
            norm_invert_dve(v, "n2", T2)
            norm_apply_dve(v, "n2b", residual, 0, T2, lambda k: norm_c[:, 0, k:k + 1])

            v.done(eng.memset(cv[:, 0:2], 0.0))
            with v.trips("cin", 8):
                for u in range(2):
                    f = bass.ds(v.i * 2 + u, 1)
                    v.wait(f"cin_ev{4 * u + 1}")
                    v.wait(f"cin_g{4 * u + 2}")
                    v.after_own()
                    for b, t0, n in TB2:
                        v.done(tt(cv[:, 2 + t0:2 + t0 + n], cc[:, t0:t0 + n], lin[0][:, b, 0:n], ALU.mult),
                               f"cin_ev{4 * u + 2}")
                    v.after_own()
                    v.done(ts(cy[:], cv[:, 0:T2], flat(conv_c[:, f, 0:1]), None, ALU.mult))
                    for w in (1, 2):
                        v.after_own()
                        v.done(stt(cy[:], cv[:, w:w + T2], flat(conv_c[:, f, w:w + 1]), cy[:], ALU.mult, ALU.add))
                    v.after_own()
                    v.done(tt(cy[:], cy[:], cb[:], ALU.mult))
                    v.wait(f"conv_th{u}")
                    for b, t0, n in TB2:
                        v.done(stt(cz[:, t0:t0 + n], cz[:, t0:t0 + n], 1.0, lin[1][:, b, 0:n], ALU.add, ALU.mult),
                               f"cin_ev{4 * u + 3}")
                    v.after_own()
                    v.done(stt(tmp[:, u, :], cy[:], 0.5, cz[:], ALU.mult, ALU.mult), f"conv{u}")
                    v.wait(f"conv_hi{u}")
                    v.done(tt(flat(vlo[:, f, :]), tmp[:, u, :], flat(vhi[:, f, :]).bitcast(F32), ALU.subtract),
                           f"conv_lo{u}")
            with v.trips("cout", 2):
                for c in range(4):
                    tile_full("cout", 4, c, True, None)
                    r = bass.ds(v.i * 4 + c, 1)
                    for b, t0, n in TB2:
                        v.done(tt(flat(res[:, r, t0:t0 + n]), flat(res[:, r, t0:t0 + n]), lin[c % 2][:, b, 0:n], ALU.add),
                               f"cout_ev{c}")
            norm_adds_dve(v, "n3", T2, KD)
            norm_invert_dve(v, "n3", T2)
            norm_apply_dve(v, "n3b", residual, 0, T2, lambda k: norm_c[:, 1, k:k + 1])

            eng.wait_ge(s_x2, 32)
            v.done(copy(wm_hi[:], wm[:]))
            for h in range(LH):
                v.done(ts(sel[0:LH, h, :], ones[0:LH, :], ident[0:LH, h:h + 1], None, ALU.mult))
            v.after_own()
            v.done(tt(wm_lo[:], wm[:], wm_hi[:].bitcast(F32), ALU.subtract), "wm_split")
            v.done(eng.memset(rows[0:LH, 5, :], 0.0))
            v.done(eng.memset(u_c[:], 0.0))
            row = [rows[0:LH, r, :] for r in range(7)]
            v.wait("mgates")
            for b, t0, n in TB2:
                v.done(ts(rows[0:LH, 0, t0:t0 + n], aux[b][0:LH, 0:n], mb_c[0:LH, :], None, ALU.add))
                v.done(ts(rows[0:LH, 1, t0:t0 + n], aux[b][32:32 + LH, 0:n], mb_c[32:32 + LH, :], None, ALU.add), "rows_f")
            v.after_own()
            v.done(ts(row[3], row[1], 0.0, None, ALU.min))
            v.wait("rows_ln")
            v.after_own()
            v.done(tt(row[3], row[3], row[2], ALU.subtract))
            v.after_own()
            v.done(eng.tensor_tensor_scan(row[1], row[3], row[5], 0.0, ALU.add, ALU.add))
            v.after_own()
            v.done(tt(row[4], row[0], row[1], ALU.subtract))
            v.after_own()
            v.done(eng.tensor_tensor_scan(row[3], row[4], row[5], 0.0, ALU.max, ALU.max))
            v.after_own()
            v.done(tt(row[6], row[1], row[3], ALU.add), "rows_m")
            v.done(ts(row[5], row[3], -1.0, None, ALU.mult), "rows_done")
            for x, dst in enumerate((neg_m, e_m)):
                for h in range(LH):
                    for b, t0, n in TB2:
                        q = (x * LH + h) * 2 + b
                        v.wait(f"bc{q}")
                        v.done(copy(dst[:, h, t0:t0 + n], aux[2 + b][:, 0:n]), f"bc_ev{q}")
            v.wait("u_T")
            for j, (s0, ln) in enumerate(STILES):
                v.done(copy(u_c[0:ln, j, :], aux[0][0:ln, LH * j:LH * j + LH]), "ml_ready")
            v.after_own()

            with v.trips("mlstm", LH):
                hd = bass.ds(v.i, 1)
                v.done(move(ucur[:], u_c[:, :, hd].rearrange("p j a -> p (j a)")))
                v.done(move(hcur[:], head_c[:, bass.ds(v.i * 4, 4)]))
                for j, (s0, ln) in enumerate(STILES):
                    v.done(tt(att[0:ln, j, s0:s0 + ln], flat(neg_m[0:ln, hd, s0:s0 + ln]), mask[0:ln, 0:ln], ALU.add), "masked")
                for j, (s0, ln) in enumerate(STILES):
                    v.wait(f"vtr{j}")
                    v.done(copy(v_tok[0:ln, j, :], aux[2 + j % 2][0:ln, :]), f"vtk{j}")
                v.wait(f"decay{len(STILES) - 1}")
                for q, (b, t0, n, j) in enumerate(SBLOCKS):
                    ln = STILES[j][1]
                    v.wait(f"st{q}")
                    v.after_own()
                    v.done(stt(att[0:ln, j, t0:t0 + n], att[0:ln, j, t0:t0 + n], DK ** -0.5, aux[q % 2][0:ln, 0:n],
                               ALU.mult, ALU.mult), f"st_ev{q}")
                v.wait("h_ev1")
                v.done(tt(rden[:], rden[:], flat(e_m[:, hd, :]), ALU.max))
                v.after_own()
                v.done(eng.reciprocal(rden[:], rden[:]))
                v.after_own()
                for x in range(1, 5):
                    for b, t0, n in TB2:
                        v.wait(f"h{2 * x + b}")
                        v.done(tt(v_T[:, x - 1, t0:t0 + n], aux[2 + b][:, 0:n], rden[:, t0:t0 + n], ALU.mult),
                               f"h_ev{2 * x + b}")
                    points[f"h_done{x - 1}"] = ("dve", "mlstm", v.own.n)
                norm_adds_dve(v, "hn", T2, 4)
                v.after_own()

                def output_gates(k):
                    v.wait(f"z_ml{k}")
                    for b, t0, n in TB2:
                        v.done(stt(sq[:, 1, t0:t0 + n], tmp[:, 0, t0:t0 + n], 1.0, lin[k % 2][:, b, 0:n], ALU.add, ALU.mult),
                               f"ml_ev{12 + k}")
                    v.after_own()
                    v.done(stt(oz[:, k, :], oz[:, k, :], 1.0, sq[:, 1, :], ALU.add, ALU.mult), f"oz{k}")
                    v.after_own()
                output_gates(0)
                output_gates(1)
                norm_invert_dve(v, "hn", T2)
                output_gates(2)
                output_gates(3)
                for k in range(4):
                    v.after_own()
                    v.done(stt(tmp[:, 1, :], v_T[:, k, :], hcur[:, k:k + 1], rstd[:], ALU.mult, ALU.mult))
                    v.after_own()
                    v.done(stt(tmp[:, 1, :], tmp[:, 1, :], 0.25, oz[:, k, :], ALU.mult, ALU.mult), f"g{k}")
                    v.wait(f"g_hi{k}")
                    v.done(tt(glo[:, k, :], tmp[:, 1, :], ghi[:, k, :].bitcast(F32), ALU.subtract), f"g_lo{k}")
                    v.after_own()
                for j in range(KD):
                    c, g = divmod(j, 4)
                    tile_full("mlstm", 10, 8 + c, g == 3, f"mlo_g{j}")
                    for b, t0, n in TB2:
                        v.done(tt(res[:, j, t0:t0 + n], res[:, j, t0:t0 + n], lin[j % 2][:, b, 0:n], ALU.add), f"mlo_ev{j}")
            norm_adds_dve(v, "n4", T1, KD)
            norm_invert_dve(v, "n4", T1)
            for k in range(KD):
                v.done(stt(res[:, k, META:T2], res[:, k, META:T2], norm_c[:, 2, k:k + 1], rstd[:, 0:T1],
                           ALU.mult, ALU.mult), f"out_t{k}")
            loops.update({("dve", k): val for k, val in dve_n.loops.items()})
    trips = dict(proj=2, att=NPAIR, cin=8, cout=2, mlstm=LH)
    return points, {k: (first, per, trips[k[1]]) for k, (first, per) in loops.items()}



def lay_out(i):
    def chunks(w, cols):
        k, n = w.shape
        return w.reshape(k // P, P, n // cols, cols).transpose(2, 1, 0, 3).reshape(n // cols, P, k // P * cols)

    def pairs(w, axis):
        s = list(w.shape)
        w = w.reshape(s[:axis] + [2, NPAIR, DH] + s[axis + 1:])
        return np.ascontiguousarray(np.swapaxes(w, axis, axis + 1)).reshape(s)

    def per_partition(a):
        return np.ascontiguousarray(a.reshape(-1, P).T)

    i = {k: np.asarray(a) for k, a in i.items()}
    ada, win = i['w_ada'][0], i['w_in'][0]
    q_a, kv3, g_n, z_a, q_b, kv_b, z_b, m_a, m_b = np.split(win, [512, 1280, 1304, 1816, 2328, 2584, 3096, 4120], axis=1)
    q_a, q_b, z_a, z_b = (pairs(w, 1) for w in (q_a, q_b, z_a, z_b))
    out = [chunks(np.concatenate([q_a, kv3, q_b, kv_b], 1), 256),
           chunks(i['w_cmp_k1'][0], P), chunks(i['w_cmp_v1'][0], P)]
    for t in range(NPAIR):
        cols = slice(P * t, P * t + P)
        wide = slice(256 * t, 256 * t + 256)
        out.append(chunks(np.concatenate([z_a[:, cols], z_b[:, cols], m_a[:, wide], m_b[:, wide],
                                          ada[:, 2 * D:][:, wide]], 1), 256))
    wo = [chunks(pairs(i[n][0], 0), 256) for n in ('w_o_nsa', 'w_o_swa')]
    out.append(np.concatenate(wo, 2))
    out.append(chunks(i['w_out'][0], 256))
    b_c_x_z = i['conv_in_w_2'][0].reshape(D, 4, KE, P)
    out.append(chunks(np.ascontiguousarray(b_c_x_z.transpose(0, 2, 1, 3)).reshape(D, -1), 256))
    out.append(chunks(i['conv_out_w_2'][0], P))
    q, k, v, o, z, g = np.split(i['mlstm_in_w_2'][0], [1024, 2048, 4096, 6144, 8192], axis=1)
    for h in range(LH):
        a, b = slice(DK * h, DK * (h + 1)), slice(DV * h, DV * (h + 1))
        out.append(chunks(np.concatenate([q[:, a], k[:, a], v[:, b], o[:, b], z[:, b]], 1), 256))
        out.append(chunks(i['mlstm_out_w_2'][0][b], 512))
    out.append(np.zeros((1, P, CHUNK), np.float32))
    stream = np.concatenate(out, 0)
    assert stream.shape == (N_CHUNKS + 1, P, CHUNK)
    w_mgate = np.zeros((D, P), np.float32)
    w_mgate[:, 0:LH], w_mgate[:, 32:32 + LH] = g[:, :LH], g[:, LH:]
    mgate_b = np.zeros((P, 1), np.float32)
    mgate_b[0:LH, 0], mgate_b[32:32 + LH, 0] = i['mlstm_gate_b_2'][0, :LH], i['mlstm_gate_b_2'][0, LH:]

    def tiles(w):
        return np.ascontiguousarray(w.reshape(-1, P, w.shape[1]).transpose(1, 0, 2))
    w2k = i['w_cmp_k2'][0]
    return dict(
        wstream=stream, w_ada=np.ascontiguousarray(chunks(ada[:, :2 * D], 256)), x_t=tiles(i['x'][0].T), meta_t=tiles(i['meta_tokens_2'].T), c_t=per_partition(i['c']),
        b_ada=per_partition(i['b_ada']), g_pre=per_partition(i['g_pre']), g_post=per_partition(i['g_post']),
        w_gate=tiles(g_n), pe_k=np.ascontiguousarray(i['pe_cmp_k'][0].T), pe_v=np.ascontiguousarray(i['pe_cmp_v'][0].T),
        w_k2=tiles(np.concatenate([w2k, w2k], 1)), w_v2=tiles(i['w_cmp_v2'][0]),
        sinks=np.ascontiguousarray(np.broadcast_to(i['sinks'], (P, NH))),
        norm_w=np.ascontiguousarray(np.stack([per_partition(i['norm_w_2'][0]), per_partition(i['norm_w_2'][1]),
                                              per_partition(i['final_norm_w_2'])], 1)),
        conv_w=np.ascontiguousarray(i['conv_w_2'][0].reshape(3, KE, P).transpose(2, 1, 0)),
        w_mgate=tiles(w_mgate), mgate_b=mgate_b, head_w=per_partition(i['mlstm_head_norm_w_2']),
    )


def kernel(**inputs):
    import concourse.bacc as _bacc
    from concourse import mybir as _mybir
    from concourse.bass_utils import run_bass_kernel_spmd as _run

    arrays = lay_out(inputs)
    known = dict(points={}, loops={}, sems={})
    for _ in range(2):
        nc = _bacc.Bacc("TRN2", target_bir_lowering=False, num_devices=1)
        args = {n: nc.dram_tensor(n, a.shape, _mybir.dt.from_np(a.dtype), kind="ExternalInput").ap()
                for n, a in arrays.items()}
        out = nc.dram_tensor("out_t", (D, T1), _mybir.dt.float32, kind="ExternalOutput").ap()
        points, loops = build(nc, known, out_t=out, **args)
        known = dict(points=points, loops=loops, sems={})
    r = _run(nc, [arrays], core_ids=[0])
    return np.ascontiguousarray(r.results[0]["out_t"].T).reshape(1, T1, D)
```

```python
import numpy as np

import concourse.bass as bass
from concourse import mybir
from concourse.alu_op_type import AluOpType as ALU
from contextlib import ExitStack, contextmanager

F32 = mybir.dt.float32
F32R = mybir.dt.float32r
ACT = mybir.ActivationFunctionType
AX = mybir.AxisListType

P = 128
D = 1024
KD = D // P
T1 = 512
META = 16
T2 = META + T1
EPS = 1e-6
NEG = -1e30
DH = 64
NH = 8
QT = T1 // P
NPAIR = NH // 2
CB, CS = 32, 16
NC = (T1 - CB) // CS + 1
WINDOW = 128
LH = 4
DK, DV = 256, 512
KE = 2 * D // P
CHUNK = 2048

TB1 = [(0, 0, T1)]
TB2 = [(0, 0, META + 256), (1, META + 256, 256)]
STILES = [(0, META)] + [(META + P * j, P) for j in range(T1 // P)]

N_ADA = 8
N_PROJ, N_CMP, N_ATT, N_WO, N_OUT = 8, 4, 16, 4, 4
N_CIN, N_COUT, N_MLSTM = 32, 8, 40
STAGES = dict(proj=N_PROJ, cmp=N_CMP, att=N_ATT, wo=N_WO, out=N_OUT,
              cin=N_CIN, cout=N_COUT, mlstm=N_MLSTM)
START = {}
for _name, _n in STAGES.items():
    START[_name] = sum(v for k, v in list(STAGES.items())[:len(START)])
N_CHUNKS = sum(STAGES.values())
MG = 32 + LH
SMALL = [("c", KD), ("b_ada", 24), ("g_pre", KD), ("g_post", KD), ("w_gate", 24 * KD), ("w_mgate", MG * KD), ("sinks", NH),
         ("w_k2", 2 * P), ("w_v2", 2 * DH), ("norm_w", 3 * KD), ("conv_w", 3 * KE), ("head_w", KE),
         ("mgate_b", 1), ("pe", 2 * CB)]


class Counter:

    def __init__(self, name, sem, known):
        self.name, self.sem, self.known, self.n = name, sem, known, 0
        self.loop, self.outer, self.loops = None, 0, {}

    def enter(self, loop):
        self.loop, self.outer, self.n = loop, self.n, 0

    def leave(self, trips):
        self.loops[self.loop] = (self.outer, self.n)
        self.n = self.outer + trips * self.n
        self.loop = None


class Engine:

    def __init__(self, eng, counters, known, points):
        self.e, self.counters, self.known, self.points = eng, counters, known, points
        self.own = counters[0]
        self.loop = None
        self.i = 0

    @contextmanager
    def trips(self, name, count):
        for c in self.counters:
            c.enter(name)
        self.loop = name
        with self.e.bass.Fori(0, count, 1, engines=[self.e.engine]) as i:
            self.i = i
            yield i
        for c in self.counters:
            c.leave(count)
        self.loop, self.i = None, 0

    def done(self, ins, point=None, counter=None):
        c = counter or self.own
        ins.then_inc(c.sem, 1)
        c.n += 1
        if point:
            self.points[point] = (c.name, c.loop, c.n)
        return ins

    def value(self, name, loop, local, lag=0):
        if loop is None:
            return local
        first, per, trips = self.known["loops"][name, loop]
        if loop == self.loop:
            assert first + local - lag * per >= 0
            return self.i * per + (first + local - lag * per)
        return first + (trips - 1) * per + local

    def wait(self, point, lag=0):
        if point in self.known["points"]:
            name, loop, local = self.known["points"][point]
            self.e.wait_ge(self.known["sems"][name], self.value(name, loop, local, lag))
        else:
            assert not self.known["points"], point

    def after_own(self):
        if self.known["points"]:
            self.e.wait_ge(self.own.sem, self.value(self.own.name, self.loop, self.own.n))


def build(nc, known, wstream, w_ada, smalls, x_t, meta_t, out_t):
    points, ctx = {}, ExitStack()
    with ctx:
        def sb(name, shape, dt=F32, stack=ctx, side="left"):
            return stack.enter_context(nc.sbuf_tensor(name, [P] + list(shape), dt, side=side))

        def psum(name, shape):
            return ctx.enter_context(nc.psum_tensor(name, [P] + list(shape), F32))

        def sem(name):
            return ctx.enter_context(nc.semaphore(name))

        raw_full = [sem("raw_full0"), sem("raw_full1")]
        s_hi = sem("chunk_hi")
        s_lo = sem("chunk_lo")
        s_small = sem("small_in")
        s_x = sem("x_in")
        s_x2 = sem("x_again")
        s_const = sem("const")
        s_ada = [sem(f"ada{i}") for i in range(N_ADA)]
        s_out = sem("out_stored")
        s_pe, s_chunk, s_act, s_dve = sem("pe"), sem("pe_chunk"), sem("act"), sem("dve")
        known["sems"] = dict(pe=s_pe, chunk=s_chunk, act=s_act, dve=s_dve)

        lin = [psum("lin0", [2, 512]), psum("lin1", [2, 512])]
        aux = [psum(f"aux{i}", [512]) for i in range(4)]

        raw = [sb(f"w_raw{i}", [CHUNK]) for i in range(2)]
        whi = [sb(f"w_hi{i}", [CHUNK], F32R) for i in range(2)]
        wlo = [sb(f"w_lo{i}", [CHUNK], F32R) for i in range(2)]
        xhi = sb("x_hi", [KD, T2], F32R)
        xlo = sb("x_lo", [KD, T2], F32R)
        res = sb("residual", [KD, T2])
        ident = sb("ident", [P])
        ones = sb("ones", [P])
        tmp = sb("tmp", [2, T2])
        sq = sb("squares", [2, T2])
        ssum = sb("square_sum", [T2])
        rstd = sb("rstd", [T2])
        rcol = sb("rstd_columns", [len(STILES)])
        mask = sb("mask", [P])
        eps = sb("eps", [1])
        small_c = sb("small_inputs", [sum(n for _, n in SMALL)])

        def small_of(name):
            start = 0
            for other, n in SMALL:
                if other == name:
                    return small_c[:, start:start + n]
                start += n

        norm_c = small_of("norm_w").rearrange("p (a k) -> p a k", a=3)
        conv_c = small_of("conv_w").rearrange("p (k w) -> p k w", w=3)
        head_c, mb_c, c_in, bada = (small_of(n) for n in ("head_w", "mgate_b", "c", "b_ada"))
        gpre, gpost, sink_c = (small_of(n) for n in ("g_pre", "g_post", "sinks"))
        wg = small_of("w_gate").rearrange("p (k n) -> p k n", k=KD)
        wm = small_of("w_mgate").rearrange("p (k n) -> p k n", k=KD)
        w2k = small_of("w_k2").rearrange("p (k n) -> p k n", k=2)
        w2v = small_of("w_v2").rearrange("p (k n) -> p k n", k=2)
        pe_c = small_of("pe").rearrange("p (s b) -> p s b", s=2)

        one, stage_c, stage_d = ExitStack(), ExitStack(), ExitStack()

        def sb1(name, shape, dt=F32):
            return sb(name, shape, dt, one)

        K_C, V_C, K_S, V_S, K_W, V_W, Q_B, K_B, V_B = 4, 5, 6, 7, 8, 9, 10, 14, 15
        o_tok = sq[:, :, 0:2 * P].rearrange("p a (x d) -> p a x d", x=2)
        dist = sb1("dist", [T1])
        dist_w = sb1("dist_w", [2 * P])
        dist_c = sb1("dist_c", [QT, 32])
        c_hi = sb1("c_hi", [KD, 2], F32R)
        c_lo = sb1("c_lo", [KD, 2], F32R)
        mod = sb1("mod", [24])
        scale_c = sb1("scale_c", [KD])
        gate = sb1("gates", [QT, 24])
        gcur = sb1("gates_pair", [2, QT, 3])
        slopes = sb1("slopes", [NH])
        scur = sb1("slopes_pair", [2])
        sinkcur = sb1("sinks_pair", [2])
        seen = sb1("cmp_seen", [1])
        nmaxs = sb1("neg_max", [2, 4])
        prob_ss = sb1("prob_sum", [2, 4])
        coefs = sb1("coef", [2, 4])
        kct = sb1("kc_T", [2 * NC])
        vct = sb1("vc_tok", [2, DH])
        wg_hi = sb("w_gate_hi", [KD, 24], F32R, stage_c)
        wg_lo = sb("w_gate_lo", [KD, 24], F32R, stage_c)
        cmp_th = sb("cmp_th", [2 * NC], stack=stage_c)
        hid = sb("cmp_hid", [2, 2, 2 * NC], stack=stage_c)
        stage_a = ExitStack()
        ada_w = sb("ada_shift_scale", [N_ADA, CHUNK], stack=stage_a, side="right")
        ada_acc = sb("ada_sums", [N_ADA, 256], stack=stage_a, side="right")
        stage_a.close()
        proj = sb("proj", [16, T1], stack=stage_d, side="right")
        probs = [sb(f"prob{i}", [1316], stack=stage_d, side="right") for i in range(2)]
        probs_T = [sb(f"prob_T{i}", [1408], stack=stage_d, side="right") for i in range(2)]
        cin = sb("cmp_in", [CB // 2, 2, NC], stack=stage_c)
        cin_hi = [sb(f"cmp_in_hi{s}", [CB // 2, 2, NC], F32R, stage_c) for s in range(2)]
        cin_lo = [sb(f"cmp_in_lo{s}", [CB // 2, 2, NC], F32R, stage_c) for s in range(2)]
        stage_c.close()
        zz = sb1("z", [2, NPAIR, T1])
        m_a = sb1("merge_a", [KD, T1])
        m_b = res
        stage_d.close()
        stage_e = ExitStack()
        yhi = sb("y_hi", [KD, T1], F32R, stage_e, "right")
        ylo = sb("y_lo", [KD, T1], F32R, stage_e, "right")
        stage_e.close()
        one.close()

        conv, ml = ExitStack(), ExitStack()
        wm_hi = sb("w_mgate_hi", [KD, MG], F32R)
        wm_lo = sb("w_mgate_lo", [KD, MG], F32R)
        vhi = sb("conv_hi", [KE, T2], F32R, conv)
        vlo = sb("conv_lo", [KE, T2], F32R, conv)
        cb = sb("conv_b", [T2], stack=conv)
        cc = sb("conv_c_gate", [T2], stack=conv)
        cv = sb("conv_in", [2 + T2], stack=conv)
        cy = sb("conv_y", [T2], stack=conv)
        cz = sb("conv_tanh", [T2], stack=conv)
        conv.close()

        def sb2(name, shape, dt=F32):
            return sb(name, shape, dt, ml)

        ghi = sb2("mix_hi", [4, T2], F32R)
        glo = sb2("mix_lo", [4, T2], F32R)
        qk = sb2("qk_T", [4, T2])
        v_T = sb2("v_T", [4, T2])
        v_tok = sb2("v_tok", [len(STILES), DV])
        att = sb2("att_T", [len(STILES), T2])
        oz = sb2("oz", [4, T2])
        neg_m = sb2("neg_m", [T2])
        e_m = sb2("e_m", [T2])
        rden = sb2("rden", [T2])
        ucur = sb2("u_head", [len(STILES)])
        head_row = sb2("head_row", [P])
        hcur = sb2("head_w_cur", [4])
        rows = sb2("gate_rows", [7, T2])
        ml.close()

        loops = {}
        pe_n, ch_n = Counter("pe", s_pe, known), Counter("chunk", s_chunk, known)
        act_n, dve_n = Counter("act", s_act, known), Counter("dve", s_dve, known)
        block = ctx.enter_context(nc.Block())


        @block.sync
        def _(eng):
            eng.dma_start(small_c[:], smalls).then_inc(s_small, 16)
            for c in range(N_ADA):
                eng.dma_start(ada_w[:, c, :], w_ada[c, :, :]).then_inc(s_ada[c], 16)
            for h in range(2):
                eng.dma_start(raw[h][:], wstream[h, :, :]).then_inc(raw_full[h], 16)
            with eng.bass.Fori(0, N_CHUNKS // 2 - 1, 1, engines=[eng.engine]) as i:
                for h in range(2):
                    eng.wait_ge(s_lo, i * 2 + (h + 1))
                    eng.dma_start(raw[h][:], wstream[bass.ds(i * 2 + (h + 2), 1), :, :]
                                  .rearrange("a p n -> (a p) n")).then_inc(raw_full[h], 16)
            eng.wait_ge(s_lo, N_CHUNKS - 1)
            eng.dma_start(raw[0][:], wstream[N_CHUNKS, :, :]).then_inc(raw_full[0], 16)
            eng.wait_ge(s_out, 16 * KD)

        @block.gpsimd
        def _(eng):
            eng.memset(ident[:], 0.0).then_inc(s_const, 1)
            eng.memset(ones[:], 1.0).then_inc(s_const, 1)
            eng.memset(mask[:], 0.0).then_inc(s_const, 1)
            eng.memset(eps[:], EPS).then_inc(s_const, 1)
            for h in range(NH):
                eng.memset(slopes[:, h:h + 1], 2.0 ** -(8.0 * (h + 1) / NH)).then_inc(s_const, 1)
            eng.memset(seen[:], 1.0).then_inc(s_const, 1)
            eng.iota(dist[:], [[1, T1]], base=-(T1 - P), channel_multiplier=-1,
                     allow_small_or_imprecise_dtypes=True).then_inc(s_const, 1)
            eng.iota(dist_c[:], [[-P, QT], [CS, 32]], base=CB - 1, channel_multiplier=-1,
                     allow_small_or_imprecise_dtypes=True).then_inc(s_const, 1)
            eng.wait_ge(s_const, 15)
            eng.affine_select(out=ident[:], in_=ident[:], compare_op=ALU.not_equal, fill=1.0, base=0,
                              pattern=[[-1, P]], channel_multiplier=1).then_inc(s_const, 1)
            eng.affine_select(out=mask[:], in_=mask[:], compare_op=ALU.is_ge, fill=NEG, base=0,
                              pattern=[[1, P]], channel_multiplier=-1).then_inc(s_const, 1)
            eng.affine_select(out=seen[:], in_=seen[:], compare_op=ALU.is_ge, fill=0.0, base=-(CB - 1),
                              pattern=[[0, 1]], channel_multiplier=1).then_inc(s_const, 1)
            eng.affine_select(out=dist[:], in_=dist[:], compare_op=ALU.is_ge, fill=NEG, base=T1 - P,
                              pattern=[[-1, T1]], channel_multiplier=1).then_inc(s_const, 1)
            eng.affine_select(out=dist_c[:], in_=dist_c[:], compare_op=ALU.is_ge, fill=NEG, base=-(CB - 1),
                              pattern=[[P, QT], [-CS, 32]], channel_multiplier=1).then_inc(s_const, 1)
            eng.wait_ge(s_const, 20)
            eng.affine_select(out=dist_w[:], in_=dist[:, T1 - 2 * P:T1], compare_op=ALU.is_gt, fill=NEG,
                              base=0, pattern=[[1, 2 * P]], channel_multiplier=-1).then_inc(s_const, 1)
            with eng.bass.Fori(0, N_CHUNKS // 2, 1, engines=[eng.engine]) as i:
                for h in range(2):
                    eng.wait_ge(s_hi, i * 2 + (h + 1))
                    eng.tensor_tensor(wlo[h][:], raw[h][:], whi[h][:].bitcast(F32), ALU.subtract).then_inc(s_lo, 1)
            eng.wait_ge(s_hi, N_CHUNKS + 1)
            eng.tensor_tensor(wlo[0][:], raw[0][:], whi[0][:].bitcast(F32), ALU.subtract).then_inc(s_lo, 1)


        def chunk_lands_and_splits(a, per, first):
            h = first % 2
            a.e.wait_ge(raw_full[h], a.i * (8 * per) + 16 * (first // 2 + 1) if per else 16 * (first // 2 + 1))
            if per:
                a.e.wait_ge(s_chunk, a.i * per + (N_ADA + first - 1))
            elif first > 1:
                a.e.wait_ge(s_chunk, N_ADA + first - 1)
            a.e.activation(whi[h][:], raw[h][:], ACT.Copy).then_inc(s_hi, 1)

        def all_chunks(a, stage):
            a.e.wait_ge(s_chunk, N_ADA + START[stage] + STAGES[stage])

        def chunk_ready(t, per, first):
            t.e.wait_ge(s_lo, t.i * per + (first + 1) if per else first + 1)

        def group(t, half, col, stride, kts, outs, hi_of, lo_of, point=None, chunk_end=False, ks=None, ready=None):
            ks = range(kts) if ks is None else ks
            n = 3 * ks[0]
            for k in ks:
                if ready:
                    t.wait(f"{ready}{k}")
                c0 = k * stride + col
                for w, x in ((whi, hi_of), (whi, lo_of), (wlo, hi_of)):
                    for o, (_, t0, cnt) in outs:
                        ins = t.e.matmul(o, w[half][:, c0:c0 + P], x(k, t0, cnt), start=(n == 0),
                                         stop=(n == 3 * kts - 1))
                    n += 1
            if n == 3 * kts:
                t.done(ins, point, ch_n if chunk_end else None)

        def lin_outs(slot, tbs):
            return [(lin[slot][:, b, 0:n], (b, t0, n)) for b, t0, n in tbs]

        def x_hi(k, t0, n):
            return xhi[:, k, t0:t0 + n]

        def x_lo(k, t0, n):
            return xlo[:, k, t0:t0 + n]


        def norm_squares_act(a, nm, src, t0, n, tiles, ready=None):
            for k in range(tiles):
                if ready:
                    a.wait(f"{ready}{k}")
                if k >= 2:
                    a.wait(f"{nm}_add{k - 2}")
                a.done(a.e.activation(sq[:, k % 2, 0:n], src(k, t0, n), ACT.Square), f"{nm}_sq{k}")

        def norm_add_dve(v, nm, k, n):
            v.wait(f"{nm}_sq{k}")
            if k == 1:
                v.done(v.e.tensor_tensor(ssum[:, 0:n], sq[:, 0, 0:n], sq[:, 1, 0:n], ALU.add), f"{nm}_add1")
            elif k > 1:
                v.after_own()
                v.done(v.e.tensor_tensor(ssum[:, 0:n], ssum[:, 0:n], sq[:, k % 2, 0:n], ALU.add), f"{nm}_add{k}")
            else:
                points[f"{nm}_add0"] = (v.own.name, v.loop, v.own.n + 1)

        def norm_adds_dve(v, nm, n, tiles):
            for k in range(tiles):
                norm_add_dve(v, nm, k, n)

        def token_tiles(tbs):
            return [(j, s0 - (META if tbs is TB1 else 0), ln) for j, (s0, ln) in enumerate(STILES)
                    if j or tbs is TB2]

        def total_columns(t, src, tbs, bank_of, first=True, last=True):
            for j, t0, ln in token_tiles(tbs):
                ins = t.e.matmul(bank_of(j)[0:ln, j:j + 1], src[:, t0:t0 + ln], ones[:, 0:1], start=first, stop=last)
            return ins

        def norm_total_pe(t, nm, tbs, tiles, bank=2):
            t.wait(f"{nm}_add{tiles - 1}")
            t.done(total_columns(t, ssum, tbs, lambda j: aux[bank]), f"{nm}_tot")

        def column_parts(tbs):
            return [(P, 1, len(STILES))] + ([(META, 0, 1)] if tbs is TB2 else [])

        def norm_root_act(a, nm, tbs, width, bank=2):
            a.wait(f"{nm}_tot")
            for rows_, c0, c1 in column_parts(tbs):
                a.done(a.e.activation(rcol[0:rows_, c0:c1], aux[bank][0:rows_, c0:c1], ACT.Sqrt, bias=eps[0:rows_, :],
                                      scale=1.0 / width), f"{nm}_root")

        sum_banks = aux + [lin[0][:, 1, :]]

        def norm_invert_dve(v, nm, tbs):
            v.wait(f"{nm}_root")
            for rows_, c0, c1 in column_parts(tbs):
                v.done(v.e.reciprocal(rcol[0:rows_, c0:c1], rcol[0:rows_, c0:c1]), f"{nm}_inv")

        def norm_spread_pe(t, nm, tbs, banks=(2, 3)):
            t.wait(f"{nm}_inv")
            for j, t0, ln in token_tiles(tbs):
                b = max(b for b, first, _ in tbs if first <= t0)
                o = t0 - tbs[b][1]
                ins = t.e.matmul(aux[banks[b]][:, o:o + ln], rcol[0:ln, j:j + 1].to_broadcast([ln, P]), ident[0:ln, 0:ln],
                                 start=True, stop=True)
            t.done(ins, f"{nm}_spread")

        def norm_rstd_dve(v, nm, tbs, banks=(2, 3)):
            v.wait(f"{nm}_spread")
            for b, t0, n in tbs:
                v.done(v.e.tensor_copy(rstd[:, t0:t0 + n], aux[banks[b]][:, 0:n]), f"{nm}_rstd")
            v.after_own()

        def norm_apply_dve(v, nm, src, t0, n, weight):
            def low(k):
                v.wait(f"{nm}_hi{k}")
                v.done(v.e.tensor_tensor(xlo[:, k, 0:n], tmp[:, k % 2, 0:n], xhi[:, k, 0:n].bitcast(F32), ALU.subtract),
                       f"{nm}_lo{k}")
            for k in range(KD):
                v.after_own()
                v.done(v.e.scalar_tensor_tensor(tmp[:, k % 2, 0:n], src(k, t0, n), weight(k), rstd[:, 0:n],
                                                ALU.mult, ALU.mult), f"{nm}_n{k}")
                if k >= 1:
                    low(k - 1)
            low(KD - 1)

        def norm_high_act(a, nm, n):
            for k in range(KD):
                a.wait(f"{nm}_n{k}")
                a.done(a.e.activation(xhi[:, k, 0:n], tmp[:, k % 2, 0:n], ACT.Copy), f"{nm}_hi{k}")

        def residual(k, t0, n):
            return res[:, k, t0:t0 + n]

        v_banks = [aux[2], aux[3], lin[0][:, 1, :]]

        def att_banks(e):
            return (aux[0], aux[1], aux[2]) if e == 0 else (aux[3], lin[0][:, 1, :], lin[1][:, 1, :])

        def v_of(tile, j, e):
            return proj[:, tile, P * j + e * DH:P * j + (e + 1) * DH]

        SBLOCKS = [(b, max(STILES[j][0], t0), t0 + n - max(STILES[j][0], t0), j)
                   for b, t0, n in TB2 for j in range(len(STILES)) if STILES[j][0] < t0 + n]

        gbuf = [tmp[:, 1, :], sq[:, 0, :]]
        U_COL = 300

        def h_banks(x):
            return aux[2:4] if x % 2 == 0 else aux[0:2]

        PAIR = [(e * DH, e * DH + DH) for e in range(2)]


        @block.tensor
        def _(eng):
            t = Engine(eng, [pe_n, ch_n], known, points)

            def ada_group(half, col, out, point, chunk_end):
                n = 0
                for k in range(KD):
                    c0 = k * 256 + col
                    for w, x in ((whi, c_hi), (whi, c_lo), (wlo, c_hi)):
                        ins = eng.matmul(out, w[half][:, c0:c0 + P], x[:, k, :], start=(n == 0), stop=(n == 3 * KD - 1))
                        n += 1
                t.done(ins, point, ch_n if chunk_end else None)

            eng.wait_ge(s_const, 21)
            for c in range(N_ADA):
                t.wait(f"ada{c}")
                for j in (2 * c, 2 * c + 1):
                    ins = eng.matmul(aux[0][:, j:j + 1], ada_acc[:, c, P * (j % 2):P * (j % 2) + P], ones[:, 0:1],
                                     start=True, stop=True)
                t.done(ins, None, ch_n)
                if c == N_ADA // 2:
                    norm_total_pe(t, "n0", TB1, KD)
                if c == N_ADA - 2:
                    norm_spread_pe(t, "n0", TB1)

            with t.trips("proj", 2):
                for c in range(4):
                    chunk_ready(t, 4, START["proj"] + c)
                    for g in range(2):
                        j = 2 * c + g
                        t.wait(f"proj_ev{(j - 2) % 8}", 0 if j >= 2 else 1)
                        group(t, c % 2, g * P, 256, KD, lin_outs(g, TB1), x_hi, x_lo, f"proj_g{j}", g == 1,
                              ready="n0b_lo" if j == 0 else None)
            t.wait("wg_split")
            for i in range(QT):
                n = 0
                for k in range(KD):
                    for x, w in ((xhi, wg_hi), (xlo, wg_hi), (xhi, wg_lo)):
                        ins = eng.matmul(aux[1][:, 24 * i:24 * i + 24], x[:, k, P * i:P * i + P], w[:, k, :],
                                         start=(n == 0), stop=(n == 3 * KD - 1))
                        n += 1
            t.done(ins, "gates")

            t.wait("proj_ev7")
            t.wait("n0_root")
            for s, tile in enumerate((V_S, V_W, V_B)):
                for i in range(QT):
                    ins = eng.transpose(v_banks[s][:, P * i:P * i + P], proj[:, tile, P * i:P * i + P], ident[:])
                t.done(ins, f"vt{s}")

            for src in range(2):
                t.wait(f"cin_lo{src}")
                if src == 1:
                    t.wait("vtok2")
                for j in range(2):
                    c = 2 * src + j
                    chunk_ready(t, 0, START["cmp"] + c)
                    n = 0
                    for k in range(16):
                        for w, x in ((whi, cin_hi[src]), (whi, cin_lo[src]), (wlo, cin_hi[src])):
                            ins = eng.matmul(lin[j][:, src, 0:2 * NC], w[c % 2][:, k * P:k * P + P],
                                             x[:, k, :, :].rearrange("p g j -> p (g j)"), start=(n == 0), stop=(n == 47))
                            n += 1
                    t.done(ins, None, ch_n)
            t.wait("gate_th")
            t.wait("hid0")
            for j in range(2):
                ins = eng.matmul(aux[0][:, 0:2 * NC], w2k[:, j, :], hid[:, 0, j, :], start=(j == 0), stop=(j == 1))
            t.done(ins, "kc")
            t.wait("hid1")
            for g in range(2):
                for j in range(2):
                    ins = eng.matmul(aux[1][0:NC, 128 + g * DH:128 + (g + 1) * DH], hid[:, 1, j, g * NC:(g + 1) * NC],
                                     w2v[:, j, :], start=(j == 0), stop=(j == 1))
            t.done(ins, "vc")

            t.wait("kvc_ready")
            t.wait("vtok2")
            with t.trips("att", NPAIR):
                def scores(s):
                    i, e = divmod(s, 2)
                    lo, hi = PAIR[e]
                    b = att_banks(e)
                    keys, k0 = P * (i + 1), max(0, P * (i - 1))
                    if s >= 2:
                        t.wait(f"out{s - 2}")
                    if e == 0 and i >= 2:
                        t.wait(f"o_T_ev{i - 2}")
                    qa = proj[lo:hi, K_C, P * i:P * i + P]
                    qb = proj[lo:hi, V_C, P * i:P * i + P]
                    eng.matmul(b[0][:, 0:keys], qa, proj[lo:hi, K_S, 0:keys], start=True, stop=True)
                    eng.matmul(b[1][:, 0:keys], qa, proj[lo:hi, K_W, 0:keys], start=True, stop=True)
                    eng.matmul(b[2][:, 0:NC], qa, kct[lo:hi, e * NC:(e + 1) * NC], start=True, stop=True)
                    w0 = 32 + (P if i == 0 else 0)
                    t.done(eng.matmul(b[2][:, w0:w0 + keys - k0], qb, proj[lo:hi, K_B, k0:keys], start=True, stop=True),
                           f"s{s}")

                def turn_outputs(i):
                    t.wait(f"out{2 * i + 1}")
                    for x in range(2):
                        ins = eng.transpose(aux[1][:, P * x:P * x + P], o_tok[:, i % 2, x, :], ident[:])
                    t.done(ins, f"o_T{i}")

                t.wait("staged")
                scores(0)
                for s in range(2 * QT):
                    i, e = divmod(s, 2)
                    b = att_banks(e)
                    prob, prob_T = probs[e], probs_T[e]
                    c, g = divmod(s, 2)
                    if g == 0:
                        chunk_ready(t, 4, START["att"] + c)
                    if s >= 2:
                        t.wait(f"att_ev{s - 2}")
                    if c < 3:
                        group(t, c % 2, g * P, 256, KD, lin_outs(g, TB1), x_hi, x_lo, ks=range(KD // 2))
                    else:
                        ada_group(c % 2, g * P, lin[g][:, 0, 0:2], f"att_g{s}", g == 1)
                    t.wait(f"exp{s}")
                    for j in range(i + 1):
                        eng.transpose(b[0][:, P * j:P * j + P], prob[:, P * j:P * j + P], ident[:])
                    for j in range(i + 1):
                        eng.transpose(b[1][:, P * j:P * j + P], prob[:, 512 + P * j:512 + P * j + P], ident[:])
                    eng.transpose(b[2][0:NC, 0:P], prob[:, 1024:1024 + NC], ident[:])
                    js = (1,) if i == 0 else (0, 1)
                    for j in js:
                        ins = eng.transpose(b[2][:, P + P * j:2 * P + P * j],
                                            prob[:, 1056 + P * j:1056 + P * j + P], ident[:])
                    t.done(ins, f"pt{s}")
                    if s + 1 < 2 * QT:
                        scores(s + 1)
                    if c < 3:
                        group(t, c % 2, g * P, 256, KD, lin_outs(g, TB1), x_hi, x_lo, f"att_g{s}", g == 1,
                              ks=range(KD // 2, KD))
                    t.wait(f"pt_ev{s}_act")
                    t.wait(f"pt_ev{s}_dve")
                    o = b[0]
                    eng.matmul(o[:, 0:DH], prob_T[0:NC, 1024:1152], vct[0:NC, e, :], start=True, stop=True)
                    for x, tile in ((0, V_S), (1, V_W)):
                        for j in range(i + 1):
                            eng.matmul(o[:, DH * (x + 1):DH * (x + 2)], prob_T[:, 512 * x + P * j:512 * x + P * j + P],
                                       v_of(tile, j, e), start=(j == 0), stop=(j == i))
                    for j in js:
                        ins = eng.matmul(o[:, 3 * DH:4 * DH], prob_T[:, 1152 + P * j:1152 + P * j + P],
                                         v_of(V_B, i - 1 + j, e), start=(j == js[0]), stop=(j == 1))
                    t.done(ins, f"pv{s}")
                    if e == 0 and i:
                        turn_outputs(i - 1)
                turn_outputs(QT - 1)
                t.wait(f"o_T_ev{QT - 1}")

            t.wait(f"og_lo{KD - 1}")
            t.wait("att_ev6")
            t.wait("att_ev7")
            for c in range(N_WO):
                chunk_ready(t, 0, START["wo"] + c)
                for m in range(2):
                    for x in range(2):
                        j = 4 * c + 2 * m + x
                        if j >= 2:
                            t.wait(f"wo_ev{j - 2}")
                        group(t, c % 2, x * 1024 + m * P, 256, 4, lin_outs(x, TB1),
                              lambda k, t0, n, x=x: x_hi(4 * x + k, t0, n), lambda k, t0, n, x=x: x_lo(4 * x + k, t0, n),
                              f"wo_g{j}", m == 1 and x == 1)
            t.wait(f"y_lo{KD - 1}")
            t.wait("wo_ev14")
            for c in range(N_OUT):
                chunk_ready(t, 0, START["out"] + c)
                for g in range(2):
                    j = 2 * c + g
                    if j >= 2:
                        t.wait(f"out_ev{j - 2}")
                    else:
                        t.wait(f"wo_ev{14 + j}")
                    group(t, c % 2, g * P, 256, KD, lin_outs(g, TB1), lambda k, t0, n: yhi[:, k, t0:t0 + n],
                          lambda k, t0, n: ylo[:, k, t0:t0 + n], f"out_g{j}", g == 1)
            norm_total_pe(t, "n1", TB1, KD)
            norm_spread_pe(t, "n1", TB1)

            for k in range(KD):
                t.wait(f"n2_sq{k}")
                t.done(total_columns(t, sq[:, k % 2, :], TB2, lambda j: sum_banks[j], k == 0, k == KD - 1),
                       f"n2_part{k}" if k < KD - 1 else "n2_tot")
            norm_spread_pe(t, "n2", TB2)

            t.wait(f"u_lo{KD - 1}")
            with t.trips("cin", 8):
                for c in range(4):
                    chunk_ready(t, 4, START["cin"] + c)
                    for g in range(2):
                        j = 2 * c + g
                        t.wait(f"cin_ev{(j - 2) % 8}", 0 if j >= 2 else 1)
                        group(t, c % 2, g * P, 256, KD, lin_outs(g, TB2), x_hi, x_lo, f"cin_g{j}", g == 1)
            t.wait("conv_lo1")
            t.wait("cin_ev6")
            t.wait("cin_ev7")
            with t.trips("cout", 2):
                for c in range(4):
                    chunk_ready(t, 4, START["cout"] + c)
                    t.wait(f"cout_ev{(c - 2) % 4}", 0 if c >= 2 else 1)
                    group(t, c % 2, 0, P, KE, lin_outs(c % 2, TB2), lambda k, t0, n: vhi[:, k, t0:t0 + n],
                          lambda k, t0, n: vlo[:, k, t0:t0 + n], None, True)
            norm_total_pe(t, "n3", TB2, 4)
            norm_spread_pe(t, "n3", TB2)

            t.wait("wm_split")
            m = 0
            for k in range(KD):
                t.wait(f"n3b_lo{k}")
                for w, x in ((wm_hi, xhi), (wm_hi, xlo), (wm_lo, xhi)):
                    for b, t0, n in TB2:
                        ins = eng.matmul(aux[b][0:MG, 0:n], w[:, k, :], x[:, k, t0:t0 + n], start=(m == 0), stop=(m == 3 * KD - 1))
                    m += 1
            t.done(ins, "mgates")
            with t.trips("mlstm", LH):
                def projections(chunks, after_first=None):
                    for c in chunks:
                        chunk_ready(t, 10, START["mlstm"] + c)
                        for g in range(2):
                            j = 2 * c + g
                            t.wait(f"ml_ev{j - 2}" if j >= 2 else f"mlo_ev{6 + j}", 0 if j >= 2 else 1)
                            group(t, c % 2, g * P, 256, KD, lin_outs(g, TB2), x_hi, x_lo, f"ml_g{j}", g == 1)
                            if g == 0 and after_first:
                                after_first()
                projections(range(1))
                t.wait("rows_done")
                t.wait("head_row")
                t.wait("hn_rstd", 1)
                for x in range(2):
                    for b, t0, n in TB2:
                        eng.matmul(aux[2 * x + b][:, 0:n], head_row[0:LH, :], rows[0:LH, 5 + x, t0:t0 + n],
                                   start=True, stop=True)
                for j, (s0, ln) in enumerate(STILES):
                    ins = eng.matmul(aux[3][0:ln, U_COL + j:U_COL + j + 1], rows[0:LH, 4, s0:s0 + ln],
                                     head_row[0:LH, 0:1], start=True, stop=True)
                t.done(ins, "bc")
                projections(range(1, 3))
                t.wait("ml_ev3")
                t.wait("bc_ev_act")
                t.wait("bc_ev_dve")
                for q, (b, t0, n, j) in enumerate(SBLOCKS):
                    s0, ln = STILES[j]
                    if q >= 4:
                        t.wait(f"st_ev{q - 4}")
                    for k in range(2):
                        ins = eng.matmul(aux[q % 4][0:ln, 0:n], qk[:, 2 + k, s0:s0 + ln], qk[:, k, t0:t0 + n],
                                         start=(k == 0), stop=(k == 1))
                    t.done(ins, f"st{q}")
                projections(range(3, 5))
                t.wait("ml_ev7")
                for j, (s0, ln) in enumerate(STILES):
                    t.wait(f"vtk{j - 4}" if j >= 4 else f"st_ev{len(SBLOCKS) - 1}")
                    for vt in range(4):
                        ins = eng.transpose(aux[j % 4][0:ln, P * vt:P * vt + P], v_T[:, vt, s0:s0 + ln], ident[:])
                    t.done(ins, f"vtr{j}")
                projections(range(5, 6))
                t.wait(f"vtk{len(STILES) - 1}")
                for x in range(5):
                    for b, t0, n in TB2:
                        q = 2 * x + b
                        if x >= 2:
                            t.wait(f"h_ev{q - 4}")
                        js = [j for j, (s0, _) in enumerate(STILES) if s0 < t0 + n]
                        for j in js:
                            s0, ln = STILES[j]
                            f = max(s0, t0)
                            w = ones[0:ln, :] if x == 0 else v_tok[0:ln, j, P * (x - 1):P * x]
                            ins = eng.matmul(h_banks(x)[b][:, f - t0:n], w, att[0:ln, j, f:t0 + n],
                                             start=(j == 0), stop=(j == js[-1]))
                        t.done(ins, f"h{q}")
                projections(range(6, 7), after_first=lambda: norm_total_pe(t, "hn", TB2, 4))
                norm_spread_pe(t, "hn", TB2)
                projections(range(7, 8))
                def out_tile(j, **more):
                    group(t, (j // 4) % 2, (j % 4) * P, 512, 4, lin_outs(j % 2, TB2), lambda k, t0, n: ghi[:, k, t0:t0 + n],
                          lambda k, t0, n: glo[:, k, t0:t0 + n], f"mlo_g{j}", j % 4 == 3, **more)
                chunk_ready(t, 10, START["mlstm"] + 8)
                for j in range(2):
                    t.wait(f"ml_ev{14 + j}")
                    out_tile(j, ks=range(3), ready="g_lo")
                for j in range(2):
                    out_tile(j, ks=range(3, 4), ready="g_lo")
                for j in range(2, KD):
                    if j == 4:
                        chunk_ready(t, 10, START["mlstm"] + 9)
                    t.wait(f"mlo_ev{j - 2}")
                    out_tile(j)
            norm_total_pe(t, "n4", TB1, KD)
            norm_spread_pe(t, "n4", TB1)
            loops.update({(c.name, k): v for c in (pe_n, ch_n) for k, v in c.loops.items()})


        @block.scalar
        def _(eng):
            a = Engine(eng, [act_n], known, points)
            act = eng.activation

            eng.dma_start(res[:, :, META:T2], x_t).then_inc(s_x, 16)
            eng.dma_start(res[:, :, 0:META], meta_t).then_inc(s_x, 16)
            eng.wait_ge(s_x, 32)
            norm_squares_act(a, "n0", residual, META, T1, KD)
            chunk_lands_and_splits(a, 0, 0)
            eng.wait_ge(s_const, 21)
            norm_root_act(a, "n0", TB1, D)
            for k in range(KD):
                a.wait(f"n0b_n{k}")
                a.done(act(xhi[:, k, 0:T1], tmp[:, k % 2, 0:T1], ACT.Identity, bias=mod[:, k:k + 1]), f"n0b_hi{k}")

            with a.trips("proj", 2):
                for c in range(4):
                    chunk_lands_and_splits(a, 4, START["proj"] + c + 1)
            a.wait("gates")
            a.done(act(gate[:].rearrange("p i b -> p (i b)"), aux[1][:, 0:24 * QT], ACT.Tanh, scale=0.5), "gate_th")
            for src in range(2):
                a.wait(f"cin_sum{src}")
                a.done(act(cin_hi[src][:], cin[:], ACT.Copy), f"cin_hi{src}")
            for src in range(2):
                for j in range(2):
                    c = 2 * src + j
                    chunk_lands_and_splits(a, 0, START["cmp"] + c + 1)
                    eng.wait_ge(s_chunk, N_ADA + START["cmp"] + c + 1)
                    if c:
                        a.wait(f"hid_use{c - 1}")
                    a.done(act(cmp_th[:], lin[j][:, src, 0:2 * NC], ACT.Tanh, scale=0.5), f"cmp_th{c}")

            with a.trips("att", NPAIR):
                def exps(s):
                    i, e = divmod(s, 2)
                    keys, w0 = P * (i + 1), 1056 + (P if i == 0 else 0)
                    a.wait(f"max{s}")
                    spans = [(1024, 1024 + NC), (0, keys), (512, 512 + keys), (w0, 1313)]
                    for x, (p0, p1) in enumerate(spans):
                        a.done(act(probs[e][:, p0:p1], probs[e][:, p0:p1], ACT.Exp, bias=nmaxs[:, e, x:x + 1],
                                   accum_out=prob_ss[:, e, x:x + 1]), f"exp{s}")

                for s in range(2 * QT):
                    i, e = divmod(s, 2)
                    c, g = divmod(s, 2)
                    if g == 0:
                        chunk_lands_and_splits(a, 4, START["att"] + c + 1)
                    if s == 0:
                        exps(0)
                    a.wait(f"pt{s}")
                    keys = P * (i + 1)
                    a.done(act(probs_T[e][:, 0:keys], att_banks(e)[0][:, 0:keys], ACT.Copy), f"pt_ev{s}_act")
                    if s + 1 < 2 * QT:
                        exps(s + 1)
                    if c in (0, 1, 2):
                        if g == 1:
                            eng.wait_ge(s_chunk, a.i * 4 + (N_ADA + START["att"] + c + 1))
                        else:
                            a.wait(f"att_g{s}")
                        src = lin[g][:, 0, 0:T1]
                        if c == 0:
                            a.done(act(tmp[:, g, 0:T1], src, ACT.Tanh, scale=0.5), f"z_th{g}")
                        else:
                            dst = m_a[:, bass.ds(a.i * 2 + g, 1), :] if c == 1 else \
                                m_b[:, bass.ds(a.i * 2 + g, 1), META:T2]
                            a.done(act(dst.rearrange("p a n -> p (a n)"), src, ACT.Tanh, scale=0.5), f"att_ev{s}")

            for k in range(KD):
                a.wait(f"og{k}")
                a.done(act(xhi[:, k, 0:T1], tmp[:, k % 2, 0:T1], ACT.Copy), f"og_hi{k}")
            for c in range(N_WO):
                chunk_lands_and_splits(a, 0, START["wo"] + c + 1)
                for m in range(2):
                    k = 2 * c + m
                    a.wait(f"y{k}")
                    a.done(act(yhi[:, k, :], tmp[:, 1, 0:T1], ACT.Copy), f"y_hi{k}")
            eng.dma_start(res[:, :, META:T2], x_t).then_inc(s_x2, 16)
            for c in range(N_OUT):
                chunk_lands_and_splits(a, 0, START["out"] + c + 1)
                for g in range(2):
                    j = 2 * c + g
                    if g == 0:
                        a.wait(f"out_g{j}")
                    else:
                        eng.wait_ge(s_chunk, N_ADA + START["out"] + c + 1)
                    if j >= 2:
                        a.wait(f"n1_add{j - 2}")
                    a.done(act(sq[:, g, 0:T1], lin[g][:, 0, 0:T1], ACT.Square, scale=0.5), f"n1_sq{j}")
                    a.done(act(m_a[:, j, :], lin[g][:, 0, 0:T1], ACT.Copy, scale=0.5), f"out_ev{j}")
            norm_root_act(a, "n1", TB1, D)
            for k in range(KD):
                a.wait(f"x1_{k}")
                a.done(act(xhi[:, k, :], res[:, k, :], ACT.Copy, scale=norm_c[:, 0, k:k + 1]), f"u_hi{k}")
                if k >= 2:
                    a.wait(f"n2_part{k - 2}")
                a.done(act(sq[:, k % 2, :], res[:, k, :], ACT.Square), f"n2_sq{k}")
            a.wait("n2_tot")
            for j, (_, ln) in enumerate(STILES):
                a.done(act(rcol[0:ln, j:j + 1], sum_banks[j][0:ln, j:j + 1], ACT.Sqrt, bias=eps[0:ln, :], scale=1.0 / D),
                       "n2_root")

            def slot_full(stage, per, c, g, point):
                if g == 1:
                    eng.wait_ge(s_chunk, a.i * per + (N_ADA + START[stage] + c + 1))
                else:
                    a.wait(point)

            with a.trips("cin", 8):
                for c in range(4):
                    u = c // 2
                    chunk_lands_and_splits(a, 4, START["cin"] + c + 1)
                    if c % 2 == 0:
                        for g, dst in ((0, cb), (1, cc)):
                            slot_full("cin", 4, c, g, f"cin_g{2 * c}")
                            a.wait(f"conv_lo{1 - u}", 0 if u else 1)
                            for b, t0, n in TB2:
                                a.done(act(dst[:, t0:t0 + n], lin[g][:, b, 0:n], ACT.Copy), f"cin_ev{2 * c + g}")
                    else:
                        a.wait(f"cin_ev{4 * u + 3}")
                        a.done(act(sq[:, 0, :], cz[:], ACT.Tanh, scale=0.5), f"conv_th{u}")
                        a.wait(f"conv{u}")
                        a.done(act(vhi[:, bass.ds(a.i * 2 + u, 1), :].rearrange("p a n -> p (a n)"), tmp[:, u, :], ACT.Copy),
                               f"conv_hi{u}")
            with a.trips("cout", 2):
                for c in range(4):
                    chunk_lands_and_splits(a, 4, START["cout"] + c + 1)
                    a.wait(f"cout_ev{c}")
                    a.wait(f"n3_add{(c - 2) % 4}", 0 if c >= 2 else 1)
                    a.done(act(sq[:, c % 2, :], res[:, bass.ds(a.i * 4 + c, 1), :].rearrange("p a n -> p (a n)"), ACT.Square),
                           f"n3_sq{c}")
            norm_root_act(a, "n3", TB2, D)
            norm_high_act(a, "n3b", T2)

            a.wait("rows_f")
            a.done(act(rows[0:LH, 2, :], rows[0:LH, 1, :], ACT.Abs))
            a.after_own()
            a.done(act(rows[0:LH, 2, :], rows[0:LH, 2, :], ACT.Exp, scale=-1.0))
            a.after_own()
            a.done(act(rows[0:LH, 2, :], rows[0:LH, 2, :], ACT.Ln, bias=1.0), "rows_ln")

            with a.trips("mlstm", LH):
                def evacs(c):
                    for g in range(2):
                        j = 2 * c + g
                        slot_full("mlstm", 10, c, g, f"ml_g{j}")
                        dst = qk[:, j, :] if j < 4 else v_T[:, j - 4, :] if j < 8 else oz[:, j - 8, :]
                        fn = ACT.Tanh if j >= 8 else ACT.Copy
                        for b, t0, n in TB2:
                            a.done(act(dst[:, t0:t0 + n], lin[g][:, b, 0:n], fn, scale=0.5 if j >= 8 else 1.0),
                                   f"ml_ev{j}")

                def gate_tanh(k):
                    slot_full("mlstm", 10, 6 + k // 2, k % 2, f"ml_g{12 + k}")
                    a.wait(f"ml_ev{11 + k}" if k else "g_lo3", 0 if k else 1)
                    for b, t0, n in TB2:
                        a.done(act(tmp[:, 0, t0:t0 + n], lin[k % 2][:, b, 0:n], ACT.Tanh, scale=0.5), f"z_ml{k}")

                for c in range(8):
                    chunk_lands_and_splits(a, 10, START["mlstm"] + c + 1)
                    if c == 2:
                        a.wait("g_lo3", 1)
                    if c < 6:
                        evacs(c)
                    if c == 0:
                        a.wait("bc")
                        for b, t0, n in TB2:
                            if b == 1:
                                a.wait("bc_ev_dve")
                            a.done(act(e_m[:, t0:t0 + n], aux[2 + b][:, 0:n], ACT.Exp, scale=-1.0), "bc_ev_act")
                    if c == 1:
                        a.wait("masked")
                        for j, (s0, ln) in enumerate(STILES):
                            if s0 + ln < T2:
                                a.done(act(att[0:ln, j, s0 + ln:T2], neg_m[0:ln, s0 + ln:T2], ACT.Exp,
                                           bias=ucur[0:ln, j:j + 1]))
                            a.done(act(att[0:ln, j, s0:s0 + ln], att[0:ln, j, s0:s0 + ln], ACT.Exp,
                                       bias=ucur[0:ln, j:j + 1]), f"decay{j}")
                    if c == 5:
                        for b, t0, n in TB2:
                            a.wait(f"h{b}")
                            a.done(act(rden[:, t0:t0 + n], h_banks(0)[b][:, 0:n], ACT.Abs), f"h_ev{b}")
                    if c == 6:
                        norm_squares_act(a, "hn", lambda k, t0, n: v_T[:, k, t0:t0 + n], 0, T2, 4, "h_done")
                        gate_tanh(0)
                        norm_root_act(a, "hn", TB2, DV)
                        gate_tanh(1)
                    if c == 7:
                        for k in range(4):
                            if k == 2:
                                gate_tanh(2)
                            if k == 3:
                                gate_tanh(3)
                            a.wait(f"g{k}")
                            a.done(act(ghi[:, k, :], gbuf[k % 2], ACT.Copy), f"g_hi{k}")
                chunk_lands_and_splits(a, 10, START["mlstm"] + 9)
                for k in range(KD):
                    if k == 4:
                        chunk_lands_and_splits(a, 10, START["mlstm"] + 10)
                    a.wait(f"mlo_ev{k}")
                    if k >= 2:
                        a.wait(f"n4_add{k - 2}")
                    a.done(act(sq[:, k % 2, 0:T1], res[:, k, META:T2], ACT.Square), f"n4_sq{k}")
            norm_root_act(a, "n4", TB1, D)
            for k in range(KD):
                a.wait(f"out_t{k}")
                eng.dma_start(out_t[P * k:P * k + P, :], res[:, k, META:T2]).then_inc(s_out, 16)
            loops.update({("act", k): v for k, v in act_n.loops.items()})



        @block.vector
        def _(eng):
            v = Engine(eng, [dve_n], known, points)
            tt, ts, stt, copy = eng.tensor_tensor, eng.tensor_scalar, eng.scalar_tensor_tensor, eng.tensor_copy

            def move(out, src):
                return ts(out, src, 1.0, None, ALU.mult)

            def flat(ap):
                return ap.rearrange("p a n -> p (a n)")

            eng.wait_ge(s_small, 16)
            for j in range(2):
                v.done(copy(c_hi[:, :, j], c_in[:]))
            v.done(copy(wg_hi[:], wg[:]))
            v.after_own()
            for j in range(2):
                v.done(tt(c_lo[:, :, j], c_in[:], c_hi[:, :, j].bitcast(F32), ALU.subtract), "c_split")
            v.done(tt(wg_lo[:], wg[:], wg_hi[:].bitcast(F32), ALU.subtract), "wg_split")

            for c in range(N_ADA):
                eng.wait_ge(s_ada[c], 16)
                for k in range(KD):
                    w = ada_w[:, c, 256 * k:256 * k + 256]
                    if k == 0:
                        v.done(ts(ada_acc[:, c, :], w, c_in[:, 0:1], None, ALU.mult))
                    else:
                        v.after_own()
                        v.done(stt(ada_acc[:, c, :], w, c_in[:, k:k + 1], ada_acc[:, c, :], ALU.mult, ALU.add), f"ada{c}")
                if c == N_ADA // 2 - 1:
                    norm_adds_dve(v, "n0", T1, KD)
                if c == N_ADA - 3:
                    norm_invert_dve(v, "n0", TB1)
            norm_rstd_dve(v, "n0", TB1)
            eng.wait_ge(s_chunk, N_ADA)
            v.done(tt(mod[:, 0:16], aux[0][:, 0:16], bada[:, 0:16], ALU.add))
            v.after_own()
            v.done(stt(scale_c[:], mod[:, 8:16], 1.0, gpre[:], ALU.add, ALU.mult))

            def low(k):
                v.wait(f"n0b_hi{k}")
                v.done(stt(xlo[:, k, 0:T1], tmp[:, k % 2, 0:T1], mod[:, k:k + 1], xhi[:, k, 0:T1].bitcast(F32),
                           ALU.add, ALU.subtract), f"n0b_lo{k}")
            for k in range(KD):
                v.after_own()
                v.done(stt(tmp[:, k % 2, 0:T1], res[:, k, META:T2], scale_c[:, k:k + 1], rstd[:, 0:T1],
                           ALU.mult, ALU.mult), f"n0b_n{k}")
                if k:
                    low(k - 1)
            low(KD - 1)

            def tile_full(stage, per, c, last, point):
                if last:
                    eng.wait_ge(s_chunk, v.i * per + (N_ADA + START[stage] + c + 1) if per
                                else N_ADA + START[stage] + c + 1)
                else:
                    v.wait(point)

            with v.trips("proj", 2):
                for c in range(4):
                    for g in range(2):
                        j = 2 * c + g
                        tile_full("proj", 4, c, g == 1, f"proj_g{j}")
                        v.done(move(flat(proj[:, bass.ds(v.i * 8 + j, 1), :]), lin[g][:, 0, :]), f"proj_ev{j}")
            v.after_own()

            for src in range(2):
                if src:
                    v.wait(f"cin_hi{src - 1}")
                    v.after_own()
                for g in range(2):
                    gs = slice(g * DH, (g + 1) * DH)
                    rows_of = proj[gs, K_C + src, :].rearrange("p (j a r) -> p r a j", a=8, r=2)
                    emb = pe_c[gs, src, :].rearrange("p (a r) -> p r a", r=2)
                    for r in range(2):
                        for a1 in range(2):
                            v.done(tt(cin[r * DH:(r + 1) * DH, 8 * a1:8 * a1 + 8, g, :], rows_of[:, r, :, a1:a1 + NC],
                                      emb[:, r, 8 * a1:8 * a1 + 8].unsqueeze(2).to_broadcast([DH, 8, NC]), ALU.add),
                                   f"cin_sum{src}")
                v.wait(f"cin_hi{src}")
                v.done(tt(cin_lo[src][:], cin[:], cin_hi[src][:].bitcast(F32), ALU.subtract), f"cin_lo{src}")
            for s, tile in enumerate((V_S, V_W, V_B)):
                v.wait(f"vt{s}")
                v.done(copy(proj[:, tile, :], v_banks[s][:, 0:T1]), f"vtok{s}")
            v.wait("gate_th")
            v.done(ts(gate[:], gate[:], 0.5, 0.5, ALU.mult, ALU.add))
            v.after_own()
            eng.wait_ge(s_const, 21)
            v.done(ts(gate[:, 0, 0:NH], gate[:, 0, 0:NH], seen[:], None, ALU.mult))
            for src in range(2):
                for j in range(2):
                    c = 2 * src + j
                    v.wait(f"cmp_th{c}")
                    v.done(stt(hid[:, src, j, :], cmp_th[:], 1.0, lin[j][:, src, 0:2 * NC], ALU.add, ALU.mult),
                           f"hid_use{c}")
                points[f"hid{src}"] = ("dve", None, v.own.n)
            v.wait("kc")
            v.done(ts(kct[:], aux[0][:, 0:2 * NC], 0.5, None, ALU.mult))
            v.wait("vc")
            v.done(ts(vct[0:NC, :, :].rearrange("p g d -> p (g d)"), aux[1][0:NC, 128:256], 0.5, None, ALU.mult),
                   "kvc_ready")

            with v.trips("att", NPAIR):
                v.done(ts(proj[:, K_C, :], flat(proj[:, bass.ds(v.i, 1), :]), DH ** -0.5, None, ALU.mult))
                v.done(ts(proj[:, V_C, :], flat(proj[:, bass.ds(v.i + Q_B, 1), :]), DH ** -0.5, None, ALU.mult))
                for e in range(2):
                    v.done(move(scur[:, e:e + 1], slopes[:, bass.ds(v.i + 4 * e, 1)]))
                    v.done(move(sinkcur[:, e:e + 1], sink_c[:, bass.ds(v.i + 4 * e, 1)]))
                    for br in range(3):
                        v.done(move(gcur[:, e, :, br:br + 1], gate[:, :, bass.ds(v.i + (4 * e + NH * br), 1)]), "staged")
                v.after_own()
                def maxima(s):
                    i, e = divmod(s, 2)
                    b, prob = att_banks(e), probs[e]
                    keys, k0, w0 = P * (i + 1), max(0, P * (i - 1)), (P if i == 0 else 0)
                    v.wait(f"s{s}")
                    v.after_own()
                    sl = scur[:, e:e + 1]
                    v.done(stt(prob[:, 1024:1024 + NC], dist_c[:, i, 0:NC], sl, b[2][:, 0:NC], ALU.mult, ALU.add))
                    v.done(stt(prob[:, 0:keys], dist[:, T1 - keys:T1], sl, b[0][:, 0:keys], ALU.mult, ALU.add))
                    v.done(stt(prob[:, 512:512 + keys], dist[:, T1 - keys:T1], sl, b[1][:, 0:keys], ALU.mult, ALU.add))
                    v.done(stt(prob[:, 1056 + w0:1312], dist_w[:, w0:2 * P], sl, b[2][:, 32 + w0:32 + w0 + keys - k0],
                               ALU.mult, ALU.add))
                    v.done(copy(prob[:, 1312:1313], sinkcur[:, e:e + 1]))
                    v.after_own()
                    spans = [(1024, 1024 + NC), (0, keys), (512, 512 + keys), (1056 + w0, 1313)]
                    for x, (p0, p1) in enumerate(spans):
                        v.done(eng.tensor_reduce(nmaxs[:, e, x:x + 1], prob[:, p0:p1], AX.X, ALU.max, negate=True),
                               f"max{s}")

                def outputs_turned(i):
                    v.wait(f"o_T{i}")
                    for x in range(2):
                        v.done(move(flat(proj[:, bass.ds(v.i + Q_B * x, 1), P * i:P * i + P]),
                                    aux[1][:, P * x:P * x + P]), f"o_T_ev{i}")

                maxima(0)
                for s in range(2 * QT):
                    i, e = divmod(s, 2)
                    b, prob_T, coef = att_banks(e), probs_T[e], coefs[:, e, :]
                    keys, w0 = P * (i + 1), (P if i == 0 else 0)
                    v.wait(f"pt{s}")
                    v.done(copy(prob_T[0:NC, 1024:1152], b[2][0:NC, 0:P]))
                    v.done(copy(prob_T[:, 1152 + w0:1408], b[2][:, P + w0:3 * P]))
                    v.done(copy(prob_T[:, 512:512 + keys], b[1][:, 0:keys]), f"pt_ev{s}_dve")
                    v.wait(f"exp{s}")
                    v.done(eng.reciprocal(coef, prob_ss[:, e, :]))
                    v.after_own()
                    v.done(tt(coef[:, 0:3], coef[:, 0:3], gcur[:, e, i, :], ALU.mult))
                    if s + 1 < 2 * QT:
                        maxima(s + 1)
                    v.wait(f"pv{s}")
                    v.after_own()
                    o, es = b[0], slice(e * DH, (e + 1) * DH)
                    o_a, o_b = o_tok[:, i % 2, 0, es], o_tok[:, i % 2, 1, es]
                    v.done(ts(o_a, o[:, 0:DH], coef[:, 0:1], None, ALU.mult))
                    v.done(ts(o_b, o[:, 3 * DH:4 * DH], coef[:, 3:4], None, ALU.mult))
                    for x in (1, 2):
                        v.after_own()
                        v.done(stt(o_a, o[:, x * DH:(x + 1) * DH], coef[:, x:x + 1], o_a, ALU.mult, ALU.add), f"out{s}")
                    c, g = divmod(s, 2)
                    if c == 0:
                        v.wait(f"z_th{g}")
                        v.done(stt(flat(zz[:, g, bass.ds(v.i, 1), :]), tmp[:, g, 0:T1], 1.0, lin[g][:, 0, :],
                                   ALU.add, ALU.mult), f"att_ev{s}")
                    if c == 3:
                        tile_full("att", 4, c, g == 1, f"att_g{s}")
                        v.done(tt(mod[:, bass.ds(v.i * 2 + (16 + g), 1)], lin[g][:, 0, 0:1],
                                  bada[:, bass.ds(v.i * 2 + (16 + g), 1)], ALU.add), f"att_ev{s}")
                    if e == 0 and i:
                        outputs_turned(i - 1)
                outputs_turned(QT - 1)
                v.after_own()

            all_chunks(v, "att")

            def low_og(k):
                v.wait(f"og_hi{k}")
                v.done(tt(xlo[:, k, 0:T1], tmp[:, k % 2, 0:T1], xhi[:, k, 0:T1].bitcast(F32), ALU.subtract), f"og_lo{k}")
            for k in range(KD):
                x, pr = divmod(k, NPAIR)
                v.after_own()
                v.done(stt(tmp[:, k % 2, 0:T1], zz[:, x, pr, :], 0.5, proj[:, Q_B * x + pr, :], ALU.mult, ALU.mult), f"og{k}")
                if k:
                    low_og(k - 1)
            low_og(KD - 1)
            for k in range(KD):
                c, m = divmod(k, 2)
                v.wait(f"wo_g{2 * k}")
                v.after_own()
                v.done(stt(tmp[:, 0, 0:T1], m_a[:, k, :], 1.0, lin[0][:, 0, :], ALU.add, ALU.mult), f"wo_ev{2 * k}")
                tile_full("wo", 0, c, m == 1, f"wo_g{2 * k + 1}")
                v.done(stt(sq[:, 0, 0:T1], m_b[:, k, META:T2], 1.0, lin[1][:, 0, :], ALU.add, ALU.mult), f"wo_ev{2 * k + 1}")
                v.after_own()
                v.done(tt(tmp[:, 1, 0:T1], tmp[:, 0, 0:T1], sq[:, 0, 0:T1], ALU.add), f"y{k}")
                v.wait(f"y_hi{k}")
                v.done(tt(ylo[:, k, :], tmp[:, 1, 0:T1], yhi[:, k, :].bitcast(F32), ALU.subtract), f"y_lo{k}")
            v.done(tt(gpost[:], gpost[:], mod[:, 16:24], ALU.mult))
            norm_adds_dve(v, "n1", T1, KD)
            norm_invert_dve(v, "n1", TB1)
            norm_rstd_dve(v, "n1", TB1)
            eng.wait_ge(s_x2, 16)

            def low_u(k):
                v.wait(f"u_hi{k}")
                v.done(stt(xlo[:, k, :], res[:, k, :], norm_c[:, 0, k:k + 1], xhi[:, k, :].bitcast(F32),
                           ALU.mult, ALU.subtract), f"u_lo{k}")
            for k in range(KD):
                v.after_own()
                v.done(stt(tmp[:, k % 2, 0:T1], m_a[:, k, :], gpost[:, k:k + 1], rstd[:, 0:T1], ALU.mult, ALU.mult))
                v.after_own()
                v.done(tt(res[:, k, META:T2], res[:, k, META:T2], tmp[:, k % 2, 0:T1], ALU.add), f"x1_{k}")
                if k:
                    low_u(k - 1)
            low_u(KD - 1)
            norm_invert_dve(v, "n2", TB2)
            norm_rstd_dve(v, "n2", TB2)
            v.done(tt(ssum[:], rstd[:], rstd[:], ALU.mult))

            v.done(eng.memset(cv[:, 0:2], 0.0))
            v.done(copy(wm_hi[:], wm[:]))
            v.after_own()
            v.done(tt(wm_lo[:], wm[:], wm_hi[:].bitcast(F32), ALU.subtract), "wm_split")
            with v.trips("cin", 8):
                for u in range(2):
                    f = bass.ds(v.i * 2 + u, 1)
                    v.wait(f"cin_ev{4 * u + 1}")
                    v.wait(f"cin_g{4 * u + 2}")
                    v.after_own()
                    for b, t0, n in TB2:
                        v.done(tt(cv[:, 2 + t0:2 + t0 + n], cc[:, t0:t0 + n], lin[0][:, b, 0:n], ALU.mult),
                               f"cin_ev{4 * u + 2}")
                    v.after_own()
                    v.done(tt(cv[:, 2:2 + T2], cv[:, 2:2 + T2], ssum[:], ALU.mult))
                    v.after_own()
                    v.done(ts(cy[:], cv[:, 0:T2], flat(conv_c[:, f, 0:1]), None, ALU.mult))
                    for w in (1, 2):
                        v.after_own()
                        v.done(stt(cy[:], cv[:, w:w + T2], flat(conv_c[:, f, w:w + 1]), cy[:], ALU.mult, ALU.add))
                    v.after_own()
                    v.done(tt(cy[:], cy[:], cb[:], ALU.mult))
                    v.after_own()
                    v.done(tt(cy[:], cy[:], rstd[:], ALU.mult))
                    tile_full("cin", 4, 2 * u + 1, True, None)
                    for b, t0, n in TB2:
                        v.done(tt(cz[:, t0:t0 + n], rstd[:, t0:t0 + n], lin[1][:, b, 0:n], ALU.mult),
                               f"cin_ev{4 * u + 3}")
                    v.wait(f"conv_th{u}")
                    v.done(stt(cz[:], sq[:, 0, :], 1.0, cz[:], ALU.add, ALU.mult))
                    v.after_own()
                    v.done(stt(tmp[:, u, :], cy[:], 0.5, cz[:], ALU.mult, ALU.mult), f"conv{u}")
                    v.wait(f"conv_hi{u}")
                    v.done(tt(flat(vlo[:, f, :]), tmp[:, u, :], flat(vhi[:, f, :]).bitcast(F32), ALU.subtract),
                           f"conv_lo{u}")
            v.done(eng.memset(ssum[:], 0.0))
            with v.trips("cout", 2):
                for c in range(4):
                    tile_full("cout", 4, c, True, None)
                    r = bass.ds(v.i * 4 + c, 1)
                    for b, t0, n in TB2:
                        v.done(tt(flat(res[:, r, t0:t0 + n]), flat(res[:, r, t0:t0 + n]), lin[c % 2][:, b, 0:n], ALU.add),
                               f"cout_ev{c}")
                    v.wait(f"n3_sq{c}")
                    v.after_own()
                    v.done(tt(ssum[:], ssum[:], sq[:, c % 2, :], ALU.add), f"n3_add{c}")
            norm_invert_dve(v, "n3", TB2)
            norm_rstd_dve(v, "n3", TB2)
            norm_apply_dve(v, "n3b", residual, 0, T2, lambda k: norm_c[:, 1, k:k + 1])

            v.done(eng.memset(rows[0:LH, 5, :], 0.0))
            v.done(eng.memset(ucur[:], 0.0))
            row = [rows[0:LH, r, :] for r in range(7)]
            v.wait("mgates")
            for b, t0, n in TB2:
                v.done(ts(rows[0:LH, 0, t0:t0 + n], aux[b][0:LH, 0:n], mb_c[0:LH, :], None, ALU.add))
                v.done(ts(rows[0:LH, 1, t0:t0 + n], aux[b][32:32 + LH, 0:n], mb_c[32:32 + LH, :], None, ALU.add), "rows_f")
            v.after_own()
            v.done(ts(row[3], row[1], 0.0, None, ALU.min))
            v.wait("rows_ln")
            v.after_own()
            v.done(tt(row[3], row[3], row[2], ALU.subtract))
            v.after_own()
            v.done(eng.tensor_tensor_scan(row[1], row[3], row[5], 0.0, ALU.add, ALU.add))
            v.after_own()
            v.done(tt(row[4], row[0], row[1], ALU.subtract))
            v.after_own()
            v.done(eng.tensor_tensor_scan(row[3], row[4], row[5], 0.0, ALU.max, ALU.max))
            v.after_own()
            v.done(tt(row[6], row[1], row[3], ALU.add))
            v.done(ts(row[5], row[3], -1.0, None, ALU.mult), "rows_done")
            v.after_own()

            with v.trips("mlstm", LH):
                hd = bass.ds(v.i, 1)
                v.done(ts(head_row[0:LH, :], ones[0:LH, :], ident[0:LH, hd], None, ALU.mult), "head_row")
                v.done(move(hcur[:], head_c[:, bass.ds(v.i * 4, 4)]))
                v.wait("bc")
                for b, t0, n in TB2:
                    v.done(copy(neg_m[:, t0:t0 + n], aux[b][:, 0:n]))
                s0, ln = STILES[0]
                v.done(copy(ucur[0:ln, 0:1], aux[3][0:ln, U_COL:U_COL + 1]))
                v.done(copy(ucur[:, 1:], aux[3][:, U_COL + 1:U_COL + len(STILES)]), "bc_ev_dve")
                v.after_own()
                for j, (s0, ln) in enumerate(STILES):
                    v.done(tt(att[0:ln, j, s0:s0 + ln], neg_m[0:ln, s0:s0 + ln], mask[0:ln, 0:ln], ALU.add), "masked")
                v.wait(f"decay{len(STILES) - 1}")
                for q, (b, t0, n, j) in enumerate(SBLOCKS):
                    ln = STILES[j][1]
                    v.wait(f"st{q}")
                    v.after_own()
                    v.done(stt(att[0:ln, j, t0:t0 + n], att[0:ln, j, t0:t0 + n], DK ** -0.5, aux[q % 4][0:ln, 0:n],
                               ALU.mult, ALU.mult), f"st_ev{q}")
                for j, (s0, ln) in enumerate(STILES):
                    v.wait(f"vtr{j}")
                    v.done(copy(v_tok[0:ln, j, :], aux[j % 4][0:ln, :]), f"vtk{j}")
                v.wait("h_ev1")
                v.done(tt(rden[:], rden[:], e_m[:], ALU.max))
                v.after_own()
                v.done(eng.reciprocal(rden[:], rden[:]))
                v.after_own()
                for x in range(1, 5):
                    for b, t0, n in TB2:
                        v.wait(f"h{2 * x + b}")
                        v.done(tt(v_T[:, x - 1, t0:t0 + n], h_banks(x)[b][:, 0:n], rden[:, t0:t0 + n], ALU.mult),
                               f"h_ev{2 * x + b}")
                    points[f"h_done{x - 1}"] = ("dve", "mlstm", v.own.n)
                norm_adds_dve(v, "hn", T2, 4)
                v.after_own()

                def z_gate(k):
                    v.wait(f"z_ml{k}")
                    for b, t0, n in TB2:
                        v.done(stt(sq[:, 1, t0:t0 + n], tmp[:, 0, t0:t0 + n], 1.0, lin[k % 2][:, b, 0:n], ALU.add, ALU.mult),
                               f"ml_ev{12 + k}")
                    v.after_own()

                def low_g(k):
                    v.wait(f"g_hi{k}")
                    v.done(tt(glo[:, k, :], gbuf[k % 2], ghi[:, k, :].bitcast(F32), ALU.subtract), f"g_lo{k}")

                z_gate(0)
                v.done(stt(oz[:, 0, :], oz[:, 0, :], 1.0, sq[:, 1, :], ALU.add, ALU.mult))
                norm_invert_dve(v, "hn", TB2)
                norm_rstd_dve(v, "hn", TB2)
                z_gate(1)
                v.done(stt(oz[:, 1, :], oz[:, 1, :], 1.0, sq[:, 1, :], ALU.add, ALU.mult))
                for k in range(4):
                    v.after_own()
                    v.done(stt(v_T[:, k, :], v_T[:, k, :], hcur[:, k:k + 1], rstd[:], ALU.mult, ALU.mult))
                    v.after_own()
                    if k >= 2:
                        v.done(stt(v_T[:, k, :], oz[:, k, :], 1.0, v_T[:, k, :], ALU.add, ALU.mult))
                        if k == 2:
                            low_g(1)
                        z_gate(k)
                    v.done(stt(gbuf[k % 2], v_T[:, k, :], 0.25, sq[:, 1, :] if k >= 2 else oz[:, k, :], ALU.mult, ALU.mult),
                           f"g{k}")
                    if k != 1:
                        low_g(k)
                v.after_own()
                for j in range(KD):
                    c, g = divmod(j, 4)
                    tile_full("mlstm", 10, 8 + c, g == 3, f"mlo_g{j}")
                    for b, t0, n in TB2:
                        v.done(tt(res[:, j, t0:t0 + n], res[:, j, t0:t0 + n], lin[j % 2][:, b, 0:n], ALU.add), f"mlo_ev{j}")
                    norm_add_dve(v, "n4", j, T1)
            norm_invert_dve(v, "n4", TB1)
            norm_rstd_dve(v, "n4", TB1)
            for k in range(KD):
                v.done(stt(res[:, k, META:T2], res[:, k, META:T2], norm_c[:, 2, k:k + 1], rstd[:, 0:T1],
                           ALU.mult, ALU.mult), f"out_t{k}")
            loops.update({("dve", k): val for k, val in dve_n.loops.items()})
    trips = dict(proj=2, att=NPAIR, cin=8, cout=2, mlstm=LH)
    return points, {k: (first, per, trips[k[1]]) for k, (first, per) in loops.items()}



def lay_out(i):
    def chunks(w, cols):
        k, n = w.shape
        return w.reshape(k // P, P, n // cols, cols).transpose(2, 1, 0, 3).reshape(n // cols, P, k // P * cols)

    def pairs(w, axis):
        s = list(w.shape)
        w = w.reshape(s[:axis] + [2, NPAIR, DH] + s[axis + 1:])
        return np.ascontiguousarray(np.swapaxes(w, axis, axis + 1)).reshape(s)

    def per_partition(a):
        return np.ascontiguousarray(a.reshape(-1, P).T)

    i = {k: np.asarray(a) for k, a in i.items()}
    ada, win = i['w_ada'][0], i['w_in'][0]
    q_a, kv3, g_n, z_a, q_b, kv_b, z_b, m_a, m_b = np.split(win, [512, 1280, 1304, 1816, 2328, 2584, 3096, 4120], axis=1)
    q_a, q_b, z_a, z_b = (pairs(w, 1) for w in (q_a, q_b, z_a, z_b))
    out = [chunks(np.concatenate([q_a, kv3, q_b, kv_b], 1), 256),
           chunks(i['w_cmp_k1'][0], P), chunks(i['w_cmp_v1'][0], P)]
    for t in range(NPAIR):
        cols = slice(P * t, P * t + P)
        wide = slice(256 * t, 256 * t + 256)
        out.append(chunks(np.concatenate([z_a[:, cols], z_b[:, cols], m_a[:, wide], m_b[:, wide],
                                          ada[:, 2 * D:][:, wide]], 1), 256))
    wo = [chunks(pairs(i[n][0], 0), 256) for n in ('w_o_nsa', 'w_o_swa')]
    out.append(np.concatenate(wo, 2))
    out.append(chunks(i['w_out'][0], 256))
    b_c_x_z = i['conv_in_w_2'][0].reshape(D, 4, KE, P)
    out.append(chunks(np.ascontiguousarray(b_c_x_z.transpose(0, 2, 1, 3)).reshape(D, -1), 256))
    out.append(chunks(i['conv_out_w_2'][0], P))
    q, k, v, o, z, g = np.split(i['mlstm_in_w_2'][0], [1024, 2048, 4096, 6144, 8192], axis=1)
    for h in range(LH):
        a, b = slice(DK * h, DK * (h + 1)), slice(DV * h, DV * (h + 1))
        out.append(chunks(np.concatenate([q[:, a], k[:, a], v[:, b], o[:, b], z[:, b]], 1), 256))
        out.append(chunks(i['mlstm_out_w_2'][0][b], 512))
    out.append(np.zeros((1, P, CHUNK), np.float32))
    stream = np.concatenate(out, 0)
    assert stream.shape == (N_CHUNKS + 1, P, CHUNK)
    w_mgate = np.zeros((D, MG), np.float32)
    w_mgate[:, 0:LH], w_mgate[:, 32:MG] = g[:, :LH], g[:, LH:]
    mgate_b = np.zeros((P, 1), np.float32)
    mgate_b[0:LH, 0], mgate_b[32:32 + LH, 0] = i['mlstm_gate_b_2'][0, :LH], i['mlstm_gate_b_2'][0, LH:]

    def tiles(w):
        return np.ascontiguousarray(w.reshape(-1, P, w.shape[1]).transpose(1, 0, 2))
    def twice(a):
        return np.concatenate([a, a], 0)

    w2k = i['w_cmp_k2'][0]
    small = dict(
        c=per_partition(i['c']), b_ada=per_partition(i['b_ada']), g_pre=per_partition(i['g_pre']),
        g_post=per_partition(i['g_post']), w_gate=tiles(g_n), w_mgate=tiles(w_mgate), sinks=np.broadcast_to(i['sinks'], (P, NH)),
        w_k2=tiles(np.concatenate([w2k, w2k], 1)), w_v2=tiles(i['w_cmp_v2'][0]),
        norm_w=np.concatenate([per_partition(i['norm_w_2'][0]), per_partition(i['norm_w_2'][1]),
                               per_partition(i['final_norm_w_2'])], 1),
        conv_w=i['conv_w_2'][0].reshape(3, KE, P).transpose(2, 1, 0), head_w=per_partition(i['mlstm_head_norm_w_2']),
        mgate_b=mgate_b, pe=np.concatenate([twice(i['pe_cmp_k'][0].T), twice(i['pe_cmp_v'][0].T)], 1))
    smalls = np.concatenate([small[n].reshape(P, width) for n, width in SMALL], 1)
    return dict(wstream=stream, w_ada=np.ascontiguousarray(chunks(ada[:, :2 * D], 256)), smalls=smalls,
                x_t=tiles(i['x'][0].T), meta_t=tiles(i['meta_tokens_2'].T))


def kernel(**inputs):
    import concourse.bacc as _bacc
    from concourse import mybir as _mybir
    from concourse.bass_utils import run_bass_kernel_spmd as _run

    arrays = lay_out(inputs)
    known = dict(points={}, loops={}, sems={})
    for _ in range(2):
        nc = _bacc.Bacc("TRN2", target_bir_lowering=False, num_devices=1)
        args = {n: nc.dram_tensor(n, a.shape, _mybir.dt.from_np(a.dtype), kind="ExternalInput").ap()
                for n, a in arrays.items()}
        out = nc.dram_tensor("out_t", (D, T1), _mybir.dt.float32, kind="ExternalOutput").ap()
        points, loops = build(nc, known, out_t=out, **args)
        known = dict(points=points, loops=loops, sems={})
    r = _run(nc, [arrays], core_ids=[0])
    return np.ascontiguousarray(r.results[0]["out_t"].T).reshape(1, T1, D)
```

```python
import numpy as np

import concourse.bass as bass
from concourse import mybir
from concourse.alu_op_type import AluOpType as ALU
from contextlib import ExitStack, contextmanager

F32 = mybir.dt.float32
F32R = mybir.dt.float32r
ACT = mybir.ActivationFunctionType
AX = mybir.AxisListType

P = 128
D = 1024
KD = D // P
T1 = 512
META = 16
T2 = META + T1
EPS = 1e-6
NEG = -1e30
DH = 64
NH = 8
QT = T1 // P
NPAIR = NH // 2
CB, CS = 32, 16
NC = (T1 - CB) // CS + 1
WINDOW = 128
LH = 4
DK, DV = 256, 512
KE = 2 * D // P
CHUNK = 2048

TB1 = [(0, 0, T1)]
TB2 = [(0, 0, META + 256), (1, META + 256, 256)]
STILES = [(0, META)] + [(META + P * j, P) for j in range(T1 // P)]

N_ADA, N_GATE = 8, 4
POOL_ADA = [1, 4]
N_PROJ, N_ATT, N_WO, N_OUT = 10, 16, 4, 4
N_CIN, N_COUT, N_MLSTM = 32, 8, 40
STAGES = dict(proj=N_PROJ, att=N_ATT, wo=N_WO, out=N_OUT,
              cin=N_CIN, cout=N_COUT, mlstm=N_MLSTM)
START = {}
for _stage in STAGES:
    START[_stage] = sum(list(STAGES.values())[:len(START)])
N_CHUNKS = sum(STAGES.values())
N_SELECT, SELECT_BLOCK = 16, 64
assert N_SELECT * SELECT_BLOCK >= T1 and WINDOW == P
MG = 32 + LH
SMALL = [("c", KD), ("b_ada", 24), ("g_pre", KD), ("g_post", KD), ("w_gate", 24 * KD), ("w_mgate", MG * KD), ("sinks", NH),
         ("w_k2", 2 * P), ("w_v2", 2 * DH), ("norm_w", 3 * KD), ("conv_w", 3 * KE), ("head_w", KE),
         ("mgate_b", 2), ("pe", 2 * CB)]


class Counter:

    def __init__(self, name, sem, known):
        self.name, self.sem, self.known, self.n = name, sem, known, 0
        self.loop, self.outer, self.loops = None, 0, {}

    def enter(self, loop):
        self.loop, self.outer, self.n = loop, self.n, 0

    def leave(self, trips):
        self.loops[self.loop] = (self.outer, self.n)
        self.n = self.outer + trips * self.n
        self.loop = None


class Engine:

    def __init__(self, eng, counters, known, points):
        self.e, self.counters, self.known, self.points = eng, counters, known, points
        self.own = counters[0]
        self.loop = None
        self.i = 0

    @contextmanager
    def trips(self, name, count):
        for c in self.counters:
            c.enter(name)
        self.loop = name
        with self.e.bass.Fori(0, count, 1, engines=[self.e.engine]) as i:
            self.i = i
            yield i
        for c in self.counters:
            c.leave(count)
        self.loop, self.i = None, 0

    def done(self, ins, point=None, counter=None):
        c = counter or self.own
        ins.then_inc(c.sem, 1)
        c.n += 1
        if point:
            self.points[point] = (c.name, c.loop, c.n)
        return ins

    def value(self, name, loop, local, lag=0):
        if loop is None:
            return local
        first, per, trips = self.known["loops"][name, loop]
        if loop == self.loop:
            assert first + local - lag * per > 0
            return self.i * per + (first + local - lag * per)
        return first + (trips - 1) * per + local

    def wait(self, point, lag=0):
        if point in self.known["points"]:
            name, loop, local = self.known["points"][point]
            self.e.wait_ge(self.known["sems"][name], self.value(name, loop, local, lag))
        else:
            assert not self.known["points"], point

    def after_own(self):
        if self.known["points"]:
            self.e.wait_ge(self.own.sem, self.value(self.own.name, self.loop, self.own.n))


def build(nc, known, wstream, w_ada, smalls, x_t, meta_t, out_t):
    points, ctx = {}, ExitStack()
    with ctx:
        def sb(name, shape, dt=F32, stack=ctx, side="left"):
            return stack.enter_context(nc.sbuf_tensor(name, [P] + list(shape), dt, side=side))

        def psum(name, shape):
            return ctx.enter_context(nc.psum_tensor(name, [P] + list(shape), F32))

        def sem(name):
            return ctx.enter_context(nc.semaphore(name))

        raw_full = [sem("raw_full0"), sem("raw_full1")]
        s_hi = sem("chunk_hi")
        s_lo = sem("chunk_lo")
        s_small = sem("small_in")
        s_x = sem("x_in")
        s_x2 = sem("x_again")
        s_const = sem("const")
        s_ada = [sem(f"ada{i}") for i in range(N_ADA + N_GATE)]
        s_sum = sem("pool_sums")
        s_out = sem("out_stored")
        s_pe, s_chunk, s_act, s_dve = sem("pe"), sem("pe_chunk"), sem("act"), sem("dve")
        s_slot = sem("last_slots")
        known["sems"] = dict(pe=s_pe, chunk=s_chunk, act=s_act, dve=s_dve, slot=s_slot)

        lin = [psum("lin0", [2, 512]), psum("lin1", [2, 512])]
        aux = [psum(f"aux{i}", [512]) for i in range(4)]

        raw = [sb(f"w_raw{i}", [CHUNK]) for i in range(2)]
        whi = [sb(f"w_hi{i}", [CHUNK], F32R) for i in range(2)]
        wlo = [sb(f"w_lo{i}", [CHUNK], F32R) for i in range(2)]
        xhi = sb("x_hi", [KD, T2], F32R)
        xlo = sb("x_lo", [KD, T2], F32R)
        res = sb("residual", [KD, T2])
        ident = sb("ident", [P])
        ones = sb("ones", [P])
        tmp = sb("tmp", [2, T2])
        sq = sb("squares", [2, T2])
        ssum = sb("square_sum", [T2])
        rstd = sb("rstd", [T2])
        rcol = sb("rstd_columns", [len(STILES)])
        mask = sb("mask", [P])
        eps = sb("eps", [1])
        small_c = sb("small_inputs", [sum(n for _, n in SMALL)])

        def small_of(name):
            start = 0
            for other, n in SMALL:
                if other == name:
                    return small_c[:, start:start + n]
                start += n

        norm_c = small_of("norm_w").rearrange("p (a k) -> p a k", a=3)
        conv_c = small_of("conv_w").rearrange("p (k w) -> p k w", w=3)
        head_c, mb_c, c_in, bada = (small_of(n) for n in ("head_w", "mgate_b", "c", "b_ada"))
        gpre, gpost, sink_c = (small_of(n) for n in ("g_pre", "g_post", "sinks"))
        wg = small_of("w_gate").rearrange("p (k n) -> p k n", k=KD)
        wm = small_of("w_mgate").rearrange("p (k n) -> p k n", k=KD)
        w2k = small_of("w_k2").rearrange("p (k n) -> p k n", k=2)
        w2v = small_of("w_v2").rearrange("p (k n) -> p k n", k=2)
        pe_c = small_of("pe").rearrange("p (s b) -> p s b", s=2)

        one, stage_c, stage_d = ExitStack(), ExitStack(), ExitStack()

        def sb1(name, shape, dt=F32):
            return sb(name, shape, dt, one)

        K_C, V_C, K_S, V_S, K_W, V_W, Q_B, K_B, V_B = 4, 5, 6, 7, 8, 9, 10, 14, 15
        o_tok = sq[:, :, 0:2 * P].rearrange("p a (x d) -> p a x d", x=2)
        dist = sb1("dist", [T1])
        dist_w = sb1("dist_w", [2 * P])
        dist_c = sb1("dist_c", [QT, 32])
        mod = sb1("mod", [24])
        scale_c = sb1("scale_c", [KD])
        gate = sb1("gates", [QT, 24])
        gcur = sb1("gates_pair", [2, QT, 3])
        slopes = sb1("slopes", [NH])
        scur = sb1("slopes_pair", [2])
        sinkcur = sb1("sinks_pair", [2])
        seen = sb1("cmp_seen", [1])
        nmaxs = sb1("neg_max", [2, 4])
        prob_ss = sb1("prob_sum", [2, 4])
        coefs = sb1("coef", [2, 4])
        kct = sb1("kc_T", [2 * NC])
        vct = sb1("vc_tok", [2, DH])
        Q_HEADS = K_C
        wg_hi = sb("w_gate_hi", [KD, 24], F32R, stage_c)
        wg_lo = sb("w_gate_lo", [KD, 24], F32R, stage_c)
        cmp_th = sb("cmp_th", [256], stack=stage_c)
        hid_tok = sb("cmp_hid_tok", [256], stack=stage_c)
        hid = sb("cmp_hid", [2, 2, 2 * NC], stack=stage_c)
        stage_a = ExitStack()
        ada_w = sb("ada_shift_scale", [N_ADA, CHUNK], stack=stage_a, side="right")
        ada_acc = sb("ada_sums", [N_ADA, 256], stack=stage_a, side="right")
        stage_a.close()
        proj = sb("proj", [16, T1], stack=stage_d, side="right")
        probs = [sb(f"prob{i}", [1316], stack=stage_d, side="right") for i in range(2)]
        probs_T = [sb(f"prob_T{i}", [1408], stack=stage_d, side="right") for i in range(2)]
        cin = sb("cmp_in", [CB // 2, 2, NC], stack=stage_c)
        cin_hi = [sb(f"cmp_in_hi{s}", [CB // 2, 2, NC], F32R, stage_c) for s in range(2)]
        cin_lo = [sb(f"cmp_in_lo{s}", [CB // 2, 2, NC], F32R, stage_c) for s in range(2)]
        stage_c.close()
        zz = sb1("z", [2, NPAIR, T1])
        m_a = sb1("merge_a", [KD, T1])
        m_b = res
        stage_d.close()
        stage_e = ExitStack()
        yhi = sb("y_hi", [KD, T1], F32R, stage_e, "right")
        ylo = sb("y_lo", [KD, T1], F32R, stage_e, "right")
        gate_w = sb("ada_gate", [2, CHUNK], stack=stage_e, side="right")
        gate_acc = sb("ada_gate_sums", [N_GATE, 256], stack=stage_e, side="right")
        stage_e.close()
        one.close()

        conv, ml = ExitStack(), ExitStack()
        wm_hi = sb("w_mgate_hi", [KD, MG], F32R)
        wm_lo = sb("w_mgate_lo", [KD, MG], F32R)
        vhi = sb("conv_hi", [KE, T2], F32R, conv)
        vlo = sb("conv_lo", [KE, T2], F32R, conv)
        cb = sb("conv_b", [T2], stack=conv)
        cc = sb("conv_c_gate", [T2], stack=conv)
        cv = sb("conv_in", [2 + T2], stack=conv)
        cy = sb("conv_y", [T2], stack=conv)
        cz = sb("conv_tanh", [T2], stack=conv)
        conv.close()

        def sb2(name, shape, dt=F32):
            return sb(name, shape, dt, ml)

        mix = sb2("mix", [2 * len(STILES) * DV], F32R)
        v_hi, v_lo = (mix[:, x * len(STILES) * DV:(x + 1) * len(STILES) * DV].rearrange("p (j n) -> p j n", j=len(STILES))
                      for x in range(2))
        ghi, glo = (mix[:, x * 4 * T2:(x + 1) * 4 * T2].rearrange("p (k n) -> p k n", k=4) for x in range(2))
        qk = sb2("qk_T", [4, T2])
        v_T = sb2("v_T", [4, T2])
        att = sb2("att_T", [len(STILES), T2])
        att_hi = sb2("att_T_hi", [len(STILES), T2], F32R)
        att_lo = sb2("att_T_lo", [len(STILES), T2], F32R)
        ones_r = sb2("ones_r", [P], F32R)
        oz = qk
        neg_m = sb2("neg_m", [T2])
        e_m = sb2("e_m", [T2])
        rden = sb2("rden", [T2])
        ucur = sb2("u_head", [len(STILES)])
        head_row = sb2("head_row", [P])
        hcur = sb2("head_w_cur", [4])
        rows = sb2("gate_rows", [3, T2])
        row = [buf[0:LH, :] for buf in (neg_m, e_m, rden, tmp[:, 0, :])] + [rows[0:LH, x, :] for x in range(3)]
        u_rstd = sb2("u_rstd", [T2])
        ml.close()

        loops = {}
        pe_n, ch_n = Counter("pe", s_pe, known), Counter("chunk", s_chunk, known)
        slot_n = Counter("slot", s_slot, known)
        act_n, dve_n = Counter("act", s_act, known), Counter("dve", s_dve, known)
        block = ctx.enter_context(nc.Block())


        @block.sync
        def _(eng):
            eng.dma_start(small_c[:], smalls).then_inc(s_small, 16)
            for c in range(N_ADA):
                eng.dma_start(ada_w[:, c, :], w_ada[c, :, :]).then_inc(s_ada[c], 16)
            for h in range(2):
                eng.dma_start(raw[h][:], wstream[h, :, :]).then_inc(raw_full[h], 16)
            with eng.bass.Fori(0, N_CHUNKS // 2 - 1, 1, engines=[eng.engine]) as i:
                for h in range(2):
                    eng.wait_ge(s_lo, i * 2 + (h + 1))
                    eng.dma_start(raw[h][:], wstream[bass.ds(i * 2 + (h + 2), 1), :, :]
                                  .rearrange("a p n -> (a p) n")).then_inc(raw_full[h], 16)
            eng.wait_ge(s_lo, N_CHUNKS - 1)
            eng.dma_start(raw[0][:], wstream[N_CHUNKS, :, :]).then_inc(raw_full[0], 16)
            eng.wait_ge(s_out, 16 * KD)

        @block.gpsimd
        def _(eng):
            eng.memset(ident[:], 0.0).then_inc(s_const, 1)
            eng.memset(ones[:], 1.0).then_inc(s_const, 1)
            eng.memset(mask[:], 0.0).then_inc(s_const, 1)
            eng.memset(eps[:], EPS).then_inc(s_const, 1)
            for h in range(NH):
                eng.memset(slopes[:, h:h + 1], 2.0 ** -(8.0 * (h + 1) / NH)).then_inc(s_const, 1)
            eng.memset(seen[:], 1.0).then_inc(s_const, 1)
            eng.iota(dist[:], [[1, T1]], base=-(T1 - P), channel_multiplier=-1,
                     allow_small_or_imprecise_dtypes=True).then_inc(s_const, 1)
            eng.iota(dist_c[:], [[-P, QT], [CS, 32]], base=CB - 1, channel_multiplier=-1,
                     allow_small_or_imprecise_dtypes=True).then_inc(s_const, 1)
            eng.wait_ge(s_const, 15)
            eng.affine_select(out=ident[:], in_=ident[:], compare_op=ALU.not_equal, fill=1.0, base=0,
                              pattern=[[-1, P]], channel_multiplier=1).then_inc(s_const, 1)
            eng.affine_select(out=mask[:], in_=mask[:], compare_op=ALU.is_ge, fill=NEG, base=0,
                              pattern=[[1, P]], channel_multiplier=-1).then_inc(s_const, 1)
            eng.affine_select(out=seen[:], in_=seen[:], compare_op=ALU.is_ge, fill=0.0, base=-(CB - 1),
                              pattern=[[0, 1]], channel_multiplier=1).then_inc(s_const, 1)
            eng.affine_select(out=dist[:], in_=dist[:], compare_op=ALU.is_ge, fill=NEG, base=T1 - P,
                              pattern=[[-1, T1]], channel_multiplier=1).then_inc(s_const, 1)
            eng.affine_select(out=dist_c[:], in_=dist_c[:], compare_op=ALU.is_ge, fill=NEG, base=-(CB - 1),
                              pattern=[[P, QT], [-CS, 32]], channel_multiplier=1).then_inc(s_const, 1)
            eng.wait_ge(s_const, 20)
            eng.affine_select(out=dist_w[:], in_=dist[:, T1 - 2 * P:T1], compare_op=ALU.is_gt, fill=NEG,
                              base=0, pattern=[[1, 2 * P]], channel_multiplier=-1).then_inc(s_const, 1)
            eng.wait_ge(s_small, 16)
            n = 0
            for c in POOL_ADA:
                eng.wait_ge(s_ada[c], 16)
                w = ada_w[:, c, :]
                eng.tensor_tensor(w.rearrange("p (k n) -> p k n", k=KD), w.rearrange("p (k n) -> p k n", k=KD),
                                  c_in.unsqueeze(2).to_broadcast([P, KD, 256]), ALU.mult).then_inc(s_sum, 1)
                n += 1
                for half in (1024, 512, 256):
                    eng.wait_ge(s_sum, n)
                    out = w[:, 0:half] if half > 256 else ada_acc[:, c, :]
                    eng.tensor_tensor(out, w[:, 0:half], w[:, half:2 * half], ALU.add).then_inc(s_sum, 1)
                    n += 1
            with eng.bass.Fori(0, N_CHUNKS // 2, 1, engines=[eng.engine]) as i:
                for h in range(2):
                    eng.wait_ge(s_hi, i * 2 + (h + 1))
                    eng.tensor_tensor(wlo[h][:], raw[h][:], whi[h][:].bitcast(F32), ALU.subtract).then_inc(s_lo, 1)
            eng.wait_ge(s_hi, N_CHUNKS + 1)
            eng.tensor_tensor(wlo[0][:], raw[0][:], whi[0][:].bitcast(F32), ALU.subtract).then_inc(s_lo, 1)


        def chunk_lands_and_splits(a, per, first):
            h = first % 2
            a.e.wait_ge(raw_full[h], a.i * (8 * per) + 16 * (first // 2 + 1) if per else 16 * (first // 2 + 1))
            if per:
                a.e.wait_ge(s_chunk, a.i * per + (N_ADA + first - 1))
            elif first > 1:
                a.e.wait_ge(s_chunk, N_ADA + first - 1)
            a.e.activation(whi[h][:], raw[h][:], ACT.Copy).then_inc(s_hi, 1)

        def chunk_ready(t, per, first):
            t.e.wait_ge(s_lo, t.i * per + (first + 1) if per else first + 1)

        def group(t, half, col, stride, kts, outs, hi_of, lo_of, point=None, chunk_end=False, ks=None, ready=None):
            ks = range(kts) if ks is None else ks
            n = 3 * ks[0]
            for k in ks:
                if ready and ready(k):
                    t.wait(ready(k))
                c0 = k * stride + col
                for w, x in ((whi, hi_of), (whi, lo_of), (wlo, hi_of)):
                    for o, (_, t0, cnt) in outs:
                        ins = t.e.matmul(o, w[half][:, c0:c0 + P], x(k, t0, cnt), start=(n == 0),
                                         stop=(n == 3 * kts - 1))
                    n += 1
            if n == 3 * kts:
                t.done(ins, point, ch_n if chunk_end else None)

        def lin_outs(slot, tbs):
            return [(lin[slot][:, b, 0:n], (b, t0, n)) for b, t0, n in tbs]

        def x_hi(k, t0, n):
            return xhi[:, k, t0:t0 + n]

        def x_lo(k, t0, n):
            return xlo[:, k, t0:t0 + n]


        def norm_squares_act(a, nm, src, t0, n, tiles, ready=None):
            for k in range(tiles):
                if ready:
                    a.wait(f"{ready}{k}")
                if k >= 2:
                    a.wait(f"{nm}_add{k - 2}")
                a.done(a.e.activation(sq[:, k % 2, 0:n], src(k, t0, n), ACT.Square), f"{nm}_sq{k}")

        def norm_add_dve(v, nm, k, n):
            v.wait(f"{nm}_sq{k}")
            if k == 1:
                v.done(v.e.tensor_tensor(ssum[:, 0:n], sq[:, 0, 0:n], sq[:, 1, 0:n], ALU.add), f"{nm}_add1")
            elif k > 1:
                v.after_own()
                v.done(v.e.tensor_tensor(ssum[:, 0:n], ssum[:, 0:n], sq[:, k % 2, 0:n], ALU.add), f"{nm}_add{k}")
            else:
                points[f"{nm}_add0"] = (v.own.name, v.loop, v.own.n + 1)

        def norm_adds_dve(v, nm, n, tiles):
            for k in range(tiles):
                norm_add_dve(v, nm, k, n)

        def token_tiles(tbs):
            return [(j, s0 - (META if tbs is TB1 else 0), ln) for j, (s0, ln) in enumerate(STILES)
                    if j or tbs is TB2]

        def total_columns(t, src, tbs, bank_of, first=True, last=True):
            for j, t0, ln in token_tiles(tbs):
                ins = t.e.matmul(bank_of(j)[0:ln, j:j + 1], src[:, t0:t0 + ln], ones[:, 0:1], start=first, stop=last)
            return ins

        def norm_total_pe(t, nm, tbs, tiles, bank=2):
            t.wait(f"{nm}_add{tiles - 1}")
            t.done(total_columns(t, ssum, tbs, lambda j: aux[bank]), f"{nm}_tot")

        sum_banks = aux + [lin[0][:, 1, :]]

        def growing_totals_pe(t, nm, tbs, n):
            for k in range(KD):
                t.wait(f"{nm}_sq{k}")
                t.done(total_columns(t, sq[:, k % 2, 0:n], tbs, lambda j: sum_banks[j], k == 0, k == KD - 1),
                       f"{nm}_part{k}" if k < KD - 1 else f"{nm}_tot")

        def grown_root_act(a, nm, tbs, width):
            a.wait(f"{nm}_tot")
            for j, _, ln in token_tiles(tbs):
                a.done(a.e.activation(rcol[0:ln, j:j + 1], sum_banks[j][0:ln, j:j + 1], ACT.Sqrt, bias=eps[0:ln, :],
                                      scale=1.0 / width), f"{nm}_root")

        def column_parts(tbs):
            return [(P, 1, len(STILES))] + ([(META, 0, 1)] if tbs is TB2 else [])

        def norm_root_act(a, nm, tbs, width, bank=2):
            a.wait(f"{nm}_tot")
            for rows_, c0, c1 in column_parts(tbs):
                a.done(a.e.activation(rcol[0:rows_, c0:c1], aux[bank][0:rows_, c0:c1], ACT.Sqrt, bias=eps[0:rows_, :],
                                      scale=1.0 / width), f"{nm}_root")

        def norm_invert_dve(v, nm, tbs):
            v.wait(f"{nm}_root")
            for rows_, c0, c1 in column_parts(tbs):
                v.done(v.e.reciprocal(rcol[0:rows_, c0:c1], rcol[0:rows_, c0:c1]), f"{nm}_inv")

        def norm_spread_pe(t, nm, tbs, banks=(2, 3)):
            t.wait(f"{nm}_inv")
            for j, t0, ln in token_tiles(tbs):
                b = max(b for b, first, _ in tbs if first <= t0)
                o = t0 - tbs[b][1]
                ins = t.e.matmul(aux[banks[b]][:, o:o + ln], rcol[0:ln, j:j + 1].to_broadcast([ln, P]), ident[0:ln, 0:ln],
                                 start=True, stop=True)
            t.done(ins, f"{nm}_spread")

        def norm_rstd_dve(v, nm, tbs, banks=(2, 3)):
            v.wait(f"{nm}_spread")
            for b, t0, n in tbs:
                v.done(v.e.tensor_copy(rstd[:, t0:t0 + n], aux[banks[b]][:, 0:n]), f"{nm}_rstd")
            v.after_own()

        v_banks = [lin[0][:, 1, :], lin[1][:, 1, :], aux[0]]

        def att_banks(e):
            return (aux[0], aux[1], aux[2]) if e == 0 else (aux[3], lin[0][:, 1, :], lin[1][:, 1, :])

        def turn_bank(i):
            return aux[1] if i < QT - 1 else lin[0][:, 1, :]

        def v_of(tile, j, e):
            return proj[:, tile, P * j + e * DH:P * j + (e + 1) * DH]

        CHUNK_TILE = {0: K_C, 1: K_S, 3: K_W, 8: K_B}
        BEFORE = {1: 0, 3: 1, 5: 3, 8: 5}
        V_TILES, V_CHUNK = (V_S, V_W, V_B), (1, 3, 8)
        SBLOCKS = [(b, max(STILES[j][0], t0), t0 + n - max(STILES[j][0], t0), j)
                   for b, t0, n in TB2 for j in range(len(STILES)) if STILES[j][0] < t0 + n]

        gbuf = [tmp[:, 1, :], sq[:, 0, :]]
        U_COL = 300

        def h_banks(x):
            return aux[2:4] if x % 2 == 0 else aux[0:2]

        PAIR = [(e * DH, e * DH + DH) for e in range(2)]


        @block.tensor
        def _(eng):
            t = Engine(eng, [pe_n, ch_n], known, points)

            eng.wait_ge(s_const, 21)
            growing_totals_pe(t, "n0", TB1, T1)
            for c in range(N_ADA):
                if c in POOL_ADA:
                    eng.wait_ge(s_sum, 4 * (POOL_ADA.index(c) + 1))
                else:
                    t.wait(f"ada{c}")
                for j in (2 * c, 2 * c + 1):
                    ins = eng.matmul(aux[0][:, j:j + 1], ada_acc[:, c, P * (j % 2):P * (j % 2) + P], ones[:, 0:1],
                                     start=True, stop=True)
                t.done(ins, None, ch_n)
                if c == N_ADA - 2:
                    norm_spread_pe(t, "n0", TB1)

            def project(c, first, between=None):
                chunk_ready(t, 0, START["proj"] + c)
                for g in range(2):
                    if not first:
                        t.wait(f"proj_ev{BEFORE[c]}{g}")
                    group(t, c % 2, g * P, 256, KD, lin_outs(g, TB1), x_hi, x_lo, f"proj_g{c}", g == 1,
                          ready=(lambda k: f"n0b_lo{k}") if first and g == 0 else None)
                    if g == 0 and between:
                        between()

            def compress(c, src, half):
                chunk_ready(t, 0, START["proj"] + c)
                t.wait(f"cin_lo{src}")
                for k in range(8):
                    for p, (x, w) in enumerate(((cin_hi[src], whi), (cin_lo[src], whi), (cin_hi[src], wlo))):
                        ins = eng.matmul(aux[2 + src][0:2 * NC, 0:256], x[:, 8 * half + k, :, :].rearrange("p g j -> p (g j)"),
                                         w[c % 2][:, 256 * k:256 * k + 256], start=(half == 0 and k == 0 and p == 0),
                                         stop=(half == 1 and k == 7 and p == 2))
                t.done(ins, None, ch_n)

            def turn_hidden(src):
                t.wait(f"hid_tok{src}")
                for j in range(2):
                    ins = eng.transpose(aux[2 + src][:, 64 * j:64 * j + 2 * NC], hid_tok[0:2 * NC, P * j:P * j + P],
                                        ident[0:2 * NC, 0:2 * NC])
                t.done(ins, f"hT{src}")

            def turn_values(s, last_chunk=False):
                t.wait(f"proj_ev{V_CHUNK[s]}1")
                for i in range(QT):
                    ins = eng.transpose(v_banks[s][:, P * i:P * i + P], proj[:, V_TILES[s], P * i:P * i + P], ident[:])
                    if i == 0 and last_chunk:
                        t.done(ins, None, ch_n)
                t.done(ins, f"vt{s}")

            project(0, True)
            project(1, False)
            compress(2, 0, 0)
            turn_values(0)
            project(3, False)
            compress(4, 0, 1)
            turn_values(1)
            project(5, False)
            turn_hidden(0)
            compress(6, 1, 0)
            t.wait("wg_split")
            n = 0
            for k in range(KD):
                for w, x in ((wg_hi, xhi), (wg_hi, xlo), (wg_lo, xhi)):
                    ins = eng.matmul(aux[0][0:24, :], w[:, k, :], x[:, k, 0:T1], start=(n == 0), stop=(n == 3 * KD - 1))
                    n += 1
            t.done(ins, "gates")
            t.wait("hid0")
            for j in range(2):
                ins = eng.matmul(aux[1][:, 0:2 * NC], w2k[:, j, :], hid[:, 0, j, :], start=(j == 0), stop=(j == 1))
            t.done(ins, "kc")
            compress(7, 1, 1)
            t.wait("gate_th")
            t.wait("kc_ready")
            for i in range(QT):
                ins = eng.transpose(aux[1][:, 24 * i:24 * i + 24], sq[0:24, 0, P * i:P * i + P], ident[0:24, 0:24])
            t.done(ins, "gates_T")
            project(8, False, lambda: turn_hidden(1))
            t.wait("gates_ready")
            t.wait("hid1")
            for g in range(2):
                for j in range(2):
                    ins = eng.matmul(aux[1][0:NC, 128 + g * DH:128 + (g + 1) * DH], hid[:, 1, j, g * NC:(g + 1) * NC],
                                     w2v[:, j, :], start=(j == 0), stop=(j == 1))
            t.done(ins, "vc")
            chunk_ready(t, 0, START["proj"] + 9)
            turn_values(2, last_chunk=True)

            t.wait("kvc_ready")
            t.wait("vtok2")
            with t.trips("att", NPAIR):
                def scores(s):
                    i, e = divmod(s, 2)
                    lo, hi = PAIR[e]
                    b = att_banks(e)
                    keys, k0 = P * (i + 1), max(0, P * (i - 1))
                    t.wait(f"out{(s - 2) % 8}", 0 if s >= 2 else 1)
                    if e == 0:
                        t.wait(f"o_T_ev{(i - 2) % 4}", 0 if i >= 2 else 1)
                    if s == 0:
                        t.wait("proj_ev51")
                        t.wait("att_ev7", 1)
                    if s == 1:
                        t.wait("o_T_ev3", 1)
                    qa = proj[lo:hi, K_C, P * i:P * i + P]
                    qb = proj[lo:hi, V_C, P * i:P * i + P]
                    eng.matmul(b[0][:, 0:keys], qa, proj[lo:hi, K_S, 0:keys], start=True, stop=True)
                    eng.matmul(b[1][:, 0:keys], qa, proj[lo:hi, K_W, 0:keys], start=True, stop=True)
                    eng.matmul(b[2][:, 0:NC], qa, kct[lo:hi, e * NC:(e + 1) * NC], start=True, stop=True)
                    w0 = 32 + (P if i == 0 else 0)
                    t.done(eng.matmul(b[2][:, w0:w0 + keys - k0], qb, proj[lo:hi, K_B, k0:keys], start=True, stop=True),
                           f"s{s}")

                def turn_outputs(i):
                    t.wait(f"out{2 * i + 1}")
                    for x in range(2):
                        ins = eng.transpose(turn_bank(i)[:, P * x:P * x + P], o_tok[:, i % 2, x, :], ident[:])
                    t.done(ins, f"o_T{i}")

                scores(0)
                for s in range(2 * QT):
                    i, e = divmod(s, 2)
                    b = att_banks(e)
                    prob, prob_T = probs[e], probs_T[e]
                    c, g = divmod(s, 2)
                    if g == 0:
                        chunk_ready(t, 4, START["att"] + c)
                    t.wait(f"att_ev{(s - 2) % 8}", 0 if s >= 2 else 1)
                    group(t, c % 2, g * P, 256, KD, lin_outs(g, TB1), x_hi, x_lo, ks=range(KD // 2))
                    t.wait(f"exp{s}")
                    for j in range(i + 1):
                        eng.transpose(b[0][:, P * j:P * j + P], prob[:, P * j:P * j + P], ident[:])
                    for j in range(i + 1):
                        eng.transpose(b[1][:, P * j:P * j + P], prob[:, 512 + P * j:512 + P * j + P], ident[:])
                    eng.transpose(b[2][0:NC, 0:P], prob[:, 1024:1024 + NC], ident[:])
                    js = (1,) if i == 0 else (0, 1)
                    for j in js:
                        ins = eng.transpose(b[2][:, P + P * j:2 * P + P * j],
                                            prob[:, 1056 + P * j:1056 + P * j + P], ident[:])
                    t.done(ins, f"pt{s}")
                    if s + 1 < 2 * QT:
                        scores(s + 1)
                    group(t, c % 2, g * P, 256, KD, lin_outs(g, TB1), x_hi, x_lo, f"att_g{s}", g == 1,
                          ks=range(KD // 2, KD))
                    t.wait(f"pt_ev{s}_act")
                    t.wait(f"pt_ev{s}_dve")
                    o = b[0]
                    eng.matmul(o[:, 0:DH], prob_T[0:NC, 1024:1152], vct[0:NC, e, :], start=True, stop=True)
                    for x, tile in ((0, V_S), (1, V_W)):
                        for j in range(i + 1):
                            eng.matmul(o[:, DH * (x + 1):DH * (x + 2)], prob_T[:, 512 * x + P * j:512 * x + P * j + P],
                                       v_of(tile, j, e), start=(j == 0), stop=(j == i))
                    for j in js:
                        ins = eng.matmul(o[:, 3 * DH:4 * DH], prob_T[:, 1152 + P * j:1152 + P * j + P],
                                         v_of(V_B, i - 1 + j, e), start=(j == js[0]), stop=(j == 1))
                    t.done(ins, f"pv{s}")
                    if e == 0 and i:
                        turn_outputs(i - 1)
                turn_outputs(QT - 1)

            t.wait("att_ev6")
            t.wait("att_ev7")
            for c in range(N_WO):
                chunk_ready(t, 0, START["wo"] + c)
                for m in range(2):
                    for x in range(2):
                        j = 4 * c + 2 * m + x
                        if j >= 2:
                            t.wait(f"wo_ev{j - 2}")
                        group(t, c % 2, x * 1024 + m * P, 256, 4, lin_outs(x, TB1),
                              lambda k, t0, n, x=x: x_hi(4 * x + k, t0, n), lambda k, t0, n, x=x: x_lo(4 * x + k, t0, n),
                              f"wo_g{j}", m == 1 and x == 1, ready=(lambda k, x=x: f"og_lo{4 * x + k}") if j < 2 else None)
            def w_out_tile(j, **more):
                group(t, (j // 2) % 2, (j % 2) * P, 256, KD, lin_outs(j % 2, TB1), lambda k, t0, n: yhi[:, k, t0:t0 + n],
                      lambda k, t0, n: ylo[:, k, t0:t0 + n], f"out_g{j}", j % 2 == 1, **more)
            chunk_ready(t, 0, START["out"])
            for j in range(2):
                t.wait(f"wo_ev{14 + j}")
                w_out_tile(j, ks=range(KD - 1), ready=lambda k: f"y_lo{k}")
            for j in range(2):
                w_out_tile(j, ks=range(KD - 1, KD), ready=lambda k: f"y_lo{k}")
            for j in range(2, KD):
                if j % 2 == 0:
                    chunk_ready(t, 0, START["out"] + j // 2)
                t.wait(f"out_ev{j - 2}")
                w_out_tile(j)
            for c in range(N_GATE):
                t.wait(f"ada_gate{c}")
                for j in range(2):
                    ins = eng.matmul(aux[0][:, 2 * c + j:2 * c + j + 1], gate_acc[:, c, P * j:P * j + P], ones[:, 0:1],
                                     start=True, stop=True)
            t.done(ins, "ada_gate")
            norm_total_pe(t, "n1", TB1, KD)
            norm_spread_pe(t, "n1", TB1)

            growing_totals_pe(t, "n2", TB2, T2)
            norm_spread_pe(t, "n2", TB2)

            with t.trips("cin", 8):
                for c in range(4):
                    chunk_ready(t, 4, START["cin"] + c)
                    for g in range(2):
                        j = 2 * c + g
                        t.wait(f"cin_ev{(j - 2) % 8}", 0 if j >= 2 else 1)
                        group(t, c % 2, g * P, 256, KD, lin_outs(g, TB2), x_hi, x_lo, f"cin_g{j}", g == 1,
                              ready=(lambda k: f"u_lo{k}") if j == 0 else None)
            with t.trips("cout", 2):
                for c in range(4):
                    chunk_ready(t, 4, START["cout"] + c)
                    if c < 2:
                        t.wait(f"cin_ev{6 + c}")
                    t.wait(f"cout_ev{(c - 2) % 4}", 0 if c >= 2 else 1)
                    group(t, c % 2, 0, P, KE, lin_outs(c % 2, TB2), lambda k, t0, n: vhi[:, k, t0:t0 + n],
                          lambda k, t0, n: vlo[:, k, t0:t0 + n], None, True,
                          ready=(lambda k: {KE - 2: "conv_lo0", KE - 1: "conv_lo1"}.get(k)) if c == 0 else None)
            t.wait("wm_split")
            m = 0
            for k in range(KD):
                t.wait(f"m_lo{max(k - 4, 0)}")
                for w, x in ((wm_hi, xhi), (wm_hi, xlo), (wm_lo, xhi)):
                    for b, t0, n in TB2:
                        ins = eng.matmul(aux[b][0:MG, 0:n], w[:, k, :], x[:, k, t0:t0 + n], start=(m == 0), stop=(m == 3 * KD - 1))
                    m += 1
            t.done(ins, "mgates")
            norm_total_pe(t, "n3", TB2, 4)
            norm_spread_pe(t, "n3", TB2)
            with t.trips("mlstm", LH):
                def projections(chunks, after_first=None):
                    for c in chunks:
                        chunk_ready(t, 10, START["mlstm"] + c)
                        for g in range(2):
                            j = 2 * c + g
                            t.wait(f"ml_ev{j - 2}" if j >= 2 else f"mlo_ev{6 + j}", 0 if j >= 2 else 1)
                            group(t, c % 2, g * P, 256, KD, lin_outs(g, TB2), x_hi, x_lo, f"ml_g{j}", g == 1)
                            if g == 0 and after_first:
                                after_first()
                projections(range(1))
                t.wait("rows_done")
                t.wait("head_row")
                t.wait("hn_rstd", 1)
                for x in range(2):
                    for b, t0, n in TB2:
                        eng.matmul(aux[2 * x + b][:, 0:n], head_row[0:LH, :], row[5 + x][:, t0:t0 + n],
                                   start=True, stop=True)
                for j, (s0, ln) in enumerate(STILES):
                    ins = eng.matmul(aux[3][0:ln, U_COL + j:U_COL + j + 1], row[4][:, s0:s0 + ln],
                                     head_row[0:LH, 0:1], start=True, stop=True)
                t.done(ins, "bc")
                projections(range(1, 3))
                t.wait("ml_ev3")
                t.wait("bc_ev_act")
                t.wait("bc_ev_dve")
                for q, (b, t0, n, j) in enumerate(SBLOCKS):
                    s0, ln = STILES[j]
                    if q >= 4:
                        t.wait(f"st_ev{q - 4}")
                    for k in range(2):
                        ins = eng.matmul(aux[q % 4][0:ln, 0:n], qk[:, 2 + k, s0:s0 + ln], qk[:, k, t0:t0 + n],
                                         start=(k == 0), stop=(k == 1))
                    t.done(ins, f"st{q}")
                projections(range(3, 5))
                t.wait("ml_ev7")
                for j, (s0, ln) in enumerate(STILES):
                    t.wait(f"vtk{j - 4}" if j >= 4 else f"st_ev{len(SBLOCKS) - 1}")
                    for vt in range(4):
                        ins = eng.transpose(aux[j % 4][0:ln, P * vt:P * vt + P], v_T[:, vt, s0:s0 + ln], ident[:])
                    t.done(ins, f"vtr{j}")
                projections(range(5, 6))
                t.wait(f"att_lo{len(SBLOCKS) - 1}")
                t.wait(f"vtk{len(STILES) - 1}")
                for x in range(5):
                    for b, t0, n in TB2:
                        q = 2 * x + b
                        if x >= 2:
                            t.wait(f"h_ev{q - 4}")
                        js = [j for j, (s0, _) in enumerate(STILES) if s0 < t0 + n]
                        for j in js:
                            s0, ln = STILES[j]
                            f = max(s0, t0)
                            fs = slice(P * (x - 1), P * x)
                            if x == 0:
                                terms = [(ones_r[0:ln, :], att_hi), (ones_r[0:ln, :], att_lo)]
                            else:
                                terms = [(v_hi[0:ln, j, fs], att_hi), (v_hi[0:ln, j, fs], att_lo), (v_lo[0:ln, j, fs], att_hi)]
                            for p, (w, a_part) in enumerate(terms):
                                ins = eng.matmul(h_banks(x)[b][:, f - t0:n], w, a_part[0:ln, j, f:t0 + n],
                                                 start=(j == 0 and p == 0), stop=(j == js[-1] and p == len(terms) - 1))
                        t.done(ins, f"h{q}")
                projections(range(6, 7), after_first=lambda: norm_total_pe(t, "hn", TB2, 4))
                norm_spread_pe(t, "hn", TB2)
                projections(range(7, 8))
                def out_tile(j, **more):
                    group(t, (j // 4) % 2, (j % 4) * P, 512, 4, lin_outs(j % 2, TB2), lambda k, t0, n: ghi[:, k, t0:t0 + n],
                          lambda k, t0, n: glo[:, k, t0:t0 + n], f"mlo_g{j}", j % 4 == 3, **more)
                chunk_ready(t, 10, START["mlstm"] + 8)
                for j in range(2):
                    t.wait(f"ml_ev{14 + j}")
                    out_tile(j, ks=range(3), ready=lambda k: f"g_lo{k}")
                for j in range(2):
                    out_tile(j, ks=range(3, 4), ready=lambda k: f"g_lo{k}")
                for j in range(2, KD):
                    if j == 4:
                        chunk_ready(t, 10, START["mlstm"] + 9)
                    t.wait(f"mlo_ev{j - 2}")
                    out_tile(j)
            norm_total_pe(t, "n4", TB1, KD)
            norm_spread_pe(t, "n4", TB1)
            loops.update({(c.name, k): v for c in (pe_n, ch_n) for k, v in c.loops.items()})


        @block.scalar
        def _(eng):
            a = Engine(eng, [act_n], known, points)
            act = eng.activation

            eng.dma_start(res[:, :, META:T2], x_t).then_inc(s_x, 16)
            eng.dma_start(res[:, :, 0:META], meta_t).then_inc(s_x, 16)
            eng.wait_ge(s_x, 32)
            for k in range(KD):
                if k >= 2:
                    a.wait(f"n0_part{k - 2}")
                a.done(act(sq[:, k % 2, 0:T1], res[:, k, META:T2], ACT.Square), f"n0_sq{k}")
            eng.wait_ge(s_const, 21)
            grown_root_act(a, "n0", TB1, D)
            chunk_lands_and_splits(a, 0, 0)
            for k in range(KD):
                a.wait(f"n0b_n{k}")
                a.done(act(xhi[:, k, 0:T1], tmp[:, k % 2, 0:T1], ACT.Identity, bias=mod[:, k:k + 1]), f"n0b_hi{k}")

            for c in range(N_PROJ):
                chunk_lands_and_splits(a, 0, START["proj"] + c + 1)
                if c in (1, 2):
                    a.wait(f"cin_sum{c - 1}")
                    a.done(act(cin_hi[c - 1][:], cin[:], ACT.Copy), f"cin_hi{c - 1}")
                if c == 6:
                    a.wait("cin_sum1")
                    for g in range(2):
                        if g == 0:
                            a.wait("proj_g5")
                        else:
                            eng.wait_ge(s_chunk, N_ADA + START["proj"] + 6)
                        a.done(act(proj[:, Q_HEADS + g, :], lin[g][:, 0, 0:T1], ACT.Copy, scale=DH ** -0.5), f"proj_ev5{g}")
                if c == 7:
                    a.wait("gates")
                    a.done(act(sq[0:24, 0, 0:T1], aux[0][0:24, :], ACT.Tanh, scale=0.5), "gate_th")
                if c in (5, 8):
                    src = c // 8
                    eng.wait_ge(s_chunk, N_ADA + START["proj"] + c)
                    a.done(act(cmp_th[0:2 * NC, :], aux[2 + src][0:2 * NC, 0:256], ACT.Tanh, scale=0.5), f"cmp_th{src}")

            with a.trips("att", NPAIR):
                def exps(s):
                    i, e = divmod(s, 2)
                    keys, w0 = P * (i + 1), 1056 + (P if i == 0 else 0)
                    a.wait(f"max{s}")
                    spans = [(1024, 1024 + NC), (0, keys), (512, 512 + keys), (w0, 1313)]
                    for x, (p0, p1) in enumerate(spans):
                        a.done(act(probs[e][:, p0:p1], probs[e][:, p0:p1], ACT.Exp, bias=nmaxs[:, e, x:x + 1],
                                   accum_out=prob_ss[:, e, x:x + 1]), f"exp{s}")

                for s in range(2 * QT):
                    i, e = divmod(s, 2)
                    c, g = divmod(s, 2)
                    if g == 0:
                        chunk_lands_and_splits(a, 4, START["att"] + c + 1)
                    if s == 0:
                        exps(0)
                    a.wait(f"pt{s}")
                    keys = P * (i + 1)
                    a.done(act(probs_T[e][:, 0:keys], att_banks(e)[0][:, 0:keys], ACT.Copy), f"pt_ev{s}_act")
                    if s + 1 < 2 * QT:
                        exps(s + 1)
                    if g == 1:
                        eng.wait_ge(s_chunk, a.i * 4 + (N_ADA + START["att"] + c + 1))
                    else:
                        a.wait(f"att_g{s}")
                    src = lin[g][:, 0, 0:T1]
                    if c == 0:
                        a.done(act(tmp[:, g, 0:T1], src, ACT.Tanh, scale=0.5), f"z_th{g}")
                    elif c == 3:
                        a.wait(f"s{2 * QT - 1}")
                        a.done(act(proj[:, Q_HEADS + g, :], src, ACT.Copy, scale=DH ** -0.5), f"att_ev{s}")
                    else:
                        dst = m_a[:, bass.ds(a.i * 2 + g, 1), :] if c == 1 else \
                            m_b[:, bass.ds(a.i * 2 + g, 1), META:T2]
                        a.done(act(dst.rearrange("p a n -> p (a n)"), src, ACT.Tanh, scale=0.5), f"att_ev{s}")

            for c in range(2):
                a.wait("pv7")
                eng.dma_start(gate_w[:, c, :], w_ada[N_ADA + c, :, :]).then_inc(s_ada[N_ADA + c], 16)
            for k in range(KD):
                a.wait(f"og{k}")
                a.done(act(xhi[:, k, 0:T1], tmp[:, k % 2, 0:T1], ACT.Copy), f"og_hi{k}")
            for c in range(N_WO):
                chunk_lands_and_splits(a, 0, START["wo"] + c + 1)
                for m in range(2):
                    k = 2 * c + m
                    a.wait(f"y{k}")
                    a.done(act(yhi[:, k, :], tmp[:, 1, 0:T1], ACT.Copy), f"y_hi{k}")
            eng.dma_start(res[:, :, META:T2], x_t).then_inc(s_x2, 16)
            for c in range(N_OUT):
                chunk_lands_and_splits(a, 0, START["out"] + c + 1)
                if c in (1, 2):
                    a.wait(f"ada_gate{c - 1}")
                    eng.dma_start(gate_w[:, c - 1, :], w_ada[N_ADA + c + 1, :, :]).then_inc(s_ada[N_ADA + c + 1], 16)
                for g in range(2):
                    j = 2 * c + g
                    if g == 0:
                        a.wait(f"out_g{j}")
                    else:
                        eng.wait_ge(s_chunk, N_ADA + START["out"] + c + 1)
                    if j >= 2:
                        a.wait(f"n1_add{j - 2}")
                    a.done(act(sq[:, g, 0:T1], lin[g][:, 0, 0:T1], ACT.Square, scale=0.5), f"n1_sq{j}")
                    a.done(act(m_a[:, j, :], lin[g][:, 0, 0:T1], ACT.Copy, scale=0.5), f"out_ev{j}")
            norm_root_act(a, "n1", TB1, D)
            for k in range(KD):
                a.wait(f"x1_{k}")
                a.done(act(xhi[:, k, :], res[:, k, :], ACT.Copy, scale=norm_c[:, 0, k:k + 1]), f"u_hi{k}")
                if k >= 2:
                    a.wait(f"n2_part{k - 2}")
                a.done(act(sq[:, k % 2, :], res[:, k, :], ACT.Square), f"n2_sq{k}")
            grown_root_act(a, "n2", TB2, D)

            def slot_full(stage, per, c, g, point):
                if g == 1:
                    eng.wait_ge(s_chunk, a.i * per + (N_ADA + START[stage] + c + 1))
                else:
                    a.wait(point)

            with a.trips("cin", 8):
                for c in range(4):
                    u = c // 2
                    chunk_lands_and_splits(a, 4, START["cin"] + c + 1)
                    if c % 2 == 0:
                        for g, dst in ((0, cb), (1, cc)):
                            slot_full("cin", 4, c, g, f"cin_g{2 * c}")
                            a.wait(f"conv_lo{1 - u}", 0 if u else 1)
                            for b, t0, n in TB2:
                                a.done(act(dst[:, t0:t0 + n], lin[g][:, b, 0:n], ACT.Copy), f"cin_ev{2 * c + g}")
                    else:
                        a.wait(f"cin_ev{4 * u + 3}")
                        a.done(act(sq[:, 0, :], cz[:], ACT.Tanh, scale=0.5), f"conv_th{u}")
                        a.wait(f"conv{u}")
                        a.done(act(vhi[:, bass.ds(a.i * 2 + u, 1), :].rearrange("p a n -> p (a n)"), tmp[:, u, :], ACT.Copy),
                               f"conv_hi{u}")
            with a.trips("cout", 2):
                for c in range(4):
                    chunk_lands_and_splits(a, 4, START["cout"] + c + 1)
                    a.wait(f"cout_ev{c}")
                    r = bass.ds(a.i * 4 + c, 1)
                    a.wait(f"n3_add{(c - 2) % 4}", 0 if c >= 2 else 1)
                    a.done(act(sq[:, c % 2, :], res[:, bass.ds(a.i * 4 + c, 1), :].rearrange("p a n -> p (a n)"), ACT.Square),
                           f"n3_sq{c}")
                    a.done(act(xhi[:, r, :].rearrange("p a n -> p (a n)"), res[:, r, :].rearrange("p a n -> p (a n)"),
                               ACT.Copy, scale=norm_c[:, 1, r]), f"m_hi{c}")
            norm_root_act(a, "n3", TB2, D)

            a.wait("rows_f")
            a.done(act(row[2], row[1], ACT.Abs))
            a.after_own()
            a.done(act(row[2], row[2], ACT.Exp, scale=-1.0))
            a.after_own()
            a.done(act(row[2], row[2], ACT.Ln, bias=1.0), "rows_ln")

            with a.trips("mlstm", LH):
                def output_gate_tanh(c):
                    for g in range(2):
                        k = 2 * (c - 4) + g
                        a.wait(f"ml_ev{8 + k}")
                        a.done(act(oz[:, k, :], oz[:, k, :], ACT.Tanh, scale=0.5), f"o_th{k}")

                def gate_tanh(k):
                    a.wait(f"ml_ev{12 + k}")
                    a.done(act(sq[:, 1, :], tmp[:, 0, :], ACT.Tanh, scale=0.5), f"z_ml{k}")

                for c in range(8):
                    chunk_lands_and_splits(a, 10, START["mlstm"] + c + 1)
                    if c == 3:
                        for q, (b, t0, n, j) in enumerate(SBLOCKS):
                            ln = STILES[j][1]
                            a.wait(f"st_ev{q}")
                            a.done(act(att_hi[0:ln, j, t0:t0 + n], att[0:ln, j, t0:t0 + n], ACT.Copy), f"att_hi{q}")
                    if c in (4, 5):
                        output_gate_tanh(c)
                    if c == 4:
                        for j, (s0, ln) in enumerate(STILES):
                            a.wait(f"vtr{j}")
                            a.done(act(v_hi[0:ln, j, :], aux[j % 4][0:ln, :], ACT.Copy), f"v_hi{j}")
                    if c == 0:
                        a.wait("bc")
                        for b, t0, n in TB2:
                            if b == 1:
                                a.wait("bc_ev_dve")
                            a.done(act(e_m[:, t0:t0 + n], aux[2 + b][:, 0:n], ACT.Exp, scale=-1.0), "bc_ev_act")
                    if c == 1:
                        a.wait("masked")
                        for j, (s0, ln) in enumerate(STILES):
                            if s0 + ln < T2:
                                a.done(act(att[0:ln, j, s0 + ln:T2], neg_m[0:ln, s0 + ln:T2], ACT.Exp,
                                           bias=ucur[0:ln, j:j + 1]))
                            a.done(act(att[0:ln, j, s0:s0 + ln], att[0:ln, j, s0:s0 + ln], ACT.Exp,
                                       bias=ucur[0:ln, j:j + 1]), f"decay{j}")
                    if c == 5:
                        for b, t0, n in TB2:
                            a.wait(f"h{b}")
                            a.done(act(rden[:, t0:t0 + n], h_banks(0)[b][:, 0:n], ACT.Abs), f"h_ev{b}")
                    if c == 6:
                        norm_squares_act(a, "hn", lambda k, t0, n: v_T[:, k, t0:t0 + n], 0, T2, 4, "h_done")
                        gate_tanh(0)
                        norm_root_act(a, "hn", TB2, DV)
                        gate_tanh(1)
                    if c == 7:
                        for k in range(4):
                            if k == 2:
                                gate_tanh(2)
                            if k == 3:
                                gate_tanh(3)
                            a.wait(f"g{k}")
                            a.done(act(ghi[:, k, :], gbuf[k % 2], ACT.Copy), f"g_hi{k}")
                chunk_lands_and_splits(a, 10, START["mlstm"] + 9)
                for k in range(KD):
                    if k == 4:
                        chunk_lands_and_splits(a, 10, START["mlstm"] + 10)
                    a.wait(f"mlo_ev{k}")
                    if k >= 2:
                        a.wait(f"n4_add{k - 2}")
                    a.done(act(sq[:, k % 2, 0:T1], res[:, k, META:T2], ACT.Square), f"n4_sq{k}")
            norm_root_act(a, "n4", TB1, D)
            for k in range(KD):
                a.wait(f"out_t{k}")
                eng.dma_start(out_t[P * k:P * k + P, :], res[:, k, META:T2]).then_inc(s_out, 16)
            loops.update({("act", k): v for k, v in act_n.loops.items()})



        @block.vector
        def _(eng):
            v = Engine(eng, [dve_n, slot_n], known, points)
            tt, ts, stt, copy = eng.tensor_tensor, eng.tensor_scalar, eng.scalar_tensor_tensor, eng.tensor_copy

            def move(out, src):
                return ts(out, src, 1.0, None, ALU.mult)

            def flat(ap):
                return ap.rearrange("p a n -> p (a n)")

            eng.wait_ge(s_small, 16)
            for half in range(2):
                ks = slice(half * KD // 2, (half + 1) * KD // 2)
                v.done(copy(wg_hi[:, ks, :], wg[:, ks, :]), f"wg_hi{half}", slot_n)
            v.wait("wg_hi1")
            v.done(tt(wg_lo[:], wg[:], wg_hi[:].bitcast(F32), ALU.subtract), "wg_split")

            def lane_sums(w, acc, point):
                for k in range(KD):
                    if k == 0:
                        v.done(ts(acc, w[:, 0:256], c_in[:, 0:1], None, ALU.mult))
                    else:
                        v.after_own()
                        v.done(stt(acc, w[:, 256 * k:256 * k + 256], c_in[:, k:k + 1], acc, ALU.mult, ALU.add), point)

            for c in range(N_ADA):
                if c not in POOL_ADA:
                    eng.wait_ge(s_ada[c], 16)
                    lane_sums(ada_w[:, c, :], ada_acc[:, c, :], f"ada{c}")
                if c == N_ADA - 3:
                    norm_invert_dve(v, "n0", TB1)
            norm_rstd_dve(v, "n0", TB1)
            eng.wait_ge(s_chunk, N_ADA)
            v.done(tt(mod[:, 0:16], aux[0][:, 0:16], bada[:, 0:16], ALU.add))
            v.after_own()
            v.done(stt(scale_c[:], mod[:, 8:16], 1.0, gpre[:], ALU.add, ALU.mult))

            def low(k):
                v.wait(f"n0b_hi{k}")
                v.done(stt(xlo[:, k, 0:T1], tmp[:, k % 2, 0:T1], mod[:, k:k + 1], xhi[:, k, 0:T1].bitcast(F32),
                           ALU.add, ALU.subtract), f"n0b_lo{k}")
            for k in range(KD):
                v.after_own()
                v.done(stt(tmp[:, k % 2, 0:T1], res[:, k, META:T2], scale_c[:, k:k + 1], rstd[:, 0:T1],
                           ALU.mult, ALU.mult), f"n0b_n{k}")
                if k:
                    low(k - 1)
            low(KD - 1)

            def tile_full(stage, per, c, last, point):
                if last:
                    eng.wait_ge(s_chunk, v.i * per + (N_ADA + START[stage] + c + 1) if per
                                else N_ADA + START[stage] + c + 1)
                else:
                    v.wait(point)

            def copy_out(c, between=None):
                for g in range(2):
                    tile_full("proj", 0, c, g == 1, f"proj_g{c}")
                    v.done(copy(proj[:, CHUNK_TILE[c] + g, :], lin[g][:, 0, :]), f"proj_ev{c}{g}")
                    if g == 0 and between:
                        between()

            def compression_input(src):
                if src:
                    v.wait(f"cin_hi{src - 1}")
                v.after_own()
                for g in range(2):
                    gs = slice(g * DH, (g + 1) * DH)
                    rows_of = proj[gs, K_C + src, :].rearrange("p (j a r) -> p r a j", a=8, r=2)
                    emb = pe_c[gs, src, :].rearrange("p (a r) -> p r a", r=2)
                    for r in range(2):
                        for a1 in range(2):
                            v.done(tt(cin[r * DH:(r + 1) * DH, 8 * a1:8 * a1 + 8, g, :], rows_of[:, r, :, a1:a1 + NC],
                                      emb[:, r, 8 * a1:8 * a1 + 8].unsqueeze(2).to_broadcast([DH, 8, NC]), ALU.add),
                                   f"cin_sum{src}")
                v.wait(f"cin_hi{src}")
                v.done(tt(cin_lo[src][:], cin[:], cin_hi[src][:].bitcast(F32), ALU.subtract), f"cin_lo{src}")

            def values_turned(s):
                v.wait(f"vt{s}")
                v.done(copy(proj[:, V_TILES[s], :], v_banks[s][:, 0:T1]), f"vtok{s}")

            def hidden(src):
                v.wait(f"cmp_th{src}")
                v.done(stt(hid_tok[0:2 * NC, :], cmp_th[0:2 * NC, :], 1.0, aux[2 + src][0:2 * NC, 0:256], ALU.add, ALU.mult),
                       f"hid_tok{src}")

            def hidden_turned(src):
                v.wait(f"hT{src}")
                v.done(copy(hid[:, src, :, :], aux[2 + src][:, 0:128].rearrange("p (j n) -> p j n", j=2)[:, :, 0:2 * NC]),
                       f"hid{src}")

            copy_out(0)
            compression_input(0)
            copy_out(1)
            compression_input(1)
            values_turned(0)
            copy_out(3)
            values_turned(1)
            hidden(0)
            hidden_turned(0)
            v.wait("kc")
            v.done(ts(kct[:], aux[1][:, 0:2 * NC], 0.5, None, ALU.mult), "kc_ready")
            v.wait("gates_T")
            v.done(ts(gate[:].rearrange("p i b -> p (i b)"), aux[1][:, 0:24 * QT], 0.5, 0.5, ALU.mult, ALU.add),
                   "gates_ready")
            v.after_own()
            eng.wait_ge(s_const, 21)
            v.done(ts(gate[:, 0, 0:NH], gate[:, 0, 0:NH], seen[:], None, ALU.mult))
            hidden(1)
            copy_out(8, lambda: hidden_turned(1))
            v.wait("vc")
            v.done(ts(vct[0:NC, :, :].rearrange("p g d -> p (g d)"), aux[1][0:NC, 128:256], 0.5, None, ALU.mult),
                   "kvc_ready")
            values_turned(2)
            v.after_own()

            with v.trips("att", NPAIR):
                for e in range(2):
                    v.done(move(scur[:, e:e + 1], slopes[:, bass.ds(v.i + 4 * e, 1)]))
                    v.done(move(sinkcur[:, e:e + 1], sink_c[:, bass.ds(v.i + 4 * e, 1)]))
                    for br in range(3):
                        v.done(move(gcur[:, e, :, br:br + 1], gate[:, :, bass.ds(v.i + (4 * e + NH * br), 1)]))
                v.after_own()
                def maxima(s):
                    i, e = divmod(s, 2)
                    b, prob = att_banks(e), probs[e]
                    keys, k0, w0 = P * (i + 1), max(0, P * (i - 1)), (P if i == 0 else 0)
                    v.wait(f"s{s}")
                    v.after_own()
                    sl = scur[:, e:e + 1]
                    v.done(stt(prob[:, 1024:1024 + NC], dist_c[:, i, 0:NC], sl, b[2][:, 0:NC], ALU.mult, ALU.add))
                    v.done(stt(prob[:, 0:keys], dist[:, T1 - keys:T1], sl, b[0][:, 0:keys], ALU.mult, ALU.add))
                    v.done(stt(prob[:, 512:512 + keys], dist[:, T1 - keys:T1], sl, b[1][:, 0:keys], ALU.mult, ALU.add))
                    v.done(stt(prob[:, 1056 + w0:1312], dist_w[:, w0:2 * P], sl, b[2][:, 32 + w0:32 + w0 + keys - k0],
                               ALU.mult, ALU.add))
                    v.done(copy(prob[:, 1312:1313], sinkcur[:, e:e + 1]))
                    v.after_own()
                    spans = [(1024, 1024 + NC), (0, keys), (512, 512 + keys), (1056 + w0, 1313)]
                    for x, (p0, p1) in enumerate(spans):
                        v.done(eng.tensor_reduce(nmaxs[:, e, x:x + 1], prob[:, p0:p1], AX.X, ALU.max, negate=True),
                               f"max{s}")

                def outputs_turned(i):
                    v.wait(f"o_T{i}")
                    for x in range(2):
                        v.done(move(flat(proj[:, bass.ds(v.i + Q_B * x, 1), P * i:P * i + P]),
                                    turn_bank(i)[:, P * x:P * x + P]), f"o_T_ev{i}")

                maxima(0)
                for s in range(2 * QT):
                    i, e = divmod(s, 2)
                    b, prob_T, coef = att_banks(e), probs_T[e], coefs[:, e, :]
                    keys, w0 = P * (i + 1), (P if i == 0 else 0)
                    v.wait(f"pt{s}")
                    v.done(copy(prob_T[0:NC, 1024:1152], b[2][0:NC, 0:P]))
                    v.done(copy(prob_T[:, 1152 + w0:1408], b[2][:, P + w0:3 * P]))
                    v.done(copy(prob_T[:, 512:512 + keys], b[1][:, 0:keys]), f"pt_ev{s}_dve")
                    v.wait(f"exp{s}")
                    v.done(eng.reciprocal(coef, prob_ss[:, e, :]))
                    v.after_own()
                    v.done(tt(coef[:, 0:3], coef[:, 0:3], gcur[:, e, i, :], ALU.mult))
                    if s + 1 < 2 * QT:
                        maxima(s + 1)
                    v.wait(f"pv{s}")
                    v.after_own()
                    o, es = b[0], slice(e * DH, (e + 1) * DH)
                    o_a, o_b = o_tok[:, i % 2, 0, es], o_tok[:, i % 2, 1, es]
                    v.done(ts(o_a, o[:, 0:DH], coef[:, 0:1], None, ALU.mult))
                    v.done(ts(o_b, o[:, 3 * DH:4 * DH], coef[:, 3:4], None, ALU.mult))
                    for x in (1, 2):
                        v.after_own()
                        v.done(stt(o_a, o[:, x * DH:(x + 1) * DH], coef[:, x:x + 1], o_a, ALU.mult, ALU.add), f"out{s}")
                    c, g = divmod(s, 2)
                    if c == 0:
                        v.wait(f"z_th{g}")
                        v.done(stt(flat(zz[:, g, bass.ds(v.i, 1), :]), tmp[:, g, 0:T1], 1.0, lin[g][:, 0, :],
                                   ALU.add, ALU.mult), f"att_ev{s}")
                    if e == 0 and i:
                        outputs_turned(i - 1)
                outputs_turned(QT - 1)
                v.after_own()

            v.wait("att_ev7")

            def low_og(k):
                v.wait(f"og_hi{k}")
                v.done(tt(xlo[:, k, 0:T1], tmp[:, k % 2, 0:T1], xhi[:, k, 0:T1].bitcast(F32), ALU.subtract), f"og_lo{k}")
            for k in range(KD):
                x, pr = divmod(k, NPAIR)
                v.after_own()
                v.done(stt(tmp[:, k % 2, 0:T1], zz[:, x, pr, :], 0.5, proj[:, Q_B * x + pr, :], ALU.mult, ALU.mult), f"og{k}")
                if k:
                    low_og(k - 1)
            low_og(KD - 1)
            for k in range(KD):
                c, m = divmod(k, 2)
                v.wait(f"wo_g{2 * k}")
                v.after_own()
                v.done(stt(tmp[:, 0, 0:T1], m_a[:, k, :], 1.0, lin[0][:, 0, :], ALU.add, ALU.mult), f"wo_ev{2 * k}")
                tile_full("wo", 0, c, m == 1, f"wo_g{2 * k + 1}")
                v.done(stt(sq[:, 0, 0:T1], m_b[:, k, META:T2], 1.0, lin[1][:, 0, :], ALU.add, ALU.mult), f"wo_ev{2 * k + 1}")
                v.after_own()
                v.done(tt(tmp[:, 1, 0:T1], tmp[:, 0, 0:T1], sq[:, 0, 0:T1], ALU.add), f"y{k}")
                v.wait(f"y_hi{k}")
                v.done(tt(ylo[:, k, :], tmp[:, 1, 0:T1], yhi[:, k, :].bitcast(F32), ALU.subtract), f"y_lo{k}")
            for c in range(N_GATE):
                eng.wait_ge(s_ada[N_ADA + c], 16)
                lane_sums(gate_w[:, c % 2, :], gate_acc[:, c, :], f"ada_gate{c}")
                for k in (2 * c, 2 * c + 1):
                    norm_add_dve(v, "n1", k, T1)
            v.wait("ada_gate")
            v.done(tt(mod[:, 16:24], aux[0][:, 0:8], bada[:, 16:24], ALU.add))
            v.after_own()
            v.done(tt(gpost[:], gpost[:], mod[:, 16:24], ALU.mult))
            norm_invert_dve(v, "n1", TB1)
            norm_rstd_dve(v, "n1", TB1)
            eng.wait_ge(s_x2, 16)

            def low_u(k):
                v.wait(f"u_hi{k}")
                v.done(stt(xlo[:, k, :], res[:, k, :], norm_c[:, 0, k:k + 1], xhi[:, k, :].bitcast(F32),
                           ALU.mult, ALU.subtract), f"u_lo{k}")
            for k in range(KD):
                v.after_own()
                v.done(stt(tmp[:, k % 2, 0:T1], m_a[:, k, :], gpost[:, k:k + 1], rstd[:, 0:T1], ALU.mult, ALU.mult))
                v.after_own()
                v.done(tt(res[:, k, META:T2], res[:, k, META:T2], tmp[:, k % 2, 0:T1], ALU.add), f"x1_{k}")
                if k:
                    low_u(k - 1)
            low_u(KD - 1)
            norm_invert_dve(v, "n2", TB2)
            norm_rstd_dve(v, "n2", TB2)
            v.done(tt(ssum[:], rstd[:], rstd[:], ALU.mult))

            v.done(eng.memset(cv[:, 0:2], 0.0))
            v.done(copy(wm_hi[:], wm[:]))
            v.after_own()
            v.done(tt(wm_lo[:], wm[:], wm_hi[:].bitcast(F32), ALU.subtract), "wm_split")
            with v.trips("cin", 8):
                for u in range(2):
                    f = bass.ds(v.i * 2 + u, 1)
                    v.wait(f"cin_ev{4 * u + 1}")
                    v.wait(f"cin_g{4 * u + 2}")
                    v.after_own()
                    for b, t0, n in TB2:
                        v.done(tt(cv[:, 2 + t0:2 + t0 + n], cc[:, t0:t0 + n], lin[0][:, b, 0:n], ALU.mult),
                               f"cin_ev{4 * u + 2}", slot_n if u and b else None)
                    v.after_own()
                    v.wait(f"cin_ev{4 * u + 2}")
                    v.done(tt(cv[:, 2:2 + T2], cv[:, 2:2 + T2], ssum[:], ALU.mult))
                    v.after_own()
                    v.done(ts(cy[:], cv[:, 0:T2], flat(conv_c[:, f, 0:1]), None, ALU.mult))
                    for w in (1, 2):
                        v.after_own()
                        v.done(stt(cy[:], cv[:, w:w + T2], flat(conv_c[:, f, w:w + 1]), cy[:], ALU.mult, ALU.add))
                    v.after_own()
                    v.done(tt(cy[:], cy[:], cb[:], ALU.mult))
                    v.after_own()
                    v.done(tt(cy[:], cy[:], rstd[:], ALU.mult))
                    tile_full("cin", 4, 2 * u + 1, True, None)
                    for b, t0, n in TB2:
                        v.done(tt(cz[:, t0:t0 + n], rstd[:, t0:t0 + n], lin[1][:, b, 0:n], ALU.mult),
                               f"cin_ev{4 * u + 3}", slot_n if u and b else None)
                    v.wait(f"conv_th{u}")
                    v.done(stt(cz[:], sq[:, 0, :], 1.0, cz[:], ALU.add, ALU.mult))
                    v.after_own()
                    v.done(stt(tmp[:, u, :], cy[:], 0.5, cz[:], ALU.mult, ALU.mult), f"conv{u}")
                    v.wait(f"conv_hi{u}")
                    v.done(tt(flat(vlo[:, f, :]), tmp[:, u, :], flat(vhi[:, f, :]).bitcast(F32), ALU.subtract),
                           f"conv_lo{u}")
            v.done(eng.memset(ssum[:], 0.0))
            with v.trips("cout", 2):
                for c in range(4):
                    tile_full("cout", 4, c, True, None)
                    r = bass.ds(v.i * 4 + c, 1)
                    for b, t0, n in TB2:
                        v.done(tt(flat(res[:, r, t0:t0 + n]), flat(res[:, r, t0:t0 + n]), lin[c % 2][:, b, 0:n], ALU.add),
                               f"cout_ev{c}")
                    v.wait(f"m_hi{c}")
                    v.after_own()
                    v.done(stt(flat(xlo[:, r, :]), flat(res[:, r, :]), norm_c[:, 1, r], flat(xhi[:, r, :]).bitcast(F32),
                               ALU.mult, ALU.subtract), f"m_lo{c}")
                    v.wait(f"n3_sq{c}")
                    v.done(tt(ssum[:], ssum[:], sq[:, c % 2, :], ALU.add), f"n3_add{c}")
            norm_invert_dve(v, "n3", TB2)

            v.done(eng.memset(row[5], 0.0))
            v.done(eng.memset(ucur[:], 0.0))
            v.done(copy(ones_r[:], ones[:]))
            v.wait("n3_spread")
            for b, t0, n in TB2:
                v.done(copy(u_rstd[:, t0:t0 + n], aux[2 + b][:, 0:n]))
            v.after_own()
            for b, t0, n in TB2:
                for x, r0 in ((0, 0), (1, 32)):
                    v.done(tt(row[x][:, t0:t0 + n], u_rstd[r0:r0 + LH, t0:t0 + n], aux[b][r0:r0 + LH, 0:n], ALU.mult))
            v.after_own()
            for x in range(2):
                v.done(ts(row[x], row[x], mb_c[0:LH, x:x + 1], None, ALU.add), "rows_f")
            v.after_own()
            v.done(ts(row[3], row[1], 0.0, None, ALU.min))
            v.wait("rows_ln")
            v.after_own()
            v.done(tt(row[3], row[3], row[2], ALU.subtract))
            v.after_own()
            v.done(eng.tensor_tensor_scan(row[1], row[3], row[5], 0.0, ALU.add, ALU.add))
            v.after_own()
            v.done(tt(row[4], row[0], row[1], ALU.subtract))
            v.after_own()
            v.done(eng.tensor_tensor_scan(row[3], row[4], row[5], 0.0, ALU.max, ALU.max))
            v.after_own()
            v.done(tt(row[6], row[1], row[3], ALU.add))
            v.done(ts(row[5], row[3], -1.0, None, ALU.mult), "rows_done")
            v.after_own()

            with v.trips("mlstm", LH):
                hd = bass.ds(v.i, 1)
                v.done(ts(head_row[0:LH, :], ones[0:LH, :], ident[0:LH, hd], None, ALU.mult), "head_row")
                v.done(ts(hcur[:], head_c[:, bass.ds(v.i * 4, 4)], 0.25, None, ALU.mult))
                def copy_out_ml(j):
                    tile_full("mlstm", 10, j // 2, j % 2 == 1, f"ml_g{j}")
                    dst = qk[:, j, :] if j < 4 else v_T[:, j - 4, :] if j < 8 else oz[:, j - 8, :] if j < 12 else tmp[:, 0, :]
                    for b, t0, n in TB2:
                        v.done(tt(dst[:, t0:t0 + n], u_rstd[:, t0:t0 + n], lin[j % 2][:, b, 0:n], ALU.mult), f"ml_ev{j}")

                copy_out_ml(0)
                copy_out_ml(1)
                v.wait("bc")
                for b, t0, n in TB2:
                    v.done(copy(neg_m[:, t0:t0 + n], aux[b][:, 0:n]))
                s0, ln = STILES[0]
                v.done(copy(ucur[0:ln, 0:1], aux[3][0:ln, U_COL:U_COL + 1]))
                v.done(copy(ucur[:, 1:], aux[3][:, U_COL + 1:U_COL + len(STILES)]), "bc_ev_dve")
                v.after_own()
                for j, (s0, ln) in enumerate(STILES):
                    v.done(tt(att[0:ln, j, s0:s0 + ln], neg_m[0:ln, s0:s0 + ln], mask[0:ln, 0:ln], ALU.add), "masked")
                for j in range(2, 6):
                    copy_out_ml(j)
                v.wait(f"decay{len(STILES) - 1}")
                for q, (b, t0, n, j) in enumerate(SBLOCKS):
                    ln = STILES[j][1]
                    v.wait(f"st{q}")
                    v.after_own()
                    v.done(stt(att[0:ln, j, t0:t0 + n], att[0:ln, j, t0:t0 + n], DK ** -0.5, aux[q % 4][0:ln, 0:n],
                               ALU.mult, ALU.mult), f"st_ev{q}")
                for q, (b, t0, n, j) in enumerate(SBLOCKS):
                    ln = STILES[j][1]
                    v.wait(f"att_hi{q}")
                    v.done(tt(att_lo[0:ln, j, t0:t0 + n], att[0:ln, j, t0:t0 + n],
                              att_hi[0:ln, j, t0:t0 + n].bitcast(F32), ALU.subtract), f"att_lo{q}")
                for j in range(6, 10):
                    copy_out_ml(j)
                for j, (s0, ln) in enumerate(STILES):
                    v.wait(f"v_hi{j}")
                    v.done(tt(v_lo[0:ln, j, :], aux[j % 4][0:ln, :], v_hi[0:ln, j, :].bitcast(F32), ALU.subtract), f"vtk{j}")
                copy_out_ml(10)
                copy_out_ml(11)
                v.wait("h_ev1")
                v.done(tt(rden[:], rden[:], e_m[:], ALU.max))
                v.after_own()
                v.done(eng.reciprocal(rden[:], rden[:]))
                v.after_own()
                for x in range(1, 5):
                    for b, t0, n in TB2:
                        v.wait(f"h{2 * x + b}")
                        v.done(tt(v_T[:, x - 1, t0:t0 + n], h_banks(x)[b][:, 0:n], rden[:, t0:t0 + n], ALU.mult),
                               f"h_ev{2 * x + b}")
                    points[f"h_done{x - 1}"] = ("dve", "mlstm", v.own.n)
                norm_adds_dve(v, "hn", T2, 4)
                v.after_own()

                def z_out(k):
                    v.after_own()
                    copy_out_ml(12 + k)

                def z_gate(k):
                    v.wait(f"z_ml{k}")
                    v.done(stt(sq[:, 1, :], sq[:, 1, :], 1.0, tmp[:, 0, :], ALU.add, ALU.mult))
                    v.after_own()

                def times_gates(k):
                    v.done(stt(oz[:, k, :], oz[:, k, :], 1.0, sq[:, 1, :], ALU.add, ALU.mult))
                    v.after_own()
                    v.done(tt(v_T[:, k, :], v_T[:, k, :], oz[:, k, :], ALU.mult))

                def normed(k, out, point=None):
                    v.done(stt(out, v_T[:, k, :], hcur[:, k:k + 1], rstd[:], ALU.mult, ALU.mult), point)

                def low_g(k):
                    v.wait(f"g_hi{k}")
                    v.done(tt(glo[:, k, :], gbuf[k % 2], ghi[:, k, :].bitcast(F32), ALU.subtract), f"g_lo{k}")

                z_out(0)
                z_gate(0)
                v.wait("o_th3")
                times_gates(0)
                for k in (2, 3):
                    v.done(stt(v_T[:, k, :], oz[:, k, :], 1.0, v_T[:, k, :], ALU.add, ALU.mult))
                norm_invert_dve(v, "hn", TB2)
                norm_rstd_dve(v, "hn", TB2)
                z_out(1)
                normed(0, gbuf[0], "g0")
                z_gate(1)
                times_gates(1)
                low_g(0)
                v.after_own()
                normed(1, gbuf[1], "g1")
                normed(2, v_T[:, 2, :])
                low_g(1)
                z_out(2)
                normed(3, v_T[:, 3, :])
                z_gate(2)
                v.done(tt(gbuf[0], v_T[:, 2, :], sq[:, 1, :], ALU.mult), "g2")
                z_out(3)
                low_g(2)
                z_gate(3)
                v.done(tt(gbuf[1], v_T[:, 3, :], sq[:, 1, :], ALU.mult), "g3")
                low_g(3)
                v.after_own()
                for j in range(KD):
                    c, g = divmod(j, 4)
                    tile_full("mlstm", 10, 8 + c, g == 3, f"mlo_g{j}")
                    for b, t0, n in TB2:
                        v.done(tt(res[:, j, t0:t0 + n], res[:, j, t0:t0 + n], lin[j % 2][:, b, 0:n], ALU.add), f"mlo_ev{j}",
                               slot_n if j >= KD - 2 and b else None)
                    norm_add_dve(v, "n4", j, T1)
            norm_invert_dve(v, "n4", TB1)
            norm_rstd_dve(v, "n4", TB1)
            for k in range(KD):
                v.done(stt(res[:, k, META:T2], res[:, k, META:T2], norm_c[:, 2, k:k + 1], rstd[:, 0:T1],
                           ALU.mult, ALU.mult), f"out_t{k}")
            loops.update({(c.name, k): val for c in (dve_n, slot_n) for k, val in c.loops.items()})
    trips = dict(att=NPAIR, cin=8, cout=2, mlstm=LH)
    return points, {k: (first, per, trips[k[1]]) for k, (first, per) in loops.items()}



def lay_out(i):
    def chunks(w, cols):
        k, n = w.shape
        return w.reshape(k // P, P, n // cols, cols).transpose(2, 1, 0, 3).reshape(n // cols, P, k // P * cols)

    def pairs(w, axis):
        s = list(w.shape)
        w = w.reshape(s[:axis] + [2, NPAIR, DH] + s[axis + 1:])
        return np.ascontiguousarray(np.swapaxes(w, axis, axis + 1)).reshape(s)

    def per_partition(a):
        return np.ascontiguousarray(a.reshape(-1, P).T)

    i = {k: np.asarray(a) for k, a in i.items()}
    ada, win = i['w_ada'][0], i['w_in'][0]
    q_a, kv3, g_n, z_a, q_b, kv_b, z_b, m_a, m_b = np.split(win, [512, 1280, 1304, 1816, 2328, 2584, 3096, 4120], axis=1)
    q_a, q_b, z_a, z_b = (pairs(w, 1) for w in (q_a, q_b, z_a, z_b))
    def queries(t):
        cols = slice(P * t, P * t + P)
        return np.concatenate([q_a[:, cols], q_b[:, cols]], 1)

    no_chunk = np.zeros((1, P, CHUNK), np.float32)
    kv = chunks(kv3, 256)
    cmp_k, cmp_v = ([chunks(w[0:D], 256), chunks(w[D:], 256)] for w in (i['w_cmp_k1'][0], i['w_cmp_v1'][0]))
    out = [kv[0:1], kv[1:2], cmp_k[0], kv[2:3], cmp_k[1], chunks(queries(0), 256), cmp_v[0], cmp_v[1],
           chunks(kv_b, 256), no_chunk]
    for t in range(NPAIR):
        cols = slice(P * t, P * t + P)
        wide = slice(256 * t, 256 * t + 256)
        out.append(chunks(np.concatenate([z_a[:, cols], z_b[:, cols], m_a[:, wide], m_b[:, wide]], 1), 256))
        out.append(chunks(queries(t + 1), 256) if t + 1 < NPAIR else no_chunk)
    wo = [chunks(pairs(i[n][0], 0), 256) for n in ('w_o_nsa', 'w_o_swa')]
    out.append(np.concatenate(wo, 2))
    out.append(chunks(i['w_out'][0], 256))
    b_c_x_z = i['conv_in_w_2'][0].reshape(D, 4, KE, P)
    out.append(chunks(np.ascontiguousarray(b_c_x_z.transpose(0, 2, 1, 3)).reshape(D, -1), 256))
    out.append(chunks(i['conv_out_w_2'][0], P))
    q, k, v, o, z, g = np.split(i['mlstm_in_w_2'][0], [1024, 2048, 4096, 6144, 8192], axis=1)
    for h in range(LH):
        a, b = slice(DK * h, DK * (h + 1)), slice(DV * h, DV * (h + 1))
        out.append(chunks(np.concatenate([q[:, a], k[:, a], v[:, b], o[:, b], z[:, b]], 1), 256))
        out.append(chunks(i['mlstm_out_w_2'][0][b], 512))
    out.append(no_chunk)
    stream = np.concatenate(out, 0)
    assert stream.shape == (N_CHUNKS + 1, P, CHUNK)
    w_mgate = np.zeros((D, MG), np.float32)
    w_mgate[:, 0:LH], w_mgate[:, 32:MG] = g[:, :LH], g[:, LH:]
    mgate_b = np.zeros((P, 2), np.float32)
    mgate_b[0:LH, 0], mgate_b[0:LH, 1] = i['mlstm_gate_b_2'][0, :LH], i['mlstm_gate_b_2'][0, LH:]

    def tiles(w):
        return np.ascontiguousarray(w.reshape(-1, P, w.shape[1]).transpose(1, 0, 2))
    def twice(a):
        return np.concatenate([a, a], 0)

    w2k = i['w_cmp_k2'][0]
    small = dict(
        c=per_partition(i['c']), b_ada=per_partition(i['b_ada']), g_pre=per_partition(i['g_pre']),
        g_post=per_partition(i['g_post']), w_gate=tiles(g_n), w_mgate=tiles(w_mgate), sinks=np.broadcast_to(i['sinks'], (P, NH)),
        w_k2=tiles(np.concatenate([w2k, w2k], 1)), w_v2=tiles(i['w_cmp_v2'][0]),
        norm_w=np.concatenate([per_partition(i['norm_w_2'][0]), per_partition(i['norm_w_2'][1]),
                               per_partition(i['final_norm_w_2'])], 1),
        conv_w=i['conv_w_2'][0].reshape(3, KE, P).transpose(2, 1, 0), head_w=per_partition(i['mlstm_head_norm_w_2']),
        mgate_b=mgate_b, pe=np.concatenate([twice(i['pe_cmp_k'][0].T), twice(i['pe_cmp_v'][0].T)], 1))
    smalls = np.concatenate([small[n].reshape(P, width) for n, width in SMALL], 1)
    return dict(wstream=stream, w_ada=np.ascontiguousarray(chunks(ada, 256)), smalls=smalls,
                x_t=tiles(i['x'][0].T), meta_t=tiles(i['meta_tokens_2'].T))


def kernel(**inputs):
    import concourse.bacc as _bacc
    from concourse import mybir as _mybir
    from concourse.bass_utils import run_bass_kernel_spmd as _run

    arrays = lay_out(inputs)
    known = dict(points={}, loops={}, sems={})
    for _ in range(2):
        nc = _bacc.Bacc("TRN2", target_bir_lowering=False, num_devices=1)
        args = {n: nc.dram_tensor(n, a.shape, _mybir.dt.from_np(a.dtype), kind="ExternalInput").ap()
                for n, a in arrays.items()}
        out = nc.dram_tensor("out_t", (D, T1), _mybir.dt.float32, kind="ExternalOutput").ap()
        points, loops = build(nc, known, out_t=out, **args)
        known = dict(points=points, loops=loops, sems={})
    r = _run(nc, [arrays], core_ids=[0])
    return np.ascontiguousarray(r.results[0]["out_t"].T).reshape(1, T1, D)
```
